# Optimizing a Trainium2 kernel written in Bass

```python
import math
import jax, jax.numpy as jnp
from jax import lax
import numpy as np

D_MODEL = 2048
BATCH = 1
SEQ = 256
DEPTH = 2

PLE_DIM = 256
BLOCK_Q = 128
NORM_EPS = 1e-6
N_BRANCH = 3
BRANCH_W = D_MODEL // 2

SSM_GROUP = 16
SSM_STATE = 64
SSM_GROUPS = BRANCH_W // SSM_GROUP
DT_MIN = 1e-3
DT_MAX = 1e-1

MLA_NOPE = 128
MLA_ROPE = 64
MLA_V = 128
MLA_HEADS = BRANCH_W // MLA_V
MLA_Q_RANK = D_MODEL // 4
MLA_KV_RANK = D_MODEL // 4
ROPE_THETA = 10000.0

SB_HEAD_DIM = 128
SB_HEADS = BRANCH_W // SB_HEAD_DIM

N_SSM_IN = BRANCH_W
N_SB_IN = 3 * BRANCH_W
N_GATE_PATH = N_BRANCH * BRANCH_W
N_MERGE = N_BRANCH * D_MODEL
SPLIT_SIZES = (N_SSM_IN, MLA_Q_RANK, MLA_KV_RANK, MLA_ROPE, N_SB_IN, N_GATE_PATH, N_MERGE)
N_IN = N_SSM_IN + MLA_Q_RANK + MLA_KV_RANK + MLA_ROPE + N_SB_IN + N_GATE_PATH + N_MERGE

kernel_name = "hybrid_s5_mla_stickbreaking_gated_merge"

def rms_norm(x, g):
    xf = x.astype(jnp.float32)
    y = xf * lax.rsqrt(jnp.mean(xf * xf, axis=-1, keepdims=True) + NORM_EPS)
    return (y * g.astype(jnp.float32)).astype(x.dtype)

def apply_rope(x, cos, sin):
    half = x.shape[-1] // 2
    xf = x.astype(jnp.float32)
    x1, x2 = xf[..., :half], xf[..., half:]
    shape = (1, x.shape[1]) + (1,) * (x.ndim - 3) + (half,)
    c = cos.reshape(shape)
    s = sin.reshape(shape)
    return jnp.concatenate([x1 * c - x2 * s, x1 * s + x2 * c], axis=-1).astype(x.dtype)

def s5_mixer(u, lam_re, lam_im, log_dt, b_re, b_im, c_re, c_im, d_skip, w_glu):
    bsz, seqlen, _ = u.shape
    f32 = jnp.float32
    uf = u.astype(f32).reshape(bsz, seqlen, SSM_GROUPS, SSM_GROUP)
    lr = lam_re.astype(f32)
    li = lam_im.astype(f32)
    dt = jnp.exp(log_dt.astype(f32))[:, None]
    mag = jnp.exp(lr * dt)
    ab_re = mag * jnp.cos(li * dt)
    ab_im = mag * jnp.sin(li * dt)
    den = lr * lr + li * li
    nr = ab_re - 1.0
    ni = ab_im
    coef_re = (nr * lr + ni * li) / den
    coef_im = (ni * lr - nr * li) / den
    br = b_re.astype(f32)
    bi = b_im.astype(f32)
    bb_re = coef_re[..., None] * br - coef_im[..., None] * bi
    bb_im = coef_re[..., None] * bi + coef_im[..., None] * br
    bu_re = jnp.einsum('bsgh,gph->bsgp', uf, bb_re)
    bu_im = jnp.einsum('bsgh,gph->bsgp', uf, bb_im)
    a_re = jnp.broadcast_to(ab_re, bu_re.shape)
    a_im = jnp.broadcast_to(ab_im, bu_im.shape)

    def combine(e1, e2):
        a1r, a1i, b1r, b1i = e1
        a2r, a2i, b2r, b2i = e2
        return (a1r * a2r - a1i * a2i,
                a1r * a2i + a1i * a2r,
                a2r * b1r - a2i * b1i + b2r,
                a2r * b1i + a2i * b1r + b2i)

    _, _, h_re, h_im = lax.associative_scan(combine, (a_re, a_im, bu_re, bu_im), axis=1)
    y = (jnp.einsum('bsgp,ghp->bsgh', h_re, c_re.astype(f32))
         - jnp.einsum('bsgp,ghp->bsgh', h_im, c_im.astype(f32))
         + d_skip.astype(f32).reshape(SSM_GROUPS, SSM_GROUP) * uf)
    y = jax.nn.gelu(y.reshape(bsz, seqlen, BRANCH_W))
    y = y * jax.nn.sigmoid(y @ w_glu.astype(f32))
    return y.astype(u.dtype)

def mla_mixer(q_lat, kv_lat, k_rope_raw, g_q, g_kv, w_uq, w_ukv, cos, sin):
    bsz, seqlen, _ = q_lat.shape
    q = (rms_norm(q_lat, g_q) @ w_uq).reshape(bsz, seqlen, MLA_HEADS, MLA_NOPE + MLA_ROPE)
    q_nope = q[..., :MLA_NOPE]
    q_rope = apply_rope(q[..., MLA_NOPE:], cos, sin)
    kv = (rms_norm(kv_lat, g_kv) @ w_ukv).reshape(bsz, seqlen, MLA_HEADS, MLA_NOPE + MLA_V)
    k_nope = kv[..., :MLA_NOPE]
    v = kv[..., MLA_NOPE:]
    k_rope = apply_rope(k_rope_raw, cos, sin)
    scale = (MLA_NOPE + MLA_ROPE) ** -0.5
    outs = []
    for blk in range(seqlen // BLOCK_Q):
        q0, q1 = blk * BLOCK_Q, (blk + 1) * BLOCK_Q
        s = (jnp.einsum('bqhd,bkhd->bhqk', q_nope[:, q0:q1], k_nope[:, :q1])
             + jnp.einsum('bqhr,bkr->bhqk', q_rope[:, q0:q1], k_rope[:, :q1]))
        s = s.astype(jnp.float32) * scale
        mask = jnp.arange(q1)[None, :] <= (q0 + jnp.arange(BLOCK_Q))[:, None]
        s = jnp.where(mask, s, -jnp.inf)
        pr = jax.nn.softmax(s, axis=-1).astype(v.dtype)
        outs.append(jnp.einsum('bhqk,bkhd->bqhd', pr, v[:, :q1]))
    o = jnp.concatenate(outs, axis=1)
    return o.reshape(bsz, seqlen, MLA_HEADS * MLA_V)

def stick_breaking_mixer(q, k, v):
    bsz, seqlen = q.shape[0], q.shape[1]
    scale = SB_HEAD_DIM ** -0.5
    outs = []
    for blk in range(seqlen // BLOCK_Q):
        q0, q1 = blk * BLOCK_Q, (blk + 1) * BLOCK_Q
        z = jnp.einsum('bqhd,bkhd->bhqk', q[:, q0:q1], k[:, :q1]).astype(jnp.float32) * scale
        mask = jnp.arange(q1)[None, :] < (q0 + jnp.arange(BLOCK_Q))[:, None]
        log_beta = jax.nn.log_sigmoid(z)
        log_rest = jnp.where(mask, jax.nn.log_sigmoid(-z), 0.0)
        later = lax.cumsum(log_rest, axis=3, reverse=True) - log_rest
        w = jnp.where(mask, jnp.exp(log_beta + later), 0.0).astype(v.dtype)
        outs.append(jnp.einsum('bhqk,bkhd->bqhd', w, v[:, :q1]))
    o = jnp.concatenate(outs, axis=1)
    return o.reshape(bsz, seqlen, SB_HEADS * SB_HEAD_DIM)

def hybrid_layer(x, p_i, ln_g, w_in, lam_re, lam_im, log_dt, b_re, b_im, c_re, c_im, d_skip, w_glu,
                 g_q, g_kv, w_uq, w_ukv, w_branch, w_out, ple_g, w_ple_gate, w_ple_proj, cos, sin):
    bsz, seqlen, _ = x.shape
    h = rms_norm(x, ln_g)
    proj = h @ w_in
    idx = []
    acc = 0
    for size in SPLIT_SIZES[:-1]:
        acc += size
        idx.append(acc)
    u_ssm, q_lat, kv_lat, k_rope_raw, qkv_sb, gate_path, merge_logits = jnp.split(proj, idx, axis=-1)

    y_ssm = s5_mixer(u_ssm, lam_re, lam_im, log_dt, b_re, b_im, c_re, c_im, d_skip, w_glu)
    y_mla = mla_mixer(q_lat, kv_lat, k_rope_raw, g_q, g_kv, w_uq, w_ukv, cos, sin)
    q_sb, k_sb, v_sb = jnp.split(qkv_sb.reshape(bsz, seqlen, 3, SB_HEADS, SB_HEAD_DIM), 3, axis=2)
    y_sb = stick_breaking_mixer(q_sb[:, :, 0], k_sb[:, :, 0], v_sb[:, :, 0])

    ys = jnp.stack([y_ssm, y_mla, y_sb], axis=2)
    ys = ys * jax.nn.silu(gate_path.reshape(bsz, seqlen, N_BRANCH, BRANCH_W))
    branch_out = jnp.einsum('bsnw,nwd->bsnd', ys, w_branch)
    merge_gate = jax.nn.sigmoid(merge_logits.reshape(bsz, seqlen, N_BRANCH, D_MODEL))
    merged = jnp.sum(merge_gate * branch_out, axis=2)
    x = x + merged @ w_out

    e = p_i @ w_ple_proj
    g = jax.nn.sigmoid(rms_norm(x, ple_g) @ w_ple_gate)
    return x + g * e

def setup_inputs(seed: int = 0) -> dict:
    key = jax.random.key(seed)
    ks = jax.random.split(key, 23)
    f32 = jnp.float32

    def nrm(k, shape, scale):
        return jax.random.normal(k, shape, f32) * scale

    def gain(k, shape):
        return 1.0 + nrm(k, shape, 0.02)

    G, P, HG, W = SSM_GROUPS, SSM_STATE, SSM_GROUP, BRANCH_W
    n_idx = jnp.arange(P, dtype=f32)
    return {
        'x': nrm(ks[0], (BATCH, SEQ, D_MODEL), 1.0),
        'p': nrm(ks[1], (DEPTH, BATCH, SEQ, PLE_DIM), 1.0),
        'ln_g': gain(ks[2], (DEPTH, D_MODEL)),
        'w_in': nrm(ks[3], (DEPTH, D_MODEL, N_IN), D_MODEL ** -0.5),
        'ssm_lam_re': -0.5 + nrm(ks[4], (DEPTH, G, P), 0.01),
        'ssm_lam_im': math.pi * n_idx + nrm(ks[5], (DEPTH, G, P), 0.01),
        'ssm_log_dt': jax.random.uniform(ks[6], (DEPTH, G), f32, math.log(DT_MIN), math.log(DT_MAX)),
        'ssm_b_re': nrm(ks[7], (DEPTH, G, P, HG), (2.0 * HG) ** -0.5),
        'ssm_b_im': nrm(ks[8], (DEPTH, G, P, HG), (2.0 * HG) ** -0.5),
        'ssm_c_re': nrm(ks[9], (DEPTH, G, HG, P), (2.0 * P) ** -0.5),
        'ssm_c_im': nrm(ks[10], (DEPTH, G, HG, P), (2.0 * P) ** -0.5),
        'ssm_d': nrm(ks[11], (DEPTH, W), 1.0),
        'ssm_w_glu': nrm(ks[12], (DEPTH, W, W), W ** -0.5),
        'mla_g_q': gain(ks[13], (DEPTH, MLA_Q_RANK)),
        'mla_g_kv': gain(ks[14], (DEPTH, MLA_KV_RANK)),
        'mla_w_uq': nrm(ks[15], (DEPTH, MLA_Q_RANK, MLA_HEADS * (MLA_NOPE + MLA_ROPE)), MLA_Q_RANK ** -0.5),
        'mla_w_ukv': nrm(ks[16], (DEPTH, MLA_KV_RANK, MLA_HEADS * (MLA_NOPE + MLA_V)), MLA_KV_RANK ** -0.5),
        'w_branch': nrm(ks[17], (DEPTH, N_BRANCH, W, D_MODEL), W ** -0.5),
        'w_out': nrm(ks[18], (DEPTH, D_MODEL, D_MODEL), D_MODEL ** -0.5),
        'ple_g': gain(ks[19], (DEPTH, D_MODEL)),
        'w_ple_gate': nrm(ks[20], (DEPTH, D_MODEL, D_MODEL), D_MODEL ** -0.5),
        'w_ple_proj': nrm(ks[21], (DEPTH, PLE_DIM, D_MODEL), PLE_DIM ** -0.5),
        'final_g': gain(ks[22], (D_MODEL,)),
    }

def reference(x, p, ln_g, w_in, ssm_lam_re, ssm_lam_im, ssm_log_dt, ssm_b_re, ssm_b_im, ssm_c_re, ssm_c_im,
              ssm_d, ssm_w_glu, mla_g_q, mla_g_kv, mla_w_uq, mla_w_ukv, w_branch, w_out, ple_g, w_ple_gate,
              w_ple_proj, final_g):
    seqlen = x.shape[1]
    pos = jnp.arange(seqlen, dtype=jnp.float32)
    inv_freq = ROPE_THETA ** (-jnp.arange(0, MLA_ROPE, 2, dtype=jnp.float32) / MLA_ROPE)
    ang = pos[:, None] * inv_freq[None, :]
    cos, sin = jnp.cos(ang), jnp.sin(ang)
    for i in range(DEPTH):
        x = hybrid_layer(x, p[i], ln_g[i], w_in[i], ssm_lam_re[i], ssm_lam_im[i], ssm_log_dt[i],
                         ssm_b_re[i], ssm_b_im[i], ssm_c_re[i], ssm_c_im[i], ssm_d[i], ssm_w_glu[i],
                         mla_g_q[i], mla_g_kv[i], mla_w_uq[i], mla_w_ukv[i], w_branch[i], w_out[i],
                         ple_g[i], w_ple_gate[i], w_ple_proj[i], cos, sin)
    return rms_norm(x, final_g)


_drawn_inputs = setup_inputs


def setup_inputs(seed=0):
    import zlib

    import numpy as np

    out = dict(_drawn_inputs(seed))
    spreads = {}
    factors = {'ln_g': 6.175,
     'ssm_lam_re': 64.0,
     'ssm_lam_im': 59.648,
     'ssm_log_dt': 61.96,
     'ssm_b_re': 64.0,
     'ssm_b_im': 64.0,
     'ssm_c_re': 64.0,
     'ssm_c_im': 64.0,
     'mla_g_q': 8.0,
     'mla_g_kv': 8.0,
     'ple_g': 64.0,
     'final_g': 7.99}
    for name, (base, spread) in spreads.items():
        noise = np.random.default_rng([zlib.crc32(name.encode()), seed]).standard_normal(out[name].shape)
        drawn = base * np.exp(spread * noise) if base else spread * noise
        out[name] = __import__('jax').numpy.asarray(drawn.astype(out[name].dtype))
    for name, factor in factors.items():
        out[name] = (out[name] * factor).astype(out[name].dtype)
    return out
```

```python
import numpy as np
import concourse.bass as bass
from concourse import mybir
from contextlib import ExitStack


SEQ, D, DEPTH, W = 256, 2048, 2, 1024
P, TOK = 128, SEQ // 128
KT = D // P
PLE, LAT, ROPE, HEADS, HD = 256, 512, 64, 8, 128
GROUP, STATE = 16, 64
NTILE = W // GROUP * STATE // P
QUADS = NTILE // 4
LEVELS = 8
EPS = 1e-6
COL_KR = W + 2 * LAT
COL_SB = COL_KR + ROPE
COL_GATE = COL_SB + 3 * W
COL_MERGE = COL_GATE + 3 * W
NB = 512
HB = 3 * HD
RING = 4
SLOT = 2 * NB

STAGES = [("proj", 4, 8), ("lat", 8, 2), ("sb", 8, 8), ("gate", 8, 8), ("merge2", 8, 6), ("merge1", 8, 6),
          ("glu", 2, 4), ("merge0", 8, 6), ("out", 4, 8), ("pproj", 4, 1), ("ple", 4, 8)]
SLAB0, PAIR0 = {}, {}
SLABS = PAIRS = 0
for _name, _blocks, _per in STAGES:
    SLAB0[_name], PAIR0[_name] = SLABS, PAIRS
    SLABS += _blocks * _per
    PAIRS += _blocks // 2
STEPS = [("ln", 8), ("qlat", 2), ("kvlat", 2), ("ys2", 4), ("ys1", 4), ("glu", 4), ("ys0", 4), ("merged", 8),
         ("p", 2), ("ple", 8)]
STEP0 = {}
NSTEP = 0
for _name, _n in STEPS:
    STEP0[_name] = NSTEP
    NSTEP += _n
NG = 40

MLA_SCALE = float((HD + ROPE) ** -0.5)
SB_SCALE = float(HD ** -0.5)
NEG = -1e30
MAGIC = 1.5 * 2.0 ** 23
TWO_PI = 2 * np.pi
TP1 = 6.28125
TP2 = 0.0019350051879882812
TP3 = float(np.float32(TWO_PI - TP1 - TP2))
PI_LOW = 3.1415925


def build(nc, x, p, ln_g, w_in, lam_re, lam_im, log_dt, b_re, b_im, c_re, c_im, d_skip, w_glu, g_q, g_kv, w_uq,
          w_ukv, w_branch, w_out, ple_g, w_ple_gate, w_ple_proj, final_g, ident_in, masks_in, rope_in, out):
    f32, f32r = mybir.dt.float32, mybir.dt.float32r
    ALU, ACT, AX = mybir.AluOpType, mybir.ActivationFunctionType, mybir.AxisListType
    ds = bass.ds
    ctx = ExitStack()
    with ctx:
        def sb(name, shape, dt=f32):
            return ctx.enter_context(nc.sbuf_tensor(name, shape, dt))

        def sem(name):
            return ctx.enter_context(nc.semaphore(name))

        x_keep = nc.dram_tensor("x_keep", [SEQ, D], f32, kind="Internal").ap()

        raw = sb("raw", [P, RING, SLOT])
        w_hi = sb("w_hi", [P, RING, SLOT], f32r)
        w_lo = sb("w_lo", [P, RING, SLOT], f32r)
        hT_hi = sb("hT_hi", [P, KT, SEQ], f32r)
        hT_lo = sb("hT_lo", [P, KT, SEQ], f32r)
        yT_hi = sb("yT_hi", [P, 8, SEQ], f32r)
        yT_lo = sb("yT_lo", [P, 8, SEQ], f32r)
        ys = sb("ys", [P, TOK, 3, W])
        ys_flat = ys[:, :, :, :].rearrange("p t b w -> p (t b w)")
        xn = ys_flat[:, 0:TOK * D].rearrange("p (t d) -> p t d", t=TOK)
        junk = ys_flat[:, TOK * D:TOK * D + D]
        gate_ssm = sb("gate_ssm", [P, TOK, W])
        p_in = gate_ssm[:, :, 0:PLE]
        fin_g = gate_ssm[:, :, :].rearrange("p t w -> p (t w)")
        reg1 = sb("reg1", [P, TOK, D])
        reg2 = sb("reg2", [P, 8192])
        lat = reg1[:, :, 0:2 * LAT]
        sb_qk = reg1[:, :, :].rearrange("p t (h c) -> p t h c", h=HEADS)
        merged = reg1
        xs = reg2[:, 0:TOK * D].rearrange("p (t d) -> p t d", t=TOK)
        mla_q = reg2[:, 0:3072].rearrange("p (t c) -> p t c", t=TOK)
        mla_kv = reg2[:, 3072:7168].rearrange("p (t c) -> p t c", t=TOK)
        kr = reg2[:, 7168:7296].rearrange("p (t c) -> p t c", t=TOK)
        rope_a = reg2[:, 7296:7552]
        rope_b = reg2[:, 7552:7808]
        rope_c = reg2[:, 7808:8064]
        tab = reg2[:, 0:2048].rearrange("p (c n) -> p c n", c=2)
        tab4 = reg2[:, 0:2048].rearrange("p (c j t) -> p c j t", c=2, j=4)
        st = reg2[:, 2048:4096].rearrange("p (c n) -> p c n", c=2)
        pr1 = reg2[:, 4096:6144].rearrange("p (c n) -> p c n", c=2)
        pr2 = reg2[:, 6144:8192].rearrange("p (c n) -> p c n", c=2)

        scr = sb("scr", [P, 4480])
        q_s = scr[:, 0:384].rearrange("p (t c) -> p t c", t=TOK)
        k_s = scr[:, 384:640].rearrange("p (t c) -> p t c", t=TOK)
        qk_s = scr[:, 0:512].rearrange("p (t c) -> p t c", t=TOK)
        qkT = scr[:, 640:1152]
        qrT = scr[0:ROPE, 1152:1408]
        krT = scr[0:ROPE, 1408:1664]
        s_a = scr[:, 1664:2048]
        s_b = scr[:, 2048:2432]
        s_c = scr[:, 2432:2816]
        pT = scr[:, 2816:3200]
        g_e = scr[:, 3200:3968].rearrange("p (t c) -> p t c", t=TOK)
        sig = scr[:, 0:1024].rearrange("p (t c) -> p t c", t=TOK)
        u_q = scr[:, 1024:1280].rearrange("p (t c) -> p t c", t=TOK)
        uT = scr[:, 1280:1536]
        bbT = scr[:, 1536:2560].rearrange("p (c j s) -> p c j s", c=2, j=4)
        b_ld = scr[:, 2560:2688].rearrange("p (c j h) -> p c j h", c=2, j=4)
        c_ld = scr[:, 2688:2944].rearrange("p (c s) -> p c s", c=2)
        b_t1 = scr[:, 2944:3072].rearrange("p (c j h) -> p c j h", c=2, j=4)
        b_t2 = scr[:, 3072:3200].rearrange("p (c j h) -> p c j h", c=2, j=4)
        d_q = scr[:, 3200:3328]
        y_q = scr[:, 3328:3584].rearrange("p (t c) -> p t c", t=TOK)
        bb = scr[:, 3968:4224].rearrange("p (c j h) -> p c j h", c=2, j=4)
        cbd = scr[:, 4224:4480].rearrange("p (c j h) -> p c j h", c=2, j=4)
        ident = sb("ident", [P, P])
        masks = sb("masks", [P, 3, 384])
        rope_t = sb("rope_t", [P, TOK, 2, ROPE // 2])
        rowsel = sb("rowsel", [P, 4])
        g_rows = sb("g_rows", [DEPTH * NG, P])
        g_all = sb("g_all", [P, DEPTH * NG])
        gc = sb("gc", [P, NG])
        lam_rows = sb("lam_rows", [NTILE, 2, P])
        dt_rows = sb("dt_rows", [NTILE, 2])
        dt_wide = sb("dt_wide", [NTILE, 2, STATE])
        lam = sb("lam", [P, 3, NTILE])
        prm = sb("prm", [P, 3, NTILE])
        prm_q = sb("prm_q", [P, 3, 4])
        pw = sb("pw", [P, LEVELS, 2, NTILE])
        pw_q = sb("pw_q", [P, LEVELS, 2, 4])
        sm = sb("sm", [P, 8, NTILE])
        st_ss = sb("st_ss", [P, 4])
        st_r = sb("st_r", [P, 4])
        mx = sb("mx", [P, 2])
        nmx = sb("nmx", [P, 2])
        sums = sb("sums", [P, 2])
        rsum = sb("rsum", [P, 2])
        one = sb("one", [P, 1])

        main = ctx.enter_context(nc.psum_tensor("main", [P, 4, NB], f32))
        trb = ctx.enter_context(nc.psum_tensor("trb", [P, 2, NB], f32))
        aux = ctx.enter_context(nc.psum_tensor("aux", [P, 2, NB], f32))

        raw_loaded = [sem(f"raw_loaded{i}") for i in range(RING)]
        hi_ready, lo_ready, slab_used = sem("hi_ready"), sem("lo_ready"), sem("slab_used")
        block_out = [sem("pair_a_out"), sem("pair_b_out")]
        tr_in, tr_hi, tr_lo = sem("tr_in"), sem("tr_hi"), sem("tr_lo")
        consts_in, gains_in, x_in, x_kept, x_back, s5_rows_in = (sem(n) for n in (
            "consts_in", "gains_in", "x_in", "x_kept", "x_back", "s5_rows_in"))
        p_loaded, fin_g_in, out_done = sem("p_loaded"), sem("fin_g_in"), sem("out_done")
        act_chain, dve_chain = sem("act_chain"), sem("dve_chain")
        gains_t, gains_ready = sem("gains_t"), sem("gains_ready")
        sq_done, ms_ready, root_ready, xn_ready = sem("sq_done"), sem("ms_ready"), sem("root_ready"), sem("xn_ready")
        dt_wide_ready, s5_cols_in, s5_lam_ready, s5_exp_ready = (sem(n) for n in (
            "dt_wide_ready", "s5_cols_in", "s5_lam_ready", "s5_exp_ready"))
        s5_ang_ready, s5_trig_ready, s5_prm_ready = sem("s5_ang_ready"), sem("s5_trig_ready"), sem("s5_prm_ready")
        lat_norm, kr_ready, kr_t, kr_out, mla_in = (sem(n) for n in (
            "lat_norm", "kr_ready", "kr_t", "kr_out", "mla_in"))
        h_static, h_qkT_in, h_qkT, h_scores, h_max, h_probs, h_pT_in, h_pT, h_o_in, h_o_out = (sem(n) for n in (
            "h_static", "h_qkT_in", "h_qkT", "h_scores", "h_max", "h_probs", "h_pT_in", "h_pT", "h_o_in", "h_o_out"))
        sb_soft, sb_arg = sem("sb_soft"), sem("sb_arg")
        gate_exp, gate_used = sem("gate_exp"), sem("gate_used")
        ys_ready = sem("ys_ready")
        q_ld, q_static, q_bb, q_T_in, q_T_out, q_bu, q_bu_used, q_h, q_y, q_y_out = (sem(n) for n in (
            "q_ld", "q_static", "q_bb", "q_T_in", "q_T_out", "q_bu", "q_bu_used", "q_h", "q_y", "q_y_out"))
        sig_ready, sig_used = sem("sig_ready"), sem("sig_used")
        gelu_ready, glu_sig, merged_ready = sem("gelu_ready"), sem("glu_sig"), sem("merged_ready")
        x1_ready, ple_sig = sem("x1_ready"), sem("ple_sig")
        layer_done, out_ready = sem("layer_done"), sem("out_ready")

        pe_mark, dve_mark = sem("pe_mark"), sem("dve_mark")

        class Chain:
            def __init__(self, eng, s):
                self.eng, self.s, self.n = eng, s, 0

            def __call__(self, ins):
                ins.then_inc(self.s, 1)
                self.n += 1
                self.eng.wait_ge(self.s, self.n)

            def clear(self):
                self.eng.sem_clear(self.s)
                self.n = 0

        block = ctx.enter_context(nc.Block())

        @block.sync
        def _(sp):
            sp.dma_start(reg2[:, 0:TOK * D].rearrange("p (t d) -> p t d", t=TOK),
                         x.rearrange("b (t p) d -> p (b t) d", p=P)).then_inc(x_in, 16)
            sp.dma_start(ident[:, :], ident_in).then_inc(consts_in, 16)
            for l in range(DEPTH):
                for src, at, n in ((ln_g, 0, 16), (ple_g, 16, 16), (g_q, 32, 4), (g_kv, 36, 4)):
                    sp.dma_start(g_rows[l * NG + at:l * NG + at + n, :],
                                 src[l, :].rearrange("(k p) -> k p", p=P)).then_inc(gains_in, 16)
            sp.dma_start(masks[:, :, :], masks_in).then_inc(consts_in, 16)
            sp.dma_start(rope_t[:, :, :, :], rope_in).then_inc(consts_in, 16)

            def slab(l, seg, j, it, per, dst, src):
                sp.wait_ge(lo_ready, l * SLABS + it * per + (SLAB0[seg] + j + 1))
                slot = (SLAB0[seg] + j) % RING
                sp.dma_start(dst(raw[:, slot, :]), src).then_inc(raw_loaded[slot], 16)

            def full(r):
                return r.rearrange("p (k n) -> p k n", k=2)

            def head_dst(r):
                return r[:, 0:2 * HB].rearrange("p (c n) -> p c n", c=3)

            def cols(w, l, k0, nk, c0, nc_):
                return w[ds(l, 1), k0 * P:(k0 + nk) * P, ds(c0, nc_)].rearrange("o (k p) n -> p (o k) n", p=P)

            with sp.Fori(0, DEPTH) as l:
                if True:
                    for c, lm in enumerate((lam_re, lam_im)):
                        sp.dma_start(lam_rows[:, c, :], lm[ds(l, 1), :, :].rearrange("o (j g) s -> (o j) (g s)", g=2))\
                          .then_inc(s5_rows_in, 16)
                    sp.dma_start(dt_rows[:, :], log_dt[ds(l, 1), :].rearrange("o (j g) -> (o j) g", g=2))\
                      .then_inc(s5_rows_in, 16)
                with sp.Fori(0, 2) as it:
                    for b in range(2):
                        for j in range(8):
                            slab(l, "proj", 8 * b + j, it, 16, full, cols(w_in, l, 2 * j, 2, it * 1024 + b * NB, NB))
                for j in range(2):
                    slab(l, "lat", j, 0, 0, lambda r: r[:, 0:8 * ROPE].rearrange("p (k n) -> p k n", k=8),
                         cols(w_in, l, 8 * j, 8, COL_KR, ROPE))
                for b in range(7):
                    w, c0 = (w_uq, b * NB) if b < 3 else (w_ukv, (b - 3) * NB)
                    for j in range(2):
                        slab(l, "lat", 2 + 2 * b + j, 0, 0, full, cols(w, l, 2 * j, 2, c0, NB))
                for seg, col in (("sb", COL_SB), ("gate", COL_GATE)):
                    with sp.Fori(0, HEADS // 2) as it:
                        for j in range(KT):
                            src = w_in[ds(l, 1), j * P:(j + 1) * P, col:col + 3 * W]
                            src = src.rearrange("o p (c n) -> (o p) c n", c=3)
                            slab(l, seg, j, it, 16, head_dst, src[:, :, ds(it * 2 * HD, 2 * HD)])

                def merge(br):
                    seg = f"merge{br}"
                    with sp.Fori(0, 4) as n:
                        for j in range(8):
                            if br and j == RING:
                                q = n + 4 * (2 - br)
                                sp.wait_ge(ys_ready, l * 3 + 2)
                                sp.wait_ge(q_T_out, l * QUADS + q + 1)
                                for c, bm in enumerate((b_re, b_im)):
                                    sp.dma_start(b_ld[:, c, :, :],
                                                 bm[ds(l, 1), ds(q * 8, 8), :, :]
                                                 .rearrange("o (j g) s h -> (g s) (o j) h", g=2)).then_inc(q_ld, 16)
                                for c, cm in enumerate((c_re, c_im)):
                                    for half in range(2):
                                        sp.dma_start(c_ld[:, c, half * STATE:(half + 1) * STATE],
                                                     cm[ds(l, 1), ds(q * 8, 8), :, :].rearrange("o g h s -> (o g h) s"))\
                                          .then_inc(q_ld, 16)
                                sp.dma_start(d_q, d_skip[ds(l, 1), ds(q * P, P)].broadcast_to([P, P])).then_inc(q_ld, 16)
                            slab(l, seg, j, n, 12, full, cols(w_in, l, 2 * j, 2, COL_MERGE + br * D + n * NB, NB))
                        for j in range(4):
                            src = w_branch[ds(l, 1), br, 2 * j * P:(2 * j + 2) * P, ds(n * NB, NB)]
                            slab(l, seg, 8 + j, n, 12, full, src.rearrange("o (k p) n -> p (o k) n", p=P))

                merge(2)
                merge(1)
                for b in range(2):
                    for j in range(4):
                        slab(l, "glu", 4 * b + j, 0, 0, full, cols(w_glu, l, 2 * j, 2, b * NB, NB))
                merge(0)
                sp.wait_ge(q_y_out, l * QUADS + QUADS)
                sp.wait_ge(x_kept, l * 16 + 16)
                sp.dma_start(xs, x_keep.rearrange("(t p) d -> p t d", p=P)).then_inc(x_back, 16)
                with sp.Fori(0, 2) as it:
                    for b in range(2):
                        for j in range(8):
                            slab(l, "out", 8 * b + j, it, 16, full, cols(w_out, l, 2 * j, 2, it * 1024 + b * NB, NB))
                sp.wait_ge(ys_ready, l * 3 + 3)
                sp.dma_start(p_in, p[ds(l, 1), 0, :, :].rearrange("o (t p) c -> p (o t) c", p=P)).then_inc(p_loaded, 16)
                for b in range(4):
                    slab(l, "pproj", b, 0, 0, full, cols(w_ple_proj, l, 0, 2, b * NB, NB))
                with sp.Fori(0, 2) as it:
                    for b in range(2):
                        for j in range(8):
                            slab(l, "ple", 8 * b + j, it, 16, full,
                                 cols(w_ple_gate, l, 2 * j, 2, it * 1024 + b * NB, NB))
            sp.wait_ge(tr_in, DEPTH * NSTEP)
            sp.dma_start(fin_g, final_g.rearrange("(o n) -> o n", o=1).broadcast_to([P, D])).then_inc(fin_g_in, 16)
            for t in range(TOK):
                sp.wait_ge(out_ready, t + 1)
                sp.dma_start(out[0, t * P:(t + 1) * P, :], xn[:, t, :]).then_inc(out_done, 16)
            sp.wait_ge(out_done, 16 * TOK)

        @block.gpsimd
        def _(pool):
            pool.sem_inc(lo_ready, RING)
            with pool.Fori(0, DEPTH) as l:
                def lows(g0, groups, n):
                    with pool.Fori(0, groups) as g:
                        for slot in range(RING):
                            i = l * SLABS + g * RING + (g0 * RING + slot)
                            pool.wait_ge(slab_used, i + 1)
                            pool.wait_ge(hi_ready, i + 1)
                            nc.gpsimd.tensor_tensor(w_lo[:, slot, 0:n], raw[:, slot, 0:n],
                                                    w_hi[:, slot, 0:n].bitcast(f32), ALU.subtract)\
                              .then_inc(lo_ready, 1)
                g1, g2, g3 = SLAB0["sb"] // RING, SLAB0["merge2"] // RING, SLABS // RING
                lows(0, g1, SLOT)
                lows(g1, g2 - g1, 2 * HB)
                lows(g2, g3 - g2, SLOT)

        @block.tensor
        def _(pe):
            pe.sem_inc(slab_used, RING)
            pe.sem_inc(block_out[0], 1)
            pe.sem_inc(block_out[1], 1)
            pe.sem_inc(tr_lo, 2)
            pe.sem_inc(h_o_out, 1)
            pe.wait_ge(consts_in, 48)
            pe.wait_ge(gains_in, 16 * 4 * DEPTH)
            nc.tensor.transpose(aux[:, 0, 0:DEPTH * NG], g_rows[:, :], ident[0:DEPTH * NG, 0:DEPTH * NG])\
              .then_inc(gains_t, 1)

            def products(l, seg, j, it, per, pair, ks, n, first, last, big=True):
                slot = (SLAB0[seg] + j) % RING
                hi, lo = (hT_hi, hT_lo) if big else (yT_hi, yT_lo)
                pe.wait_ge(lo_ready, l * SLABS + it * per + (SLAB0[seg] + j + 1 + RING))
                for i, k in enumerate(ks):
                    wh, wl = (w[:, slot, i * n:(i + 1) * n] for w in (w_hi, w_lo))
                    for t in range(TOK):
                        o = main[:, 2 * pair + t, 0:n]
                        a, b = (z[:, k, t * P:(t + 1) * P] for z in (hi, lo))
                        f, e = first and i == 0, last and i == len(ks) - 1
                        nc.tensor.matmul(o, a, wh, start=f, stop=False)
                        nc.tensor.matmul(o, a, wl, start=False, stop=False)
                        m = nc.tensor.matmul(o, b, wh, start=False, stop=e)
                m.then_inc(slab_used, 1)

            def pair_free(l, seg, it, b):
                pe.wait_ge(block_out[b % 2], l * PAIRS + it + (PAIR0[seg] + b // 2 + 1))

            def whole_block(l, seg, b, it, per, nslab, n=NB, big=True, k0=0):
                pair_free(l, seg, it, b)
                for j in range(nslab):
                    products(l, seg, nslab * b + j, it, per, b % 2, (k0 + 2 * j, k0 + 2 * j + 1), n, j == 0,
                             j == nslab - 1, big)

            def two_heads_products(l, seg, j, it):
                slot = (SLAB0[seg] + j) % RING
                pe.wait_ge(lo_ready, l * SLABS + it * 16 + (SLAB0[seg] + j + 1 + RING))
                for b in range(2):
                    if j == 0:
                        pair_free(l, seg, it, b)
                    wh, wl = (w[:, slot, 0:2 * HB].rearrange("p (c n) -> p c n", c=3)[:, :, b * HD:(b + 1) * HD]
                              for w in (w_hi, w_lo))
                    for t in range(TOK):
                        o = main[:, 2 * b + t, 0:HB].rearrange("p (c n) -> p c n", c=3)
                        x_hi, x_lo = (z[:, j, t * P:(t + 1) * P] for z in (hT_hi, hT_lo))
                        nc.tensor.matmul(o, x_hi, wh, start=j == 0, stop=False)
                        nc.tensor.matmul(o, x_hi, wl, start=False, stop=False)
                        m = nc.tensor.matmul(o, x_lo, wh, start=False, stop=j == KT - 1)
                m.then_inc(slab_used, 1)

            def transposes(l, seg, src, steps, per=2):
                for i in range(steps):
                    n = STEP0[seg] + i
                    pe.wait_ge(tr_lo, l * NSTEP + (n + 1))
                    for k in range(per):
                        for t in range(TOK):
                            m = nc.tensor.transpose(trb[:, n % 2, (2 * k + t) * P:(2 * k + t + 1) * P],
                                                    src(t)[:, (per * i + k) * P:(per * i + k + 1) * P], ident[:, :])
                    m.then_inc(tr_in, 1)

            def transposed(l, seg, steps):
                pe.wait_ge(tr_lo, l * NSTEP + (STEP0[seg] + steps + 2))

            with pe.Fori(0, DEPTH) as l:
                pe.wait_ge(xn_ready, l * 2 + 1)
                transposes(l, "ln", lambda t: xn[:, t, :], 8)
                pe.wait_ge(gains_ready, 1)
                pe.wait_ge(dt_wide_ready, l + 1)
                pe.sem_inc(pe_mark, 1)
                for c in range(2):
                    nc.tensor.transpose(aux[:, 0, c * NTILE:(c + 1) * NTILE], lam_rows[:, c, :],
                                        ident[0:NTILE, 0:NTILE])
                nc.tensor.transpose(aux[:, 0, 2 * NTILE:3 * NTILE], dt_wide[:, :, :].rearrange("j g s -> j (g s)"),
                                    ident[0:NTILE, 0:NTILE]).then_inc(s5_cols_in, 1)
                transposed(l, "ln", 8)
                pe.sem_inc(pe_mark, 1)
                with pe.Fori(0, 2) as it:
                    for b in range(2):
                        whole_block(l, "proj", b, it, 16, 8)
                pair_free(l, "lat", 0, 0)
                for j in range(2):
                    products(l, "lat", j, 0, 0, 0, range(8 * j, 8 * j + 8), ROPE, j == 0, j == 1)
                pe.wait_ge(lat_norm, l * 2 + 1)
                transposes(l, "qlat", lambda t: lat[:, t, 0:LAT], 2)
                pe.wait_ge(lat_norm, l * 2 + 2)
                transposes(l, "kvlat", lambda t: lat[:, t, LAT:2 * LAT], 2)
                transposed(l, "qlat", 2)
                for b in range(1, 8):
                    if b == 4:
                        transposed(l, "kvlat", 2)
                    whole_block(l, "lat", b, 0, 0, 2, big=False, k0=0 if b < 4 else 4)
                pe.wait_ge(kr_ready, l + 1)
                pe.sem_inc(pe_mark, 1)
                for t in range(TOK):
                    m = nc.tensor.transpose(aux[0:ROPE, 0, t * P:(t + 1) * P], kr[:, t, :], ident[:, :])
                m.then_inc(kr_t, 1)

                def head_transposes(n, rope):
                    pe.wait_ge(h_static, n + 1)
                    pe.wait_ge(h_o_out, n + 1)
                    for i, z in enumerate((q_s, k_s) if rope else (qk_s, qk_s)):
                        for t in range(TOK):
                            c = 0 if rope or i == 0 else P
                            m = nc.tensor.transpose(trb[:, 0, (2 * i + t) * P:(2 * i + t + 1) * P],
                                                    z[:, t, c:c + P], ident[:, :])
                    if rope:
                        for t in range(TOK):
                            m = nc.tensor.transpose(trb[0:ROPE, 1, t * P:(t + 1) * P], q_s[:, t, P:P + ROPE],
                                                    ident[:, :])
                    m.then_inc(h_qkT_in, 1)

                def head_scores(n, rope):
                    pe.wait_ge(h_qkT, n + 1)
                    for t, (c, nk) in enumerate(((0, P), (P, 2 * P))):
                        m = nc.tensor.matmul(aux[:, 0, c:c + nk], qkT[:, t * P:(t + 1) * P], qkT[:, 256:256 + nk],
                                             start=True, stop=not rope)
                        if rope:
                            m = nc.tensor.matmul(aux[:, 0, c:c + nk], qrT[:, t * P:(t + 1) * P], krT[:, 0:nk],
                                                 start=False, stop=True)
                    m.then_inc(h_scores, 1)

                def head_probs(n):
                    pe.wait_ge(h_probs, n + 1)
                    for i in range(3):
                        m = nc.tensor.transpose(aux[:, 1, i * P:(i + 1) * P], s_b[:, i * P:(i + 1) * P], ident[:, :])
                    m.then_inc(h_pT_in, 1)

                def head_out(n, v):
                    pe.wait_ge(h_pT, n + 1)
                    nc.tensor.matmul(trb[:, 1, 256:384], pT[:, 0:P], v(0), start=True, stop=True)
                    nc.tensor.matmul(trb[:, 1, 384:512], pT[:, P:2 * P], v(0), start=True, stop=False)
                    nc.tensor.matmul(trb[:, 1, 384:512], pT[:, 2 * P:3 * P], v(1), start=False, stop=True)\
                      .then_inc(h_o_in, 1)

                for seg in ("sb", "gate"):
                    mla = seg == "sb"
                    if mla:
                        pe.wait_ge(kr_out, l + 1)
                        pe.wait_ge(mla_in, l + 1)
                        pe.sem_inc(pe_mark, 1)
                    with pe.Fori(0, HEADS // 2) as it:
                        for b in range(2):
                            n = l * 2 * HEADS + it * 2 + (b if mla else HEADS + b)
                            for j in range(8):
                                two_heads_products(l, seg, 8 * b + j, it)
                                if j == 0:
                                    head_transposes(n, mla)
                                if j == 2:
                                    head_scores(n, mla)
                                if j == (5 if mla else 6):
                                    head_probs(n)
                            if mla:
                                head_out(n, lambda t: mla_kv[:, t, ds(it * 4 * HD + (2 * b + 1) * HD, HD)])
                            else:
                                head_out(n, lambda t: ys[:, t, 2, ds(it * 2 * HD + b * HD, HD)])

                def merge(br):
                    seg = f"merge{br}"
                    pe.wait_ge(ys_ready, l * 3 + (3 - br))
                    transposes(l, f"ys{br}", lambda t: ys[:, t, br, :], 4)
                    with pe.Fori(0, 4) as n:
                        q = l * QUADS + n + 4 * (2 - br)
                        for j in range(12):
                            if j in (0, 8):
                                pair_free(l, seg, n, j // 8)
                            if j == 8:
                                transposed(l, f"ys{br}", 4)
                            ks = (2 * j, 2 * j + 1) if j < 8 else (2 * j - 16, 2 * j - 15)
                            products(l, seg, j, n, 12, j // 8, ks, NB, j in (0, 8), j in (7, 11), j < 8)
                            if not br:
                                continue
                            if j == 1:
                                pe.wait_ge(q_bb, q + 1)
                                for t in range(TOK):
                                    nc.tensor.transpose(aux[:, 0, t * P:(t + 1) * P], u_q[:, t, :], ident[:, :])
                                for c in range(2):
                                    nc.tensor.transpose(aux[:, 0, (2 + c) * P:(3 + c) * P],
                                                        bb[:, c, :, :].rearrange("p j h -> p (j h)"), ident[:, :])
                                for c in range(2):
                                    m = nc.tensor.transpose(aux[:, 1, c * P:(c + 1) * P], c_ld[:, c, :], ident[:, :])
                                m.then_inc(q_T_in, 1)
                            if j in (3, 6):
                                half = j // 6
                                if half == 0:
                                    pe.wait_ge(q_T_out, q + 2)
                                else:
                                    pe.wait_ge(q_bu_used, q * 2 + 1)
                                for c in range(2):
                                    for i in range(2):
                                        m = nc.tensor.matmul(aux[:, c, i * SEQ:(i + 1) * SEQ],
                                                             bbT[:, c, 2 * half + i, :], uT, start=True, stop=True)
                                m.then_inc(q_bu, 1)
                        if br:
                            pe.wait_ge(q_h, q + 1)
                            for t in range(TOK):
                                for i in range(4):
                                    for c in range(2):
                                        m = nc.tensor.matmul(aux[:, 0, t * P + i * 32:t * P + (i + 1) * 32],
                                                             pr1[:, c, i * SEQ + t * P:i * SEQ + (t + 1) * P],
                                                             cbd[:, c, i, :], start=c == 0, stop=c == 1)
                            m.then_inc(q_y, 1)

                merge(2)
                merge(1)
                pe.wait_ge(gelu_ready, l + 1)
                transposes(l, "glu", lambda t: ys[:, t, 0, :], 4)
                transposed(l, "glu", 4)
                for b in range(2):
                    whole_block(l, "glu", b, 0, 0, 4, big=False)
                merge(0)
                pe.wait_ge(merged_ready, l * 4 + 4)
                transposes(l, "merged", lambda t: merged[:, t, :], 8)
                transposed(l, "merged", 8)
                pe.sem_inc(pe_mark, 1)
                with pe.Fori(0, 2) as it:
                    for b in range(2):
                        whole_block(l, "out", b, it, 16, 8)
                pe.wait_ge(p_loaded, l * 16 + 16)
                transposes(l, "p", lambda t: p_in[:, t, :], 2, per=1)
                transposed(l, "p", 2)
                for b in range(4):
                    pair_free(l, "pproj", 0, b)
                    products(l, "pproj", b, 0, 0, b % 2, (0, 1), NB, True, True, False)
                pe.wait_ge(xn_ready, l * 2 + 2)
                transposes(l, "ple", lambda t: xn[:, t, :], 8)
                transposed(l, "ple", 8)
                pe.sem_inc(pe_mark, 1)
                with pe.Fori(0, 2) as it:
                    for b in range(2):
                        whole_block(l, "ple", b, it, 16, 8)

        def used(l, seg, j, it=0, per=0):
            return l * SLABS + it * per + (SLAB0[seg] + j + 1 + RING)

        @block.scalar
        def _(act):
            A = nc.scalar.activation
            chain = Chain(act, act_chain)

            def split(l, seg, j, it=0, per=0):
                at = SLAB0[seg] + j
                slot = at % RING
                n = 2 * HB if SLAB0["sb"] <= at < SLAB0["merge2"] and not (seg == "gate" and j >= per) else SLOT
                i = l * SLABS + it * per + at
                act.wait_ge(raw_loaded[slot], (l * (SLABS // RING) + it * (per // RING) + (at // RING + 1)) * 16)
                act.wait_ge(slab_used, i + 1)
                A(w_hi[:, slot, 0:n], raw[:, slot, 0:n], ACT.Copy).then_inc(hi_ready, 1)

            def splits(l, seg, a, b, it=0, per=0):
                for j in range(a, b):
                    split(l, seg, j, it, per)

            def squares(l, k, src, n, at):
                for t in range(TOK):
                    m = A(junk[:, 0:n], src(t), ACT.Square, accum_out=st_ss[:, at + t:at + t + 1])
                    if t == 0:
                        chain(m)
                m.then_inc(sq_done, 1)

            def root(value, at):
                act.wait_ge(ms_ready, value)
                A(st_r[:, at:at + 2], st_ss[:, at:at + 2], ACT.Sqrt).then_inc(root_ready, 1)

            def highs(l, seg, steps, dst, per=2, gain=None, k0=0):
                for i in range(steps):
                    n = STEP0[seg] + i
                    act.wait_ge(tr_in, l * NSTEP + (n + 1))
                    for k in range(per):
                        kk = k0 + per * i + k
                        s = 1.0 if gain is None else gc[:, gain + per * i + k:gain + per * i + k + 1]
                        m = A(dst[:, kk, :], trb[:, n % 2, 2 * k * P:(2 * k + 2) * P], ACT.Copy, scale=s)
                    m.then_inc(tr_hi, 1)

            act.wait_ge(x_in, 16)
            with act.Fori(0, DEPTH) as l:
                splits(l, "proj", 0, RING)
                act.wait_ge(layer_done, l + 1)
                act.dma_start(x_keep.rearrange("(t p) d -> p t d", p=P), xs).then_inc(x_kept, 16)
                squares(l, 0, lambda t: xs[:, t, :], D, 0)
                root(l * 4 + 1, 0)
                highs(l, "ln", 8, hT_hi, gain=0)
                act.wait_ge(s5_lam_ready, l * 2 + 1)
                A(sm[:, 0, :], lam[:, 2, :], ACT.Exp).then_inc(s5_exp_ready, 1)
                act.wait_ge(s5_lam_ready, l * 2 + 2)
                A(prm[:, 0, :], sm[:, 1, :], ACT.Exp).then_inc(s5_exp_ready, 1)
                act.wait_ge(s5_ang_ready, l + 1)
                A(pw[:, 0, 1, :], sm[:, 2, :], ACT.Sin)
                A(pw[:, 0, 0, :], sm[:, 3, :], ACT.Sin).then_inc(s5_trig_ready, 1)
                with act.Fori(0, 2) as it:
                    for b in range(2):
                        splits(l, "proj", 8 * b + RING, 8 * b + 8 + RING, it, 16)
                for b in range(2):
                    act.wait_ge(slab_used, used(l, "proj", 16 + 8 * b + 7))
                    squares(l, 1 + b, lambda t: main[:, 2 * b + t, :], LAT, 2 * (1 - b))
                    root(l * 4 + 2 + b, 2 * (1 - b))
                highs(l, "qlat", 2, yT_hi, gain=32)
                highs(l, "kvlat", 2, yT_hi, gain=36, k0=4)
                splits(l, "lat", RING, 16 + RING)
                act.wait_ge(kr_t, l + 1)
                A(krT, aux[0:ROPE, 0, 0:SEQ], ACT.Copy).then_inc(kr_out, 1)

                with act.Fori(0, HEADS // 2) as it:
                    for b in range(2):
                        n = l * 2 * HEADS + it * 2 + b
                        splits(l, "sb", 8 * b + 4, 8 * b + 5, it, 16)
                        act.wait_ge(h_qkT_in, n + 1)
                        A(qkT[:, 0:256], trb[:, 0, 0:256], ACT.Copy, scale=MLA_SCALE)
                        A(qkT[:, 256:512], trb[:, 0, 256:512], ACT.Copy)
                        A(qrT, trb[0:ROPE, 1, 0:256], ACT.Copy, scale=MLA_SCALE).then_inc(h_qkT, 1)
                        splits(l, "sb", 8 * b + 5, 8 * b + 8, it, 16)
                        act.wait_ge(h_max, l * HEADS + it * 2 + (b + 1))
                        A(s_b[:, 0:P], s_a[:, 0:P], ACT.Exp, bias=nmx[:, 0:1], accum_out=sums[:, 0:1])
                        A(s_b[:, P:384], s_a[:, P:384], ACT.Exp, bias=nmx[:, 1:2], accum_out=sums[:, 1:2])\
                            .then_inc(h_probs, 1)
                        splits(l, "sb", 8 * b + 8, 8 * b + 10, it, 16)
                        act.wait_ge(h_pT_in, n + 1)
                        A(pT, aux[:, 1, 0:384], ACT.Copy).then_inc(h_pT, 1)
                        splits(l, "sb", 8 * b + 10, 8 * b + 12, it, 16)
                with act.Fori(0, HEADS // 2) as it:
                    for b in range(2):
                        n = l * 2 * HEADS + it * 2 + (HEADS + b)
                        g = l * HEADS + it * 2 + b
                        chain.clear()
                        splits(l, "gate", 8 * b + 4, 8 * b + 5, it, 16)
                        act.wait_ge(h_qkT_in, n + 1)
                        A(qkT[:, 0:256], trb[:, 0, 0:256], ACT.Copy, scale=SB_SCALE)
                        A(qkT[:, 256:512], trb[:, 0, 256:512], ACT.Copy).then_inc(h_qkT, 1)
                        splits(l, "gate", 8 * b + 5, 8 * b + 7, it, 16)
                        act.wait_ge(h_scores, n + 1)
                        chain(A(s_a, aux[:, 0, 0:384], ACT.Abs))
                        chain(A(s_b, s_a, ACT.Exp, scale=-1.0))
                        A(s_a, s_b, ACT.Ln, bias=one[:, 0:1]).then_inc(sb_soft, 1)
                        splits(l, "gate", 8 * b + 7, 8 * b + 9, it, 16)
                        act.wait_ge(sb_arg, g + 1)
                        A(s_b, s_c, ACT.Exp).then_inc(h_probs, 1)
                        splits(l, "gate", 8 * b + 9, 8 * b + 11, it, 16)
                        act.wait_ge(h_pT_in, n + 1)
                        A(pT, aux[:, 1, 0:384], ACT.Copy).then_inc(h_pT, 1)
                        splits(l, "gate", 8 * b + 11, 8 * b + 12, it, 16)
                    act.wait_ge(slab_used, used(l, "gate", 15, it, 16))
                    for b in range(2):
                        act.wait_ge(gate_used, l * HEADS + it * 2 + (b + 1))
                        for t in range(TOK):
                            m = A(g_e[:, t, :], main[:, 2 * b + t, 0:HB], ACT.Exp, scale=-1.0)
                        m.then_inc(gate_exp, 1)
                chain.clear()

                def merge(br):
                    seg = f"merge{br}"
                    highs(l, f"ys{br}", 4, yT_hi)
                    with act.Fori(0, 4) as n:
                        q = l * QUADS + n + 4 * (2 - br)
                        splits(l, seg, 4, 6, n, 12)
                        if br:
                            act.wait_ge(q_T_in, q + 1)
                            A(uT, aux[:, 0, 0:SEQ], ACT.Copy)
                            for c in range(2):
                                for i in range(4):
                                    A(bbT[:, c, i, :], aux[:, 0, (2 + c) * P:(3 + c) * P], ACT.Copy,
                                      scale=rowsel[:, i:i + 1])
                            for c in range(2):
                                for g in range(2):
                                    s = slice(g * STATE, (g + 1) * STATE)
                                    src = aux[s, 1, c * P:(c + 1) * P].rearrange("p (j g h) -> p j g h", j=4, g=2)
                                    m = A(cbd[s, c, :, g * GROUP:(g + 1) * GROUP], src[:, :, g, :], ACT.Copy,
                                          scale=-1.0 if c else 1.0)
                            m.then_inc(q_T_out, 1)
                        splits(l, seg, 6, 12, n, 12)
                        s = l * 12 + n + 4 * (2 - br)
                        act.wait_ge(slab_used, used(l, seg, 7, n, 12))
                        act.wait_ge(sig_used, s + 1)
                        for t in range(TOK):
                            m = A(sig[:, t, :], main[:, t, :], ACT.Sigmoid)
                        m.then_inc(block_out[0], 1)
                        act.wait_ge(block_out[0], l * PAIRS + n + (PAIR0[seg] + 2))
                        act.sem_inc(sig_ready, 1)
                        splits(l, seg, 12, 16, n, 12)

                merge(2)
                merge(1)
                act.wait_ge(q_y_out, l * QUADS + QUADS)
                A(ys[:, :, 0, :], ys[:, :, 0, :], ACT.Gelu_apprx_tanh).then_inc(gelu_ready, 1)
                highs(l, "glu", 4, yT_hi)
                for b in range(2):
                    splits(l, "glu", 4 * b + 4, 4 * b + 8)
                    act.wait_ge(slab_used, used(l, "glu", 4 * b + 3))
                    act.wait_ge(glu_sig, (l * 2 + b) * 2 + 1)
                    for t in range(TOK):
                        m = A(sig[:, t, :], main[:, 2 * b + t, :], ACT.Sigmoid)
                    m.then_inc(glu_sig, 1)
                merge(0)
                highs(l, "merged", 8, hT_hi)
                with act.Fori(0, 2) as it:
                    for b in range(2):
                        splits(l, "out", 8 * b + 4, 8 * b + 12, it, 16)
                highs(l, "p", 2, yT_hi, per=1)
                splits(l, "pproj", 4, 8)
                act.wait_ge(x1_ready, l + 1)
                squares(l, 3, lambda t: xs[:, t, :], D, 0)
                root(l * 4 + 4, 0)
                highs(l, "ple", 8, hT_hi, gain=16)

                for b in range(4):
                    splits(l, "ple", 8 * b + 4, min(8 * b + 12, 32))
                    act.wait_ge(slab_used, used(l, "ple", 8 * b + 7))
                    act.wait_ge(ple_sig, (l * 4 + b) * 2 + 1)
                    for t in range(TOK):
                        m = A(sig[:, t, :], main[:, 2 * (b % 2) + t, :], ACT.Sigmoid)
                    m.then_inc(ple_sig, 1)
                chain.clear()
            act.wait_ge(layer_done, DEPTH + 1)
            squares(0, 4, lambda t: xs[:, t, :], D, 0)
            root(DEPTH * 4 + 1, 0)

        @block.vector
        def _(dve):
            v = nc.vector
            chain = Chain(dve, dve_chain)
            dve.sem_inc(gate_used, 1)
            dve.sem_inc(sig_used, 1)
            dve.sem_inc(glu_sig, 1)
            dve.sem_inc(ple_sig, 1)
            dve.sem_inc(layer_done, 1)
            dve.sem_inc(q_T_out, 1)
            chain(v.memset(one[:, :], 1.0))
            chain(v.memset(bb, 0.0))
            chain(v.memset(cbd, 0.0))
            dve.wait_ge(consts_in, 48)
            for i in range(4):
                chain(v.reduce_sum(rowsel[:, i:i + 1], ident[:, 32 * i:32 * i + 32], AX.X))
            dve.wait_ge(gains_t, 1)
            v.tensor_copy(g_all[:, :], aux[:, 0, 0:DEPTH * NG]).then_inc(gains_ready, 1)
            dve.wait_ge(gains_ready, 1)
            chain.clear()

            def lows(l, seg, steps, hi, lo, per=2, gain=None, k0=0):
                for i in range(steps):
                    n = STEP0[seg] + i
                    dve.wait_ge(tr_hi, l * NSTEP + (n + 1))
                    for k in range(per):
                        kk = k0 + per * i + k
                        s = 1.0 if gain is None else gc[:, gain + per * i + k:gain + per * i + k + 1]
                        m = v.scalar_tensor_tensor(out=lo[:, kk, :], in0=trb[:, n % 2, 2 * k * P:(2 * k + 2) * P],
                                                   scalar=s, in1=hi[:, kk, :].bitcast(f32), op0=ALU.mult,
                                                   op1=ALU.subtract)
                    m.then_inc(tr_lo, 1)

            def mean_square(value, at, n):
                dve.wait_ge(sq_done, value)
                v.tensor_scalar(st_ss[:, at:at + 2], st_ss[:, at:at + 2], 1.0 / n, EPS, ALU.mult, ALU.add)\
                    .then_inc(ms_ready, 1)
                dve.wait_ge(root_ready, value)
                chain(v.reciprocal(st_r[:, at:at + 2], st_r[:, at:at + 2]))

            def norm(value):
                mean_square(value, 0, D)
                for t in range(TOK):
                    m = v.tensor_scalar(xn[:, t, :], xs[:, t, :], st_r[:, t:t + 1], None, ALU.mult)
                return m

            def s5_parameters(l):
                lre, lim, ldt = (lam[:, i, :] for i in range(3))
                dt, ar, ang, quarter, k, r, ni, den = (sm[:, i, :] for i in range(8))
                tt = v.tensor_tensor
                dve.wait_ge(s5_cols_in, l + 1)
                chain(v.tensor_copy(lam[:, :, :].rearrange("p c j -> p (c j)"), aux[:, 0, 0:3 * NTILE]))
                dve.sem_inc(s5_lam_ready, 1)
                dve.wait_ge(s5_exp_ready, l * 2 + 1)
                chain(tt(ar, lre, dt, ALU.mult))
                chain(tt(ang, lim, dt, ALU.mult))
                dve.sem_inc(s5_lam_ready, 1)
                chain(v.tensor_scalar(k, ang, float(1 / TWO_PI), MAGIC, ALU.mult, ALU.add))
                chain(v.tensor_scalar(k, k, MAGIC, None, ALU.subtract))
                for part in (TP1, TP2, TP3):
                    chain(v.scalar_tensor_tensor(out=ang, in0=k, scalar=-part, in1=ang, op0=ALU.mult, op1=ALU.add))
                chain(v.tensor_scalar(ang, ang, PI_LOW, -PI_LOW, ALU.min, ALU.max))
                chain(v.scalar_tensor_tensor(out=quarter, in0=ang, scalar=-1.0, in1=ang, op0=ALU.mult, op1=ALU.min))
                chain(v.tensor_scalar(quarter, quarter, float(np.pi / 2), None, ALU.add))
                dve.sem_inc(s5_ang_ready, 1)
                dve.wait_ge(s5_exp_ready, l * 2 + 2)
                dve.wait_ge(s5_trig_ready, l + 1)
                chain(tt(r, prm[:, 0, :], pw[:, 0, 0, :], ALU.mult))
                chain(v.tensor_scalar(r, r, 1.0, None, ALU.subtract))
                chain(tt(ni, prm[:, 0, :], pw[:, 0, 1, :], ALU.mult))
                chain(tt(den, lre, lre, ALU.mult))
                chain(tt(k, lim, lim, ALU.mult))
                chain(tt(den, den, k, ALU.add))
                chain(v.reciprocal(den, den))
                chain(tt(k, r, lre, ALU.mult))
                chain(tt(ang, ni, lim, ALU.mult))
                chain(tt(k, k, ang, ALU.add))
                chain(tt(prm[:, 1, :], k, den, ALU.mult))
                chain(tt(k, ni, lre, ALU.mult))
                chain(tt(ang, r, lim, ALU.mult))
                chain(tt(k, k, ang, ALU.subtract))
                chain(tt(prm[:, 2, :], k, den, ALU.mult))
                for i in range(1, LEVELS):
                    c, s = pw[:, i - 1, 0, :], pw[:, i - 1, 1, :]
                    chain(tt(k, c, c, ALU.mult))
                    chain(tt(r, s, s, ALU.mult))
                    chain(tt(pw[:, i, 0, :], k, r, ALU.subtract))
                    chain(v.scalar_tensor_tensor(out=pw[:, i, 1, :], in0=c, scalar=2.0, in1=s, op0=ALU.mult,
                                                 op1=ALU.mult))

            def rotary(x1, x2, t, heads):
                half = ROPE // 2
                shape = [P, heads, half]
                c = rope_t[:, t, 0:1, :].broadcast_to(shape)
                s = rope_t[:, t, 1:2, :].broadcast_to(shape)
                a, b_, d = (z[:, 0:heads * half].rearrange("p (h c) -> p h c", h=heads)
                            for z in (rope_a, rope_b, rope_c))
                chain(v.tensor_tensor(a, x1, s, ALU.mult))
                chain(v.tensor_tensor(b_, x2, s, ALU.mult))
                chain(v.tensor_tensor(d, x1, c, ALU.mult))
                chain(v.tensor_tensor(x1, d, b_, ALU.subtract))
                chain(v.tensor_tensor(b_, x2, c, ALU.mult))
                chain(v.tensor_tensor(x2, a, b_, ALU.add))

            def quad(l, n, br):
                q = n + 4 * (2 - br)
                g = l * QUADS + q
                tt = v.tensor_tensor
                dve.wait_ge(q_ld, (g + 1) * (16 * 7))
                chain(v.tensor_copy(u_q, ys[:, :, 0, ds(q * P, P)]))
                chain(v.tensor_copy(prm_q[:, :, :], prm[:, :, ds(q * 4, 4)]))
                chain(v.tensor_copy(pw_q[:, :, :, :].rearrange("p a b j -> p (a b) j"),
                                    pw[:, :, :, :].rearrange("p a b j -> p (a b) j")[:, :, ds(q * 4, 4)]))
                wide = [P, 4, GROUP]
                cr = prm_q[:, 1, :].rearrange("p (j o) -> p j o", o=1).broadcast_to(wide)
                ci = prm_q[:, 2, :].rearrange("p (j o) -> p j o", o=1).broadcast_to(wide)
                for c in range(2):
                    chain(tt(b_t1[:, c, :, :], b_ld[:, c, :, :], cr, ALU.mult))
                    chain(tt(b_t2[:, c, :, :], b_ld[:, c, :, :], ci, ALU.mult))
                for h in range(2):
                    s = slice(h * STATE, (h + 1) * STATE)
                    o = slice(h * GROUP, (h + 1) * GROUP)
                    chain(tt(bb[s, 0, :, o], b_t1[s, 0, :, :], b_t2[s, 1, :, :], ALU.subtract))
                    chain(tt(bb[s, 1, :, o], b_t1[s, 1, :, :], b_t2[s, 0, :, :], ALU.add))
                for t in range(TOK):
                    chain(tt(y_q[:, t, :], u_q[:, t, :], d_q, ALU.mult))
                dve.sem_inc(q_bb, 1)
                chain(v.memset(tab4[:, 0, :, 0:1], 1.0))
                chain(v.memset(tab4[:, 1, :, 0:1], 0.0))
                pa = pr1.rearrange("p c (j t) -> p c j t", j=4)
                pb = pr2.rearrange("p c (j t) -> p c j t", j=4)
                for k in range(LEVELS):
                    m = 1 << k
                    for c in range(2):
                        wr, wi = (pw_q[:, k, z, :].rearrange("p (j o) -> p j o", o=1).broadcast_to([P, 4, m])
                                  for z in range(2))
                        chain(tt(pa[:, c, :, 0:m], tab4[:, c, :, 0:m], wr, ALU.mult))
                        chain(tt(pb[:, c, :, 0:m], tab4[:, c, :, 0:m], wi, ALU.mult))
                    chain(tt(tab4[:, 0, :, m:2 * m], pa[:, 0, :, 0:m], pb[:, 1, :, 0:m], ALU.subtract))
                    chain(tt(tab4[:, 1, :, m:2 * m], pa[:, 1, :, 0:m], pb[:, 0, :, 0:m], ALU.add))
                for half in range(2):
                    s = slice(half * 512, half * 512 + 512)
                    cos, sin = (tab[:, z:z + 1, s].broadcast_to([P, 2, 512]) for z in range(2))
                    dve.wait_ge(q_bu, g * 2 + (half + 1))
                    chain(tt(pr1[:, :, s], aux[:, :, :], cos, ALU.mult))
                    chain(tt(pr2[:, :, s], aux[:, :, :], sin, ALU.mult))
                    dve.sem_inc(q_bu_used, 1)
                    chain(tt(st[:, 0, s], pr1[:, 0, s], pr2[:, 1, s], ALU.add))
                    chain(tt(st[:, 1, s], pr1[:, 1, s], pr2[:, 0, s], ALU.subtract))
                for c in range(2):
                    for i in range(4):
                        s = slice(i * SEQ, (i + 1) * SEQ)
                        chain(v.tensor_tensor_scan(st[:, c, s], prm_q[:, 0, i:i + 1].broadcast_to([P, SEQ]),
                                                   st[:, c, s], 0.0, ALU.mult, ALU.add))
                cos, sin = (tab[:, z:z + 1, :].broadcast_to([P, 2, 1024]) for z in range(2))
                chain(tt(pr1, st, cos, ALU.mult))
                chain(tt(pr2, st, sin, ALU.mult))
                chain(tt(pr1[:, 0, :], pr1[:, 0, :], pr2[:, 1, :], ALU.subtract))
                chain(tt(pr1[:, 1, :], pr1[:, 1, :], pr2[:, 0, :], ALU.add))
                dve.sem_inc(q_h, 1)
                dve.wait_ge(q_y, g + 1)
                chain(tt(ys[:, :, 0, ds(q * P, P)], y_q,
                         aux[:, 0, 0:SEQ].rearrange("p (t c) -> p t c", t=TOK), ALU.add))
                dve.sem_inc(q_y_out, 1)

            def merge(l, br):
                seg = f"merge{br}"
                lows(l, f"ys{br}", 4, yT_hi, yT_lo)
                with dve.Fori(0, 4) as n:
                    if br:
                        quad(l, n, br)
                    dve.wait_ge(sig_ready, l * 12 + n + (4 * (2 - br) + 1))
                    dve.wait_ge(slab_used, used(l, seg, 11, n, 12))
                    for t in range(TOK):
                        dst = merged[:, t, ds(n * NB, NB)]
                        if br == 2:
                            chain(v.tensor_tensor(dst, sig[:, t, :], main[:, 2 + t, :], ALU.mult))
                        else:
                            chain(v.tensor_tensor(sig[:, t, :], sig[:, t, :], main[:, 2 + t, :], ALU.mult))
                    if br != 2:
                        for t in range(TOK):
                            dst = merged[:, t, ds(n * NB, NB)]
                            chain(v.tensor_tensor(dst, dst, sig[:, t, :], ALU.add))
                    dve.sem_inc(block_out[1], 1)
                    dve.sem_inc(sig_used, 1)
                    if br == 0:
                        dve.sem_inc(merged_ready, 1)
                    chain.clear()

            dve.wait_ge(x_in, 16)
            with dve.Fori(0, DEPTH) as l:
                chain(v.tensor_copy(gc[:, :], g_all[:, ds(l * NG, NG)]))
                norm(l * 4 + 1).then_inc(xn_ready, 1)
                dve.wait_ge(s5_rows_in, l * 48 + 48)
                chain(v.tensor_copy(dt_wide[:, :, :], dt_rows[:, :].rearrange("j (g o) -> j g o", o=1)
                                    .broadcast_to([NTILE, 2, STATE])))
                dve.sem_inc(dt_wide_ready, 1)
                lows(l, "ln", 8, hT_hi, hT_lo, gain=0)
                s5_parameters(l)
                chain.clear()
                for b in range(2):
                    dve.wait_ge(slab_used, used(l, "proj", 8 * b + 7))
                    for t in range(TOK):
                        m = v.tensor_copy(ys[:, t, 0, b * NB:(b + 1) * NB], main[:, 2 * b + t, :])
                    m.then_inc(block_out[b], 1)
                for b in range(2):
                    mean_square(l * 4 + 2 + b, 2 * (1 - b), LAT)
                    for t in range(TOK):
                        chain(v.tensor_scalar(lat[:, t, b * LAT:(b + 1) * LAT], main[:, 2 * b + t, :],
                                              st_r[:, 2 * (1 - b) + t:2 * (1 - b) + t + 1], None, ALU.mult))
                    dve.sem_inc(block_out[b], 1)
                    dve.sem_inc(lat_norm, 1)
                lows(l, "qlat", 2, yT_hi, yT_lo, gain=32)
                lows(l, "kvlat", 2, yT_hi, yT_lo, gain=36, k0=4)
                dve.wait_ge(x_kept, l * 16 + 16)
                dve.wait_ge(slab_used, used(l, "lat", 1))
                for t in range(TOK):
                    chain(v.tensor_copy(kr[:, t, :], main[:, t, 0:ROPE]))
                dve.sem_inc(block_out[0], 1)
                for t in range(TOK):
                    k3 = kr[:, t, :].rearrange("p (h c) -> p h c", h=1)
                    rotary(k3[:, :, 0:ROPE // 2], k3[:, :, ROPE // 2:ROPE], t, 1)
                dve.sem_inc(kr_ready, 1)
                for b in range(1, 8):
                    dst, c = (mla_q, b - 1) if b < 4 else (mla_kv, b - 4)
                    dve.wait_ge(slab_used, used(l, "lat", 2 * b + 1))
                    for t in range(TOK):
                        chain(v.tensor_copy(dst[:, t, c * NB:(c + 1) * NB], main[:, 2 * (b % 2) + t, :]))
                    dve.sem_inc(block_out[b % 2], 1)
                    if b == 3:
                        for t in range(TOK):
                            q4 = mla_q[:, t, :].rearrange("p (h c) -> p h c", h=HEADS)
                            rotary(q4[:, :, HD:HD + ROPE // 2], q4[:, :, HD + ROPE // 2:HD + ROPE], t, HEADS)
                dve.sem_inc(mla_in, 1)
                dve.wait_ge(kr_out, l + 1)
                dve.sem_inc(dve_mark, 1)
                with dve.Fori(0, HEADS // 2) as it:
                    for b in range(2):
                        chain.clear()
                        n = l * 2 * HEADS + it * 2 + b
                        chain(v.tensor_copy(q_s, mla_q[:, :, ds(it * 384 + b * 192, 192)]))
                        chain(v.tensor_copy(k_s, mla_kv[:, :, ds(it * 512 + b * 256, HD)]))
                        dve.sem_inc(h_static, 1)
                        dve.wait_ge(h_scores, n + 1)
                        chain(v.tensor_tensor(s_a, aux[:, 0, 0:384], masks[:, 0, :], ALU.add))
                        chain(v.reduce_max(mx[:, 0:1], s_a[:, 0:P], AX.X))
                        chain(v.reduce_max(mx[:, 1:2], s_a[:, P:384], AX.X))
                        chain(v.tensor_scalar(nmx[:, :], mx[:, :], -1.0, None, ALU.mult))
                        dve.sem_inc(h_max, 1)
                        dve.wait_ge(h_probs, n + 1)
                        chain(v.reciprocal(rsum[:, :], sums[:, :]))
                        if b == 1:
                            dve.wait_ge(slab_used, used(l, "sb", 15, it, 16))
                            for h in range(2):
                                for t in range(TOK):
                                    chain(v.tensor_copy(sb_qk[:, t, ds(it * 2 + h, 1), :].rearrange("p o c -> p (o c)"),
                                                        main[:, 2 * h + t, 0:256]))
                                    chain(v.tensor_copy(ys[:, t, 2, ds(it * 256 + h * HD, HD)],
                                                        main[:, 2 * h + t, 256:384]))
                                dve.sem_inc(block_out[h], 1)
                        dve.wait_ge(h_o_in, n + 1)
                        for t in range(TOK):
                            chain(v.tensor_scalar(ys[:, t, 1, ds(it * 256 + b * HD, HD)],
                                                  trb[:, 1, 256 + t * P:384 + t * P], rsum[:, t:t + 1], None,
                                                  ALU.mult))
                        dve.sem_inc(h_o_out, 1)
                with dve.Fori(0, HEADS // 2) as it:
                    for b in range(2):
                        chain.clear()
                        n = l * 2 * HEADS + it * 2 + (HEADS + b)
                        chain(v.tensor_copy(qk_s, sb_qk[:, :, ds(it * 2 + b, 1), :].rearrange("p t o c -> p t (o c)")))
                        dve.sem_inc(h_static, 1)
                        dve.wait_ge(sb_soft, l * HEADS + it * 2 + (b + 1))
                        chain(v.scalar_tensor_tensor(out=s_a, in0=aux[:, 0, 0:384], scalar=0.0, in1=s_a, op0=ALU.max,
                                                     op1=ALU.add))
                        chain(v.tensor_tensor(s_a, s_a, masks[:, 2, :], ALU.mult))
                        for a, e in ((0, P), (P, 384)):
                            back = slice(e - 1, a - 1 if a else None, -1)
                            chain(v.tensor_tensor_scan(s_b[:, back], one[:, 0:1].broadcast_to([P, e - a]),
                                                       s_a[:, back], 0.0, ALU.mult, ALU.add))
                        chain(v.tensor_tensor(s_c, aux[:, 0, 0:384], s_b, ALU.subtract))
                        chain(v.tensor_tensor(s_c, s_c, masks[:, 1, :], ALU.add))
                        dve.sem_inc(sb_arg, 1)
                        dve.wait_ge(h_o_in, n + 1)
                        for t in range(TOK):
                            chain(v.tensor_copy(ys[:, t, 2, ds(it * 256 + b * HD, HD)],
                                                trb[:, 1, 256 + t * P:384 + t * P]))
                        dve.sem_inc(h_o_out, 1)
                    for b in range(2):
                        dve.wait_ge(gate_exp, l * HEADS + it * 2 + (b + 1))
                        chain(v.tensor_scalar(g_e, g_e, 1e38, 1.0, ALU.min, ALU.add))
                        chain(v.reciprocal(g_e, g_e))
                        for t in range(TOK):
                            chain(v.tensor_tensor(gate_ssm[:, t, ds(it * 256 + b * HD, HD)], g_e[:, t, 0:HD],
                                                  main[:, 2 * b + t, 0:HD], ALU.mult))
                            chain(v.tensor_tensor(g_e[:, t, HD:HB], g_e[:, t, HD:HB], main[:, 2 * b + t, HD:HB],
                                                  ALU.mult))
                        dve.sem_inc(block_out[b], 1)
                        for t in range(TOK):
                            y2 = ys[:, t, 1:3, ds(it * 256 + b * HD, HD)]
                            chain(v.tensor_tensor(y2, y2, g_e[:, t, HD:HB].rearrange("p (c n) -> p c n", c=2),
                                                  ALU.mult))
                        dve.sem_inc(gate_used, 1)
                chain.clear()
                dve.sem_inc(ys_ready, 2)
                merge(l, 2)
                merge(l, 1)
                dve.wait_ge(gelu_ready, l + 1)
                lows(l, "glu", 4, yT_hi, yT_lo)
                for b in range(2):
                    dve.wait_ge(glu_sig, (l * 2 + b) * 2 + 2)
                    for t in range(TOK):
                        s = slice(b * NB, (b + 1) * NB)
                        chain(v.tensor_tensor(sig[:, t, :], sig[:, t, :], gate_ssm[:, t, s], ALU.mult))
                        chain(v.tensor_tensor(ys[:, t, 0, s], ys[:, t, 0, s], sig[:, t, :], ALU.mult))
                    dve.sem_inc(glu_sig, 1)
                    dve.sem_inc(block_out[b], 1)
                dve.sem_inc(ys_ready, 1)
                chain.clear()
                merge(l, 0)
                lows(l, "merged", 8, hT_hi, hT_lo)
                dve.wait_ge(x_back, l * 16 + 16)
                for b in range(4):
                    dve.wait_ge(slab_used, used(l, "out", 8 * b + 7))
                    for t in range(TOK):
                        s = slice(b * NB, (b + 1) * NB)
                        chain(v.tensor_tensor(xs[:, t, s], xs[:, t, s], main[:, 2 * (b % 2) + t, :], ALU.add))
                    dve.sem_inc(block_out[b % 2], 1)
                dve.sem_inc(x1_ready, 1)
                lows(l, "p", 2, yT_hi, yT_lo, per=1)
                for b in range(4):
                    dve.wait_ge(slab_used, used(l, "pproj", b))
                    for t in range(TOK):
                        chain(v.tensor_copy(reg1[:, t, b * NB:(b + 1) * NB], main[:, 2 * (b % 2) + t, :]))
                    dve.sem_inc(block_out[b % 2], 1)
                norm(l * 4 + 4).then_inc(xn_ready, 1)
                lows(l, "ple", 8, hT_hi, hT_lo, gain=16)
                for b in range(4):
                    s = slice(b * NB, (b + 1) * NB)
                    dve.wait_ge(ple_sig, (l * 4 + b) * 2 + 2)
                    for t in range(TOK):
                        chain(v.tensor_tensor(reg1[:, t, s], reg1[:, t, s], sig[:, t, :], ALU.mult))
                    dve.sem_inc(ple_sig, 1)
                    dve.sem_inc(block_out[b % 2], 1)
                    for t in range(TOK):
                        chain(v.tensor_tensor(xs[:, t, s], xs[:, t, s], reg1[:, t, s], ALU.add))
                dve.sem_inc(layer_done, 1)
                chain.clear()
            mean_square(DEPTH * 4 + 1, 0, D)
            dve.wait_ge(fin_g_in, 16)
            for t in range(TOK):
                v.scalar_tensor_tensor(out=xn[:, t, :], in0=xs[:, t, :], scalar=st_r[:, t:t + 1], in1=fin_g,
                                       op0=ALU.mult, op1=ALU.mult).then_inc(out_ready, 1)


def constants():
    ident = np.eye(P, dtype=np.float32)
    q = np.arange(P)[:, None]
    k = np.arange(P)[None, :]
    masks = np.zeros((P, 3, 384), np.float32)
    for i, ok in enumerate((k <= q, k < q)):
        for c in (0, 256):
            masks[:, i, c:c + P] = np.where(ok, 0.0, NEG)
    masks[:, 2, :] = masks[:, 1, :] == 0.0
    pos = np.arange(SEQ, dtype=np.float32)
    inv = (np.float32(10000.0) ** (-np.arange(0, ROPE, 2, dtype=np.float32) / np.float32(ROPE))).astype(np.float32)
    ang = pos[:, None] * inv[None, :]
    rope = np.stack([np.cos(ang), np.sin(ang)], axis=1).astype(np.float32)
    rope = np.ascontiguousarray(rope.reshape(TOK, P, 2, ROPE // 2).transpose(1, 0, 2, 3))
    return {"ident": ident, "masks": masks, "rope": rope}


INS = ["x", "p", "ln_g", "w_in", "ssm_lam_re", "ssm_lam_im", "ssm_log_dt", "ssm_b_re", "ssm_b_im", "ssm_c_re",
       "ssm_c_im", "ssm_d", "ssm_w_glu", "mla_g_q", "mla_g_kv", "mla_w_uq", "mla_w_ukv", "w_branch", "w_out", "ple_g",
       "w_ple_gate", "w_ple_proj", "final_g"]


def kernel(**inputs):
    import concourse.bacc as bacc
    from concourse.bass_utils import run_bass_kernel_spmd

    nc = bacc.Bacc("TRN2", target_bir_lowering=False, num_devices=1)
    arrays, args = {}, []
    given = {**{n: inputs[n] for n in INS}, **constants()}
    for name, value in given.items():
        a = np.ascontiguousarray(value)
        arrays[f"in_{name}"] = a
        args.append(nc.dram_tensor(f"in_{name}", a.shape, mybir.dt.from_np(a.dtype), kind="ExternalInput").ap())
    args.append(nc.dram_tensor("out", (1, SEQ, D), mybir.dt.float32, kind="ExternalOutput").ap())
    build(nc, *args)
    r = run_bass_kernel_spmd(nc, [arrays], core_ids=[0])
    return r.results[0]["out"]
```

```python
import numpy as np
import concourse.bass as bass
from concourse import mybir
from contextlib import ExitStack


SEQ, D, DEPTH, W = 256, 2048, 2, 1024
P, TOK = 128, SEQ // 128
KT = D // P
PLE, LAT, ROPE, HEADS, HD = 256, 512, 64, 8, 128
GROUP, STATE = 16, 64
NTILE = W // GROUP * STATE // P
QUADS = NTILE // 4
LEVELS = 8
EPS = 1e-6
COL_KR = W + 2 * LAT
COL_SB = COL_KR + ROPE
COL_GATE = COL_SB + 3 * W
COL_MERGE = COL_GATE + 3 * W
NB = 512
HB = 3 * HD
RING = 4
SLOT = 2 * NB

STAGES = [("proj", 4, 8), ("lat", 8, 2), ("sb", 8, 8), ("gate", 8, 8), ("merge2", 8, 6), ("merge1", 8, 6),
          ("logit0", 1, 8), ("glu", 2, 4), ("branch0", 1, 4), ("merge0", 6, 6), ("out", 4, 8), ("pproj", 4, 1), ("ple", 4, 8)]
SLAB0, PAIR0 = {}, {}
SLABS = PAIRS = 0
_blocks_before = 0
for _name, _blocks, _per in STAGES:
    SLAB0[_name], PAIR0[_name] = SLABS, _blocks_before // 2
    SLABS += _blocks * _per
    _blocks_before += _blocks
PAIRS = _blocks_before // 2
STEPS = [("ln", 8), ("qlat", 2), ("kvlat", 2), ("ys2", 4), ("ys1", 4), ("glu", 4), ("ys0", 4), ("merged", 8),
         ("p", 2), ("ple", 8)]
STEP0 = {}
NSTEP = 0
for _name, _n in STEPS:
    STEP0[_name] = NSTEP
    NSTEP += _n
NG = 40

MLA_SCALE = float((HD + ROPE) ** -0.5)
SB_SCALE = float(HD ** -0.5)
NEG = -1e30
MAGIC = 1.5 * 2.0 ** 23
TWO_PI = 2 * np.pi
TP1 = 6.28125
TP2 = 0.0019350051879882812
TP3 = float(np.float32(TWO_PI - TP1 - TP2))
PI_LOW = 3.1415925


def build(nc, x, p, ln_g, w_in, lam_re, lam_im, log_dt, b_re, b_im, c_re, c_im, d_skip, w_glu, g_q, g_kv, w_uq,
          w_ukv, w_branch, w_out, ple_g, w_ple_gate, w_ple_proj, final_g, ident_in, masks_in, rope_in, out):
    f32, f32r = mybir.dt.float32, mybir.dt.float32r
    ALU, ACT, AX = mybir.AluOpType, mybir.ActivationFunctionType, mybir.AxisListType
    ds = bass.ds
    ctx = ExitStack()
    with ctx:
        def sb(name, shape, dt=f32):
            return ctx.enter_context(nc.sbuf_tensor(name, shape, dt))

        def sem(name):
            return ctx.enter_context(nc.semaphore(name))

        x_keep = nc.dram_tensor("x_keep", [SEQ, D], f32, kind="Internal").ap()

        raw = sb("raw", [P, RING, SLOT])
        w_hi = sb("w_hi", [P, RING, SLOT], f32r)
        w_lo = sb("w_lo", [P, RING, SLOT], f32r)
        hT_hi = sb("hT_hi", [P, KT, SEQ], f32r)
        hT_lo = sb("hT_lo", [P, KT, SEQ], f32r)
        yT_hi = sb("yT_hi", [P, 8, SEQ], f32r)
        yT_lo = sb("yT_lo", [P, 8, SEQ], f32r)
        ys = sb("ys", [P, TOK, 3, W])
        ys_flat = ys[:, :, :, :].rearrange("p t b w -> p (t b w)")
        xn = ys_flat[:, 0:TOK * D].rearrange("p (t d) -> p t d", t=TOK)
        junk = ys_flat[:, TOK * D:TOK * D + D]
        gate_ssm = sb("gate_ssm", [P, TOK, W])
        p_in = gate_ssm[:, :, 0:PLE]
        fin_g = gate_ssm[:, :, :].rearrange("p t w -> p (t w)")
        reg1 = sb("reg1", [P, TOK, D])
        reg2 = sb("reg2", [P, 8192])
        lat = reg1[:, :, 0:2 * LAT]
        sb_qk = reg1[:, :, :].rearrange("p t (h c) -> p t h c", h=HEADS)
        merged = reg1
        xs = reg2[:, 0:TOK * D].rearrange("p (t d) -> p t d", t=TOK)
        mla_q = reg2[:, 0:3072].rearrange("p (t c) -> p t c", t=TOK)
        mla_kv = reg2[:, 3072:7168].rearrange("p (t c) -> p t c", t=TOK)
        kr = reg2[:, 7168:7296].rearrange("p (t c) -> p t c", t=TOK)
        rope_a = reg2[:, 7296:7552]
        rope_b = reg2[:, 7552:7808]
        rope_c = reg2[:, 7808:8064]
        gates = reg2[:, 0:6144].rearrange("p (t b w) -> p t b w", t=TOK, b=3)
        tab = reg2[:, 0:2048].rearrange("p (c n) -> p c n", c=2)
        tab4 = reg2[:, 0:2048].rearrange("p (c j t) -> p c j t", c=2, j=4)
        st = reg2[:, 2048:4096].rearrange("p (c n) -> p c n", c=2)
        pr1 = reg2[:, 4096:6144].rearrange("p (c n) -> p c n", c=2)
        pr2 = reg2[:, 6144:8192].rearrange("p (c n) -> p c n", c=2)

        scr = sb("scr", [P, 4480])
        q_s = scr[:, 0:384].rearrange("p (t c) -> p t c", t=TOK)
        k_s = scr[:, 384:640].rearrange("p (t c) -> p t c", t=TOK)
        qk_s = scr[:, 0:512].rearrange("p (t c) -> p t c", t=TOK)
        qkT = scr[:, 640:1152]
        qrT = scr[0:ROPE, 1152:1408]
        krT = scr[0:ROPE, 1408:1664]
        s_a = scr[:, 1664:2048]
        s_b = scr[:, 2048:2432]
        s_c = scr[:, 2432:2816]
        pT = scr[:, 2816:3200]
        sig = scr[:, 0:1024].rearrange("p (t c) -> p t c", t=TOK)
        sig2 = scr[:, 1280:2304].rearrange("p (t c) -> p t c", t=TOK)
        u_q = scr[:, 1024:1280].rearrange("p (t c) -> p t c", t=TOK)
        uT = scr[:, 1280:1536]
        bbT = scr[:, 1536:2560].rearrange("p (c j s) -> p c j s", c=2, j=4)
        b_ld = scr[:, 2560:2688].rearrange("p (c j h) -> p c j h", c=2, j=4)
        c_ld = scr[:, 2688:2944].rearrange("p (c s) -> p c s", c=2)
        b_t1 = scr[:, 2944:3072].rearrange("p (c j h) -> p c j h", c=2, j=4)
        b_t2 = scr[:, 3072:3200].rearrange("p (c j h) -> p c j h", c=2, j=4)
        d_q = scr[:, 3200:3328]
        y_q = scr[:, 3328:3584].rearrange("p (t c) -> p t c", t=TOK)
        bb = scr[:, 3968:4224].rearrange("p (c j h) -> p c j h", c=2, j=4)
        cbd = scr[:, 4224:4480].rearrange("p (c j h) -> p c j h", c=2, j=4)
        ident = sb("ident", [P, P])
        masks = sb("masks", [P, 3, 384])
        rope_t = sb("rope_t", [P, TOK, 2, ROPE // 2])
        rowsel = sb("rowsel", [P, 4])
        g_rows = sb("g_rows", [DEPTH * NG, P])
        g_all = sb("g_all", [P, DEPTH * NG])
        gc = sb("gc", [P, NG])
        lam_rows = sb("lam_rows", [NTILE, 2, P])
        dt_rows = sb("dt_rows", [NTILE, 2])
        dt_wide = sb("dt_wide", [NTILE, 2, STATE])
        lam = sb("lam", [P, 3, NTILE])
        prm = sb("prm", [P, 3, NTILE])
        prm_q = sb("prm_q", [P, 3, 4])
        pw = sb("pw", [P, LEVELS, 2, NTILE])
        pw_q = sb("pw_q", [P, LEVELS, 2, 4])
        sm = sb("sm", [P, 8, NTILE])
        st_ss = sb("st_ss", [P, 4])
        st_p = sb("st_p", [P, TOK, D // NB])
        st_r = sb("st_r", [P, 4])
        mx = sb("mx", [P, 2])
        nmx = sb("nmx", [P, 2])
        sums = sb("sums", [P, 2])
        rsum = sb("rsum", [P, 2])
        one = sb("one", [P, 1])

        main = ctx.enter_context(nc.psum_tensor("main", [P, 4, NB], f32))
        trb = ctx.enter_context(nc.psum_tensor("trb", [P, 2, NB], f32))
        aux = ctx.enter_context(nc.psum_tensor("aux", [P, 2, NB], f32))

        raw_loaded = [sem(f"raw_loaded{i}") for i in range(RING)]
        hi_ready, lo_ready, slab_used = sem("hi_ready"), sem("lo_ready"), sem("slab_used")
        block_out = [sem("pair_a_out"), sem("pair_b_out")]
        tr_in, tr_hi, tr_lo = sem("tr_in"), sem("tr_hi"), sem("tr_lo")
        consts_in, gains_in, x_in, x_kept, x_back, s5_rows_in = (sem(n) for n in (
            "consts_in", "gains_in", "x_in", "x_kept", "x_back", "s5_rows_in"))
        p_loaded, fin_g_in, out_done = sem("p_loaded"), sem("fin_g_in"), sem("out_done")
        act_chain, dve_chain = sem("act_chain"), sem("dve_chain")
        gains_t, gains_ready = sem("gains_t"), sem("gains_ready")
        sq_done, ms_ready, root_ready, xn_ready = sem("sq_done"), sem("ms_ready"), sem("root_ready"), sem("xn_ready")
        dt_wide_ready, s5_cols_in, s5_lam_ready, s5_exp_ready = (sem(n) for n in (
            "dt_wide_ready", "s5_cols_in", "s5_lam_ready", "s5_exp_ready"))
        s5_ang_ready, s5_trig_ready, s5_prm_ready = sem("s5_ang_ready"), sem("s5_trig_ready"), sem("s5_prm_ready")
        lat_norm, kr_ready, kr_t, kr_out, mla_in = (sem(n) for n in (
            "lat_norm", "kr_ready", "kr_t", "kr_out", "mla_in"))
        h_static, h_qkT_in, h_qkT, h_scores, h_max, h_probs, h_pT_in, h_pT, h_o_in, h_o_out = (sem(n) for n in (
            "h_static", "h_qkT_in", "h_qkT", "h_scores", "h_max", "h_probs", "h_pT_in", "h_pT", "h_o_in", "h_o_out"))
        sb_soft, sb_arg = sem("sb_soft"), sem("sb_arg")
        silu_done, lat_sq, x_block = sem("silu_done"), sem("lat_sq"), sem("x_block")
        ys_ready = sem("ys_ready")
        q_ld, q_static, q_bb, q_T_in, q_T_out, q_bu, q_bu_used, q_h, q_y, q_y_out = (sem(n) for n in (
            "q_ld", "q_static", "q_bb", "q_T_in", "q_T_out", "q_bu", "q_bu_used", "q_h", "q_y", "q_y_out"))
        sig_ready, sig_used = sem("sig_ready"), sem("sig_used")
        gelu_ready, glu_sig, merged_ready = sem("gelu_ready"), sem("glu_sig"), sem("merged_ready")
        ple_sig = sem("ple_sig")
        layer_done, out_ready = sem("layer_done"), sem("out_ready")

        pe_mark, dve_mark = sem("pe_mark"), sem("dve_mark")

        class Chain:
            def __init__(self, eng, s):
                self.eng, self.s, self.n = eng, s, 0

            def put(self, ins):
                ins.then_inc(self.s, 1)
                self.n += 1

            def sync(self):
                self.eng.wait_ge(self.s, self.n)

            def __call__(self, ins):
                self.put(ins)
                self.sync()

            def clear(self):
                self.eng.sem_clear(self.s)
                self.n = 0

        block = ctx.enter_context(nc.Block())

        @block.sync
        def _(sp):
            sp.dma_start(reg2[:, 0:TOK * D].rearrange("p (t d) -> p t d", t=TOK),
                         x.rearrange("b (t p) d -> p (b t) d", p=P)).then_inc(x_in, 16)
            sp.dma_start(ident[:, :], ident_in).then_inc(consts_in, 16)
            for l in range(DEPTH):
                for src, at, n in ((ln_g, 0, 16), (ple_g, 16, 16), (g_q, 32, 4), (g_kv, 36, 4)):
                    sp.dma_start(g_rows[l * NG + at:l * NG + at + n, :],
                                 src[l, :].rearrange("(k p) -> k p", p=P)).then_inc(gains_in, 16)
            sp.dma_start(masks[:, :, :], masks_in).then_inc(consts_in, 16)
            sp.dma_start(rope_t[:, :, :, :], rope_in).then_inc(consts_in, 16)

            def slab(l, seg, j, it, per, dst, src):
                sp.wait_ge(lo_ready, l * SLABS + it * per + (SLAB0[seg] + j + 1))
                slot = (SLAB0[seg] + j) % RING
                sp.dma_start(dst(raw[:, slot, :]), src).then_inc(raw_loaded[slot], 16)

            def full(r):
                return r.rearrange("p (k n) -> p k n", k=2)

            def head_dst(r):
                return r[:, 0:2 * HB].rearrange("p (c n) -> p c n", c=3)

            def cols(w, l, k0, nk, c0, nc_):
                return w[ds(l, 1), k0 * P:(k0 + nk) * P, ds(c0, nc_)].rearrange("o (k p) n -> p (o k) n", p=P)

            with sp.Fori(0, DEPTH) as l:
                if True:
                    for c, lm in enumerate((lam_re, lam_im)):
                        sp.dma_start(lam_rows[:, c, :], lm[ds(l, 1), :, :].rearrange("o (j g) s -> (o j) (g s)", g=2))\
                          .then_inc(s5_rows_in, 16)
                    sp.dma_start(dt_rows[:, :], log_dt[ds(l, 1), :].rearrange("o (j g) -> (o j) g", g=2))\
                      .then_inc(s5_rows_in, 16)
                with sp.Fori(0, 2) as it:
                    for b in range(2):
                        for j in range(8):
                            slab(l, "proj", 8 * b + j, it, 16, full, cols(w_in, l, 2 * j, 2, it * 1024 + b * NB, NB))
                for j in range(2):
                    slab(l, "lat", j, 0, 0, lambda r: r[:, 0:8 * ROPE].rearrange("p (k n) -> p k n", k=8),
                         cols(w_in, l, 8 * j, 8, COL_KR, ROPE))
                for b in range(7):
                    w, c0 = (w_uq, b * NB) if b < 3 else (w_ukv, (b - 3) * NB)
                    for j in range(2):
                        slab(l, "lat", 2 + 2 * b + j, 0, 0, full, cols(w, l, 2 * j, 2, c0, NB))
                for seg, col in (("sb", COL_SB), ("gate", COL_GATE)):
                    with sp.Fori(0, HEADS // 2) as it:
                        for j in range(KT):
                            src = w_in[ds(l, 1), j * P:(j + 1) * P, col:col + 3 * W]
                            src = src.rearrange("o p (c n) -> (o p) c n", c=3)
                            slab(l, seg, j, it, 16, head_dst, src[:, :, ds(it * 2 * HD, 2 * HD)])

                def merge(br):
                    seg = f"merge{br}"
                    with sp.Fori(0 if br else 1, 4) as n:
                        for j in range(8):
                            if br and j == RING:
                                q = n + 4 * (2 - br)
                                sp.wait_ge(ys_ready, l * 4 + 2)
                                sp.wait_ge(q_T_out, l * QUADS + q + 1)
                                for c, bm in enumerate((b_re, b_im)):
                                    sp.dma_start(b_ld[:, c, :, :],
                                                 bm[ds(l, 1), ds(q * 8, 8), :, :]
                                                 .rearrange("o (j g) s h -> (g s) (o j) h", g=2)).then_inc(q_ld, 16)
                                for c, cm in enumerate((c_re, c_im)):
                                    for half in range(2):
                                        sp.dma_start(c_ld[:, c, half * STATE:(half + 1) * STATE],
                                                     cm[ds(l, 1), ds(q * 8, 8), :, :].rearrange("o g h s -> (o g h) s"))\
                                          .then_inc(q_ld, 16)
                                sp.dma_start(d_q, d_skip[ds(l, 1), ds(q * P, P)].broadcast_to([P, P])).then_inc(q_ld, 16)
                            slab(l, seg, j + (0 if br else -12), n, 12, full,
                                 cols(w_in, l, 2 * j, 2, COL_MERGE + br * D + n * NB, NB))
                        for j in range(4):
                            src = w_branch[ds(l, 1), br, 2 * j * P:(2 * j + 2) * P, ds(n * NB, NB)]
                            slab(l, seg, 8 + j + (0 if br else -12), n, 12, full, src.rearrange("o (k p) n -> p (o k) n", p=P))

                merge(2)
                merge(1)
                for j in range(8):
                    slab(l, "logit0", j, 0, 0, full, cols(w_in, l, 2 * j, 2, COL_MERGE, NB))
                for b in range(2):
                    for j in range(4):
                        slab(l, "glu", 4 * b + j, 0, 0, full, cols(w_glu, l, 2 * j, 2, b * NB, NB))
                for j in range(4):
                    src = w_branch[ds(l, 1), 0, 2 * j * P:(2 * j + 2) * P, 0:NB]
                    slab(l, "branch0", j, 0, 0, full, src.rearrange("o (k p) n -> p (o k) n", p=P))
                merge(0)
                sp.wait_ge(q_y_out, l * QUADS + QUADS)
                sp.wait_ge(x_kept, l * 16 + 16)
                sp.dma_start(xs, x_keep.rearrange("(t p) d -> p t d", p=P)).then_inc(x_back, 16)
                with sp.Fori(0, 2) as it:
                    for b in range(2):
                        for j in range(8):
                            slab(l, "out", 8 * b + j, it, 16, full, cols(w_out, l, 2 * j, 2, it * 1024 + b * NB, NB))
                sp.wait_ge(ys_ready, l * 4 + 4)
                sp.dma_start(p_in, p[ds(l, 1), 0, :, :].rearrange("o (t p) c -> p (o t) c", p=P)).then_inc(p_loaded, 16)
                for b in range(4):
                    slab(l, "pproj", b, 0, 0, full, cols(w_ple_proj, l, 0, 2, b * NB, NB))
                with sp.Fori(0, 2) as it:
                    for b in range(2):
                        for j in range(8):
                            slab(l, "ple", 8 * b + j, it, 16, full,
                                 cols(w_ple_gate, l, 2 * j, 2, it * 1024 + b * NB, NB))
            sp.wait_ge(tr_in, DEPTH * NSTEP)
            sp.dma_start(fin_g, final_g.rearrange("(o n) -> o n", o=1).broadcast_to([P, D])).then_inc(fin_g_in, 16)
            for t in range(TOK):
                sp.wait_ge(out_ready, t + 1)
                sp.dma_start(out[0, t * P:(t + 1) * P, :], xn[:, t, :]).then_inc(out_done, 16)
            sp.wait_ge(out_done, 16 * TOK)

        @block.gpsimd
        def _(pool):
            pool.sem_inc(lo_ready, RING)
            with pool.Fori(0, DEPTH) as l:
                def lows(g0, groups, n):
                    with pool.Fori(0, groups) as g:
                        for slot in range(RING):
                            i = l * SLABS + g * RING + (g0 * RING + slot)
                            pool.wait_ge(slab_used, i + 1)
                            pool.wait_ge(hi_ready, i + 1)
                            nc.gpsimd.tensor_tensor(w_lo[:, slot, 0:n], raw[:, slot, 0:n],
                                                    w_hi[:, slot, 0:n].bitcast(f32), ALU.subtract)\
                              .then_inc(lo_ready, 1)
                g1, g2, g3 = SLAB0["sb"] // RING, SLAB0["merge2"] // RING, SLABS // RING
                lows(0, g1, SLOT)
                lows(g1, g2 - g1, 2 * HB)
                lows(g2, g3 - g2, SLOT)

        @block.tensor
        def _(pe):
            pe.sem_inc(slab_used, RING)
            pe.sem_inc(block_out[0], 1)
            pe.sem_inc(block_out[1], 1)
            pe.sem_inc(tr_lo, 2)
            pe.sem_inc(h_o_out, 1)
            pe.wait_ge(consts_in, 48)
            pe.wait_ge(gains_in, 16 * 4 * DEPTH)
            nc.tensor.transpose(aux[:, 0, 0:DEPTH * NG], g_rows[:, :], ident[0:DEPTH * NG, 0:DEPTH * NG])\
              .then_inc(gains_t, 1)

            def products(l, seg, j, it, per, pair, ks, n, first, last, big=True):
                slot = (SLAB0[seg] + j) % RING
                hi, lo = (hT_hi, hT_lo) if big else (yT_hi, yT_lo)
                pe.wait_ge(lo_ready, l * SLABS + it * per + (SLAB0[seg] + j + 1 + RING))
                for i, k in enumerate(ks):
                    wh, wl = (w[:, slot, i * n:(i + 1) * n] for w in (w_hi, w_lo))
                    for t in range(TOK):
                        o = main[:, 2 * pair + t, 0:n]
                        a, b = (z[:, k, t * P:(t + 1) * P] for z in (hi, lo))
                        f, e = first and i == 0, last and i == len(ks) - 1
                        nc.tensor.matmul(o, a, wh, start=f, stop=False)
                        nc.tensor.matmul(o, a, wl, start=False, stop=False)
                        m = nc.tensor.matmul(o, b, wh, start=False, stop=e)
                m.then_inc(slab_used, 1)

            def pair_free(l, seg, it, b):
                pe.wait_ge(block_out[b % 2], l * PAIRS + it + (PAIR0[seg] + b // 2 + 1))

            def whole_block(l, seg, b, it, per, nslab, n=NB, big=True, k0=0, after=None):
                pair_free(l, seg, it, b)
                for j in range(nslab):
                    if after:
                        transposed(l, after, j + 1)
                    products(l, seg, nslab * b + j, it, per, b % 2, (k0 + 2 * j, k0 + 2 * j + 1), n, j == 0,
                             j == nslab - 1, big)

            def two_heads_products(l, seg, j, it):
                slot = (SLAB0[seg] + j) % RING
                pe.wait_ge(lo_ready, l * SLABS + it * 16 + (SLAB0[seg] + j + 1 + RING))
                for b in range(2):
                    if j == 0:
                        pair_free(l, seg, it, b)
                    wh, wl = (w[:, slot, 0:2 * HB].rearrange("p (c n) -> p c n", c=3)[:, :, b * HD:(b + 1) * HD]
                              for w in (w_hi, w_lo))
                    for t in range(TOK):
                        o = main[:, 2 * b + t, 0:HB].rearrange("p (c n) -> p c n", c=3)
                        x_hi, x_lo = (z[:, j, t * P:(t + 1) * P] for z in (hT_hi, hT_lo))
                        nc.tensor.matmul(o, x_hi, wh, start=j == 0, stop=False)
                        nc.tensor.matmul(o, x_hi, wl, start=False, stop=False)
                        m = nc.tensor.matmul(o, x_lo, wh, start=False, stop=j == KT - 1)
                m.then_inc(slab_used, 1)

            def transposes(l, seg, src, steps, per=2, at=0):
                for i in range(at, at + steps):
                    n = STEP0[seg] + i
                    pe.wait_ge(tr_lo, l * NSTEP + (n + 1))
                    for k in range(per):
                        for t in range(TOK):
                            m = nc.tensor.transpose(trb[:, n % 2, (2 * k + t) * P:(2 * k + t + 1) * P],
                                                    src(t)[:, (per * i + k) * P:(per * i + k + 1) * P], ident[:, :])
                    m.then_inc(tr_in, 1)

            def transposed(l, seg, steps):
                pe.wait_ge(tr_lo, l * NSTEP + (STEP0[seg] + steps + 2))

            with pe.Fori(0, DEPTH) as l:
                pe.wait_ge(xn_ready, l * 2 + 1)
                transposes(l, "ln", lambda t: xn[:, t, :], 8)
                pe.wait_ge(gains_ready, 1)
                pe.wait_ge(dt_wide_ready, l + 1)
                pe.sem_inc(pe_mark, 1)
                for c in range(2):
                    nc.tensor.transpose(aux[:, 0, c * NTILE:(c + 1) * NTILE], lam_rows[:, c, :],
                                        ident[0:NTILE, 0:NTILE])
                nc.tensor.transpose(aux[:, 0, 2 * NTILE:3 * NTILE], dt_wide[:, :, :].rearrange("j g s -> j (g s)"),
                                    ident[0:NTILE, 0:NTILE]).then_inc(s5_cols_in, 1)
                with pe.Fori(0, 2) as it:
                    for b in range(2):
                        whole_block(l, "proj", b, it, 16, 8, after=None if b else "ln")
                pair_free(l, "lat", 0, 0)
                for j in range(2):
                    products(l, "lat", j, 0, 0, 0, range(8 * j, 8 * j + 8), ROPE, j == 0, j == 1)
                pe.wait_ge(lat_norm, l * 2 + 1)
                transposes(l, "qlat", lambda t: lat[:, t, 0:LAT], 2)
                pe.wait_ge(lat_norm, l * 2 + 2)
                transposes(l, "kvlat", lambda t: lat[:, t, LAT:2 * LAT], 2)
                transposed(l, "qlat", 2)
                for b in range(1, 8):
                    if b == 4:
                        transposed(l, "kvlat", 2)
                    whole_block(l, "lat", b, 0, 0, 2, big=False, k0=0 if b < 4 else 4)
                pe.wait_ge(kr_ready, l + 1)
                pe.sem_inc(pe_mark, 1)
                for t in range(TOK):
                    m = nc.tensor.transpose(aux[0:ROPE, 0, t * P:(t + 1) * P], kr[:, t, :], ident[:, :])
                m.then_inc(kr_t, 1)

                def head_transposes(n, rope):
                    pe.wait_ge(h_static, n + 1)
                    pe.wait_ge(h_o_out, n + 1)
                    for i, z in enumerate((q_s, k_s) if rope else (qk_s, qk_s)):
                        for t in range(TOK):
                            c = 0 if rope or i == 0 else P
                            m = nc.tensor.transpose(trb[:, 0, (2 * i + t) * P:(2 * i + t + 1) * P],
                                                    z[:, t, c:c + P], ident[:, :])
                    if rope:
                        for t in range(TOK):
                            m = nc.tensor.transpose(trb[0:ROPE, 1, t * P:(t + 1) * P], q_s[:, t, P:P + ROPE],
                                                    ident[:, :])
                    m.then_inc(h_qkT_in, 1)

                def head_scores(n, rope):
                    pe.wait_ge(h_qkT, n + 1)
                    for t, (c, nk) in enumerate(((0, P), (P, 2 * P))):
                        m = nc.tensor.matmul(aux[:, 0, c:c + nk], qkT[:, t * P:(t + 1) * P], qkT[:, 256:256 + nk],
                                             start=True, stop=not rope)
                        if rope:
                            m = nc.tensor.matmul(aux[:, 0, c:c + nk], qrT[:, t * P:(t + 1) * P], krT[:, 0:nk],
                                                 start=False, stop=True)
                    m.then_inc(h_scores, 1)

                def head_probs(n):
                    pe.wait_ge(h_probs, n + 1)
                    for i in range(3):
                        m = nc.tensor.transpose(aux[:, 1, i * P:(i + 1) * P], s_b[:, i * P:(i + 1) * P], ident[:, :])
                    m.then_inc(h_pT_in, 1)

                def head_out(n, v):
                    pe.wait_ge(h_pT, n + 1)
                    nc.tensor.matmul(trb[:, 1, 256:384], pT[:, 0:P], v(0), start=True, stop=True)
                    nc.tensor.matmul(trb[:, 1, 384:512], pT[:, P:2 * P], v(0), start=True, stop=False)
                    nc.tensor.matmul(trb[:, 1, 384:512], pT[:, 2 * P:3 * P], v(1), start=False, stop=True)\
                      .then_inc(h_o_in, 1)

                for seg in ("sb", "gate"):
                    mla = seg == "sb"
                    if mla:
                        pe.wait_ge(kr_out, l + 1)
                        pe.wait_ge(mla_in, l + 1)
                        pe.sem_inc(pe_mark, 1)
                    with pe.Fori(0, HEADS // 2) as it:
                        for b in range(2):
                            n = l * 2 * HEADS + it * 2 + (b if mla else HEADS + b)
                            for j in range(8):
                                two_heads_products(l, seg, 8 * b + j, it)
                                if j == 0:
                                    head_transposes(n, mla)
                                if j == 2:
                                    head_scores(n, mla)
                                if j == (5 if mla else 6):
                                    head_probs(n)
                            if mla:
                                head_out(n, lambda t: mla_kv[:, t, ds(it * 4 * HD + (2 * b + 1) * HD, HD)])
                            else:
                                head_out(n, lambda t: ys[:, t, 2, ds(it * 2 * HD + b * HD, HD)])

                def merge_step(br, n, first, j0=0):
                    seg = f"merge{br}"
                    q = l * QUADS + n + 4 * (2 - br)
                    for j in range(12):
                        if j in (0, 8):
                            pair_free(l, seg, n, j // 8 + j0 // 6)
                        if j >= 8:
                            transposed(l, f"ys{br}", j - 7)
                        ks = (2 * j, 2 * j + 1) if j < 8 else (2 * j - 16, 2 * j - 15)
                        products(l, seg, j + j0, n, 12, j // 8, ks, NB, j in (0, 8), j in (7, 11), j < 8)
                        if br and j == 1:
                            pe.wait_ge(q_bb, q + 1)
                            for t in range(TOK):
                                nc.tensor.transpose(aux[:, 0, t * P:(t + 1) * P], u_q[:, t, :], ident[:, :])
                            for c in range(2):
                                nc.tensor.transpose(aux[:, 0, (2 + c) * P:(3 + c) * P],
                                                    bb[:, c, :, :].rearrange("p j h -> p (j h)"), ident[:, :])
                            for c in range(2):
                                m = nc.tensor.transpose(aux[:, 1, c * P:(c + 1) * P], c_ld[:, c, :], ident[:, :])
                            m.then_inc(q_T_in, 1)
                        if br and j in (3, 6):
                            half = j // 6
                            if half == 0:
                                pe.wait_ge(q_T_out, q + 2)
                            else:
                                pe.wait_ge(q_bu_used, q * 2 + 1)
                            for c in range(2):
                                for i in range(2):
                                    m = nc.tensor.matmul(aux[:, c, i * SEQ:(i + 1) * SEQ],
                                                         bbT[:, c, 2 * half + i, :], uT, start=True, stop=True)
                            m.then_inc(q_bu, 1)
                        if first and j == 5:
                            pe.wait_ge(ys_ready, l * 4 + (3 - br))
                            transposes(l, f"ys{br}", lambda t: ys[:, t, br, :], 4)
                    if br:
                        pe.wait_ge(q_h, q + 1)
                        for t in range(TOK):
                            for i in range(4):
                                for c in range(2):
                                    m = nc.tensor.matmul(aux[:, 0, t * P + i * 32:t * P + (i + 1) * 32],
                                                         pr1[:, c, i * SEQ + t * P:i * SEQ + (t + 1) * P],
                                                         cbd[:, c, i, :], start=c == 0, stop=c == 1)
                        m.then_inc(q_y, 1)

                for br in (2, 1):
                    merge_step(br, 0, True)
                    with pe.Fori(1, 4) as n:
                        merge_step(br, n, False)
                pair_free(l, "logit0", 0, 0)
                for j in range(8):
                    products(l, "logit0", j, 0, 0, 0, (2 * j, 2 * j + 1), NB, j == 0, j == 7)
                    if j == 5:
                        pe.wait_ge(gelu_ready, l + 1)
                        transposes(l, "glu", lambda t: ys[:, t, 0, :], 4)
                for b in range(2):
                    pe.wait_ge(block_out[1 - b], l * PAIRS + (PAIR0["logit0"] + b + 1))
                    for j in range(4):
                        transposed(l, "glu", j + 1)
                        products(l, "glu", 4 * b + j, 0, 0, 1 - b, (2 * j, 2 * j + 1), NB, j == 0, j == 3, False)
                pe.wait_ge(block_out[1], l * PAIRS + (PAIR0["logit0"] + 2))
                for i in range(2):
                    pe.wait_ge(ys_ready, l * 4 + (3 + i))
                    transposes(l, "ys0", lambda t: ys[:, t, 0, :], 2, at=2 * i)
                for j in range(4):
                    transposed(l, "ys0", j + 1)
                    products(l, "branch0", j, 0, 0, 1, (2 * j, 2 * j + 1), NB, j == 0, j == 3, False)
                with pe.Fori(1, 4) as n:
                    merge_step(0, n, False, j0=-12)
                pe.wait_ge(merged_ready, l * 4 + 4)
                transposes(l, "merged", lambda t: merged[:, t, :], 8)
                with pe.Fori(0, 2) as it:
                    for b in range(2):
                        whole_block(l, "out", b, it, 16, 8, after=None if b else "merged")
                pe.wait_ge(p_loaded, l * 16 + 16)
                transposes(l, "p", lambda t: p_in[:, t, :], 2, per=1)
                transposed(l, "p", 2)
                for b in range(4):
                    pair_free(l, "pproj", 0, b)
                    products(l, "pproj", b, 0, 0, b % 2, (0, 1), NB, True, True, False)
                pe.wait_ge(xn_ready, l * 2 + 2)
                transposes(l, "ple", lambda t: xn[:, t, :], 8)
                with pe.Fori(0, 2) as it:
                    for b in range(2):
                        whole_block(l, "ple", b, it, 16, 8, after=None if b else "ple")

        def used(l, seg, j, it=0, per=0):
            return l * SLABS + it * per + (SLAB0[seg] + j + 1 + RING)

        @block.scalar
        def _(act):
            A = nc.scalar.activation
            chain = Chain(act, act_chain)

            def split(l, seg, j, it=0, per=0):
                at = SLAB0[seg] + j
                slot = at % RING
                n = 2 * HB if SLAB0["sb"] <= at < SLAB0["merge2"] and not (seg == "gate" and j >= per) else SLOT
                i = l * SLABS + it * per + at
                act.wait_ge(raw_loaded[slot], (l * (SLABS // RING) + it * (per // RING) + (at // RING + 1)) * 16)
                act.wait_ge(slab_used, i + 1)
                A(w_hi[:, slot, 0:n], raw[:, slot, 0:n], ACT.Copy).then_inc(hi_ready, 1)

            def splits(l, seg, a, b, it=0, per=0):
                for j in range(a, b):
                    split(l, seg, j, it, per)

            def squares(b):
                for t in range(TOK):
                    m = A(junk[:, t * NB:(t + 1) * NB], xs[:, t, ds(b * NB, NB)], ACT.Square,
                          accum_out=st_p[:, t, ds(b, 1)])
                m.then_inc(sq_done, 1)

            def root(value, at):
                act.wait_ge(ms_ready, value)
                A(st_r[:, at:at + 2], st_ss[:, at:at + 2], ACT.Sqrt).then_inc(root_ready, 1)

            def highs(l, seg, steps, dst, per=2, gain=None, k0=0):
                for i in range(steps):
                    n = STEP0[seg] + i
                    act.wait_ge(tr_in, l * NSTEP + (n + 1))
                    for k in range(per):
                        kk = k0 + per * i + k
                        s = 1.0 if gain is None else gc[:, gain + per * i + k:gain + per * i + k + 1]
                        m = A(dst[:, kk, :], trb[:, n % 2, 2 * k * P:(2 * k + 2) * P], ACT.Copy, scale=s)
                    m.then_inc(tr_hi, 1)

            act.wait_ge(x_in, 16)
            for b in range(D // NB):
                act.wait_ge(sq_done, b + 1)
                squares(b)
            with act.Fori(0, DEPTH) as l:
                splits(l, "proj", 0, RING)
                act.wait_ge(layer_done, l + 1)
                act.dma_start(x_keep.rearrange("(t p) d -> p t d", p=P), xs).then_inc(x_kept, 16)
                root(l * 4 + 1, 0)
                highs(l, "ln", 8, hT_hi, gain=0)
                splits(l, "proj", RING, 8)
                act.wait_ge(s5_lam_ready, l * 2 + 1)
                A(sm[:, 0, :], lam[:, 2, :], ACT.Exp).then_inc(s5_exp_ready, 1)
                splits(l, "proj", 8, 12)
                act.wait_ge(s5_lam_ready, l * 2 + 2)
                A(prm[:, 0, :], sm[:, 1, :], ACT.Exp).then_inc(s5_exp_ready, 1)
                act.wait_ge(s5_ang_ready, l + 1)
                A(pw[:, 0, 1, :], sm[:, 2, :], ACT.Sin)
                A(pw[:, 0, 0, :], sm[:, 3, :], ACT.Sin).then_inc(s5_trig_ready, 1)
                splits(l, "proj", 12, 24 + RING)
                for b in range(2):
                    act.wait_ge(slab_used, used(l, "proj", 16 + 8 * b + 7))
                    for t in range(TOK):
                        m = A(junk[:, t * NB:(t + 1) * NB], main[:, 2 * b + t, :], ACT.Square,
                              accum_out=st_ss[:, 2 * (1 - b) + t:2 * (1 - b) + t + 1])
                    m.then_inc(lat_sq, 1)
                    root(l * 4 + 2 + b, 2 * (1 - b))
                    if b == 0:
                        splits(l, "proj", 24 + RING, 32 + RING)
                highs(l, "qlat", 2, yT_hi, gain=32)
                highs(l, "kvlat", 2, yT_hi, gain=36, k0=4)
                splits(l, "lat", RING, 16 + RING)
                act.wait_ge(kr_t, l + 1)
                A(krT, aux[0:ROPE, 0, 0:SEQ], ACT.Copy).then_inc(kr_out, 1)

                with act.Fori(0, HEADS // 2) as it:
                    for b in range(2):
                        n = l * 2 * HEADS + it * 2 + b
                        splits(l, "sb", 8 * b + 4, 8 * b + 5, it, 16)
                        act.wait_ge(h_qkT_in, n + 1)
                        A(qkT[:, 0:256], trb[:, 0, 0:256], ACT.Copy, scale=MLA_SCALE)
                        A(qkT[:, 256:512], trb[:, 0, 256:512], ACT.Copy)
                        A(qrT, trb[0:ROPE, 1, 0:256], ACT.Copy, scale=MLA_SCALE).then_inc(h_qkT, 1)
                        splits(l, "sb", 8 * b + 5, 8 * b + 8, it, 16)
                        act.wait_ge(h_max, l * HEADS + it * 2 + (b + 1))
                        A(s_b[:, 0:P], s_a[:, 0:P], ACT.Exp, bias=nmx[:, 0:1], accum_out=sums[:, 0:1])
                        A(s_b[:, P:384], s_a[:, P:384], ACT.Exp, bias=nmx[:, 1:2], accum_out=sums[:, 1:2])\
                            .then_inc(h_probs, 1)
                        splits(l, "sb", 8 * b + 8, 8 * b + 10, it, 16)
                        act.wait_ge(h_pT_in, n + 1)
                        A(pT, aux[:, 1, 0:384], ACT.Copy).then_inc(h_pT, 1)
                        splits(l, "sb", 8 * b + 10, 8 * b + 11, it, 16)
                        if b == 1:
                            act.wait_ge(slab_used, used(l, "sb", 15, it, 16))
                            A(sb_qk[:, :, ds(it * 2, 1), :].rearrange("p t o c -> p t (o c)"), main[:, 0:2, 0:256],
                              ACT.Copy)
                            A(ys[:, :, 2, ds(it * 256, HD)], main[:, 0:2, 256:384], ACT.Copy)\
                                .then_inc(block_out[0], 1)
                        splits(l, "sb", 8 * b + 11, 8 * b + 12, it, 16)
                with act.Fori(0, HEADS // 2) as it:
                    for b in range(2):
                        n = l * 2 * HEADS + it * 2 + (HEADS + b)
                        g = l * HEADS + it * 2 + b
                        chain.clear()
                        splits(l, "gate", 8 * b + 4, 8 * b + 5, it, 16)
                        act.wait_ge(h_qkT_in, n + 1)
                        A(qkT[:, 0:256], trb[:, 0, 0:256], ACT.Copy, scale=SB_SCALE)
                        A(qkT[:, 256:512], trb[:, 0, 256:512], ACT.Copy).then_inc(h_qkT, 1)
                        splits(l, "gate", 8 * b + 5, 8 * b + 7, it, 16)
                        act.wait_ge(h_scores, n + 1)
                        chain(A(s_a, aux[:, 0, 0:384], ACT.Abs))
                        chain(A(s_b, s_a, ACT.Exp, scale=-1.0))
                        A(s_a, s_b, ACT.Ln, bias=one[:, 0:1]).then_inc(sb_soft, 1)
                        splits(l, "gate", 8 * b + 7, 8 * b + 9, it, 16)
                        act.wait_ge(sb_arg, g + 1)
                        A(s_b, s_c, ACT.Exp).then_inc(h_probs, 1)
                        splits(l, "gate", 8 * b + 9, 8 * b + 11, it, 16)
                        act.wait_ge(h_pT_in, n + 1)
                        A(pT, aux[:, 1, 0:384], ACT.Copy).then_inc(h_pT, 1)
                        if b == 1:
                            act.wait_ge(slab_used, used(l, "gate", 15, it, 16))
                            A(gates[:, :, :, ds(it * 256, HD)],
                              main[:, 0:2, 0:HB].rearrange("p t (c n) -> p t c n", c=3), ACT.Copy)\
                                .then_inc(block_out[0], 1)
                        splits(l, "gate", 8 * b + 11, 8 * b + 12, it, 16)
                chain.clear()
                for b in range(2):
                    act.wait_ge(block_out[b], l * PAIRS + (PAIR0["gate"] + 5))
                A(gates[:, :, 2, :], gates[:, :, 2, :], ACT.Silu).then_inc(silu_done, 1)
                A(gates[:, :, 1, :], gates[:, :, 1, :], ACT.Silu).then_inc(silu_done, 1)
                A(gate_ssm[:, :, :], gates[:, :, 0, :], ACT.Silu).then_inc(silu_done, 1)

                def sigmoid(done, pair, dst, ready):
                    act.wait_ge(slab_used, done)
                    A(dst, main[:, 2 * pair:2 * pair + 2, :], ACT.Sigmoid).then_inc(ready, 1)

                def merge_step(br, n, first, j0=0):
                    seg = f"merge{br}"
                    q = l * QUADS + n + 4 * (2 - br)
                    splits(l, seg, 4 + j0, 6 + j0, n, 12)
                    if br:
                        act.wait_ge(q_T_in, q + 1)
                        A(uT, aux[:, 0, 0:SEQ], ACT.Copy)
                        for c in range(2):
                            for i in range(4):
                                A(bbT[:, c, i, :], aux[:, 0, (2 + c) * P:(3 + c) * P], ACT.Copy,
                                  scale=rowsel[:, i:i + 1])
                        for c in range(2):
                            for g in range(2):
                                s = slice(g * STATE, (g + 1) * STATE)
                                src = aux[s, 1, c * P:(c + 1) * P].rearrange("p (j g h) -> p j g h", j=4, g=2)
                                m = A(cbd[s, c, :, g * GROUP:(g + 1) * GROUP], src[:, :, g, :], ACT.Copy,
                                      scale=-1.0 if c else 1.0)
                        m.then_inc(q_T_out, 1)
                    if first:
                        splits(l, seg, 6 + j0, 10 + j0, n, 12)
                        highs(l, f"ys{br}", 4, yT_hi)
                        splits(l, seg, 10 + j0, 12 + j0, n, 12)
                    else:
                        splits(l, seg, 6 + j0, 12 + j0, n, 12)
                    act.wait_ge(sig_used, l * 12 + n + (4 * (2 - br) + 1))
                    sigmoid(used(l, seg, 7 + j0, n, 12), 0, sig, sig_ready)
                    act.wait_ge(sig_ready, l * 12 + n + (4 * (2 - br) + 1))
                    act.sem_inc(block_out[0], 1)
                    splits(l, seg, 12 + j0, 16 + j0, n, 12)

                for br in (2, 1):
                    merge_step(br, 0, True)
                    with act.Fori(1, 4) as n:
                        merge_step(br, n, False)
                act.wait_ge(q_y_out, l * QUADS + QUADS)
                A(ys[:, :, 0, :], ys[:, :, 0, :], ACT.Gelu_apprx_tanh).then_inc(gelu_ready, 1)
                splits(l, "logit0", 4, 10)
                highs(l, "glu", 4, yT_hi)
                splits(l, "logit0", 10, 12)
                act.wait_ge(sig_used, l * 12 + 9)
                sigmoid(used(l, "logit0", 7), 0, sig, sig_ready)
                act.wait_ge(sig_ready, l * 12 + 9)
                act.sem_inc(block_out[0], 1)
                for b in range(2):
                    splits(l, "glu", 4 * b + 4, 4 * b + 8)
                    act.wait_ge(glu_sig, (l * 2 + b) * 2 + 1)
                    sigmoid(used(l, "glu", 4 * b + 3), 1 - b, sig2, glu_sig)
                highs(l, "ys0", 4, yT_hi)
                splits(l, "branch0", 4, 8)
                with act.Fori(1, 4) as n:
                    merge_step(0, n, False, j0=-12)
                highs(l, "merged", 8, hT_hi)
                with act.Fori(0, 2) as it:
                    for b in range(2):
                        splits(l, "out", 8 * b + 4, 8 * b + 12, it, 16)
                        act.wait_ge(x_block, l * 8 + it * 2 + (b + 1))
                        act.wait_ge(sq_done, l * 8 + it * 2 + (b + 5))
                        squares(it * 2 + b)
                highs(l, "p", 2, yT_hi, per=1)
                splits(l, "pproj", 4, 8)
                root(l * 4 + 4, 0)
                highs(l, "ple", 8, hT_hi, gain=16)
                for b in range(4):
                    splits(l, "ple", 8 * b + 4, min(8 * b + 12, 32))
                    act.wait_ge(ple_sig, (l * 4 + b) * 2 + 1)
                    sigmoid(used(l, "ple", 8 * b + 7), b % 2, sig, ple_sig)
                    act.wait_ge(x_block, l * 8 + (b + 5))
                    act.wait_ge(sq_done, l * 8 + (b + 9))
                    squares(b)
            root(DEPTH * 4 + 1, 0)

        @block.vector
        def _(dve):
            v = nc.vector
            chain = Chain(dve, dve_chain)
            dve.sem_inc(sq_done, 1)
            dve.sem_inc(sig_used, 1)
            dve.sem_inc(glu_sig, 1)
            dve.sem_inc(ple_sig, 1)
            dve.sem_inc(layer_done, 1)
            dve.sem_inc(q_T_out, 1)
            chain(v.memset(one[:, :], 1.0))
            chain(v.memset(bb, 0.0))
            chain(v.memset(cbd, 0.0))
            dve.wait_ge(consts_in, 48)
            for i in range(4):
                chain(v.reduce_sum(rowsel[:, i:i + 1], ident[:, 32 * i:32 * i + 32], AX.X))
            dve.wait_ge(gains_t, 1)
            v.tensor_copy(g_all[:, :], aux[:, 0, 0:DEPTH * NG]).then_inc(gains_ready, 1)
            dve.wait_ge(gains_ready, 1)
            chain.clear()

            def lows(l, seg, steps, hi, lo, per=2, gain=None, k0=0, at=0):
                for i in range(at, at + steps):
                    n = STEP0[seg] + i
                    dve.wait_ge(tr_hi, l * NSTEP + (n + 1))
                    for k in range(per):
                        kk = k0 + per * i + k
                        s = 1.0 if gain is None else gc[:, gain + per * i + k:gain + per * i + k + 1]
                        m = v.scalar_tensor_tensor(out=lo[:, kk, :], in0=trb[:, n % 2, 2 * k * P:(2 * k + 2) * P],
                                                   scalar=s, in1=hi[:, kk, :].bitcast(f32), op0=ALU.mult,
                                                   op1=ALU.subtract)
                    m.then_inc(tr_lo, 1)

            def mean_square(value, at, n):
                v.tensor_scalar(st_ss[:, at:at + 2], st_ss[:, at:at + 2], 1.0 / n, EPS, ALU.mult, ALU.add)\
                    .then_inc(ms_ready, 1)
                dve.wait_ge(root_ready, value)
                chain(v.reciprocal(st_r[:, at:at + 2], st_r[:, at:at + 2]))

            def norm(value, blocks):
                dve.wait_ge(sq_done, blocks + 1)
                chain(v.reduce_sum(st_ss[:, 0:2], st_p[:, :, :], AX.X))
                mean_square(value, 0, D)
                for t in range(TOK):
                    m = v.tensor_scalar(xn[:, t, :], xs[:, t, :], st_r[:, t:t + 1], None, ALU.mult)
                return m

            def s5_parameters(l):
                lre, lim, ldt = (lam[:, i, :] for i in range(3))
                dt, ar, ang, quarter, k, r, ni, den = (sm[:, i, :] for i in range(8))
                tt = v.tensor_tensor
                dve.wait_ge(s5_cols_in, l + 1)
                chain(v.tensor_copy(lam[:, :, :].rearrange("p c j -> p (c j)"), aux[:, 0, 0:3 * NTILE]))
                dve.sem_inc(s5_lam_ready, 1)
                dve.wait_ge(s5_exp_ready, l * 2 + 1)
                chain(tt(ar, lre, dt, ALU.mult))
                chain(tt(ang, lim, dt, ALU.mult))
                dve.sem_inc(s5_lam_ready, 1)
                chain(v.tensor_scalar(k, ang, float(1 / TWO_PI), MAGIC, ALU.mult, ALU.add))
                chain(v.tensor_scalar(k, k, MAGIC, None, ALU.subtract))
                for part in (TP1, TP2, TP3):
                    chain(v.scalar_tensor_tensor(out=ang, in0=k, scalar=-part, in1=ang, op0=ALU.mult, op1=ALU.add))
                chain(v.tensor_scalar(ang, ang, PI_LOW, -PI_LOW, ALU.min, ALU.max))
                chain(v.scalar_tensor_tensor(out=quarter, in0=ang, scalar=-1.0, in1=ang, op0=ALU.mult, op1=ALU.min))
                chain(v.tensor_scalar(quarter, quarter, float(np.pi / 2), None, ALU.add))
                dve.sem_inc(s5_ang_ready, 1)
                dve.wait_ge(s5_exp_ready, l * 2 + 2)
                dve.wait_ge(s5_trig_ready, l + 1)
                chain(tt(r, prm[:, 0, :], pw[:, 0, 0, :], ALU.mult))
                chain(v.tensor_scalar(r, r, 1.0, None, ALU.subtract))
                chain(tt(ni, prm[:, 0, :], pw[:, 0, 1, :], ALU.mult))
                chain(tt(den, lre, lre, ALU.mult))
                chain(tt(k, lim, lim, ALU.mult))
                chain(tt(den, den, k, ALU.add))
                chain(v.reciprocal(den, den))
                chain(tt(k, r, lre, ALU.mult))
                chain(tt(ang, ni, lim, ALU.mult))
                chain(tt(k, k, ang, ALU.add))
                chain(tt(prm[:, 1, :], k, den, ALU.mult))
                chain(tt(k, ni, lre, ALU.mult))
                chain(tt(ang, r, lim, ALU.mult))
                chain(tt(k, k, ang, ALU.subtract))
                chain(tt(prm[:, 2, :], k, den, ALU.mult))
                for i in range(1, LEVELS):
                    c, s = pw[:, i - 1, 0, :], pw[:, i - 1, 1, :]
                    chain(tt(k, c, c, ALU.mult))
                    chain(tt(r, s, s, ALU.mult))
                    chain(tt(pw[:, i, 0, :], k, r, ALU.subtract))
                    chain(v.scalar_tensor_tensor(out=pw[:, i, 1, :], in0=c, scalar=2.0, in1=s, op0=ALU.mult,
                                                 op1=ALU.mult))

            def rotary(x1, x2, t, heads):
                half = ROPE // 2
                shape = [P, heads, half]
                c = rope_t[:, t, 0:1, :].broadcast_to(shape)
                s = rope_t[:, t, 1:2, :].broadcast_to(shape)
                a, b_, d = (z[:, 0:heads * half].rearrange("p (h c) -> p h c", h=heads)
                            for z in (rope_a, rope_b, rope_c))
                chain(v.tensor_tensor(a, x1, s, ALU.mult))
                chain(v.tensor_tensor(b_, x2, s, ALU.mult))
                chain(v.tensor_tensor(d, x1, c, ALU.mult))
                chain(v.tensor_tensor(x1, d, b_, ALU.subtract))
                chain(v.tensor_tensor(b_, x2, c, ALU.mult))
                chain(v.tensor_tensor(x2, a, b_, ALU.add))

            def quad(l, n, br, between):
                q = n + 4 * (2 - br)
                g = l * QUADS + q
                tt = v.tensor_tensor
                put, sync = chain.put, chain.sync
                put(v.tensor_copy(u_q, ys[:, :, 0, ds(q * P, P)]))
                put(v.tensor_copy(prm_q[:, :, :], prm[:, :, ds(q * 4, 4)]))
                put(v.tensor_copy(pw_q[:, :, :, :].rearrange("p a b j -> p (a b) j"),
                                  pw[:, :, :, :].rearrange("p a b j -> p (a b) j")[:, :, ds(q * 4, 4)]))
                put(v.memset(tab4[:, 0, :, 0:1], 1.0))
                put(v.memset(tab4[:, 1, :, 0:1], 0.0))
                sync()
                dve.wait_ge(q_ld, (g + 1) * (16 * 7))
                wide = [P, 4, GROUP]
                cr = prm_q[:, 1, :].rearrange("p (j o) -> p j o", o=1).broadcast_to(wide)
                ci = prm_q[:, 2, :].rearrange("p (j o) -> p j o", o=1).broadcast_to(wide)
                for c in range(2):
                    put(tt(b_t1[:, c, :, :], b_ld[:, c, :, :], cr, ALU.mult))
                    put(tt(b_t2[:, c, :, :], b_ld[:, c, :, :], ci, ALU.mult))
                put(tt(y_q, u_q, d_q.rearrange("p (o c) -> p o c", o=1).broadcast_to([P, TOK, P]), ALU.mult))
                sync()
                for h in range(2):
                    s = slice(h * STATE, (h + 1) * STATE)
                    o = slice(h * GROUP, (h + 1) * GROUP)
                    put(tt(bb[s, 0, :, o], b_t1[s, 0, :, :], b_t2[s, 1, :, :], ALU.subtract))
                    put(tt(bb[s, 1, :, o], b_t1[s, 1, :, :], b_t2[s, 0, :, :], ALU.add))
                sync()
                dve.sem_inc(q_bb, 1)
                pa = pr1.rearrange("p c (j t) -> p c j t", j=4)
                pb = pr2.rearrange("p c (j t) -> p c j t", j=4)
                for k in range(LEVELS):
                    m = 1 << k
                    for c in range(2):
                        wr, wi = (pw_q[:, k, z, :].rearrange("p (j o) -> p j o", o=1).broadcast_to([P, 4, m])
                                  for z in range(2))
                        put(tt(pa[:, c, :, 0:m], tab4[:, c, :, 0:m], wr, ALU.mult))
                        put(tt(pb[:, c, :, 0:m], tab4[:, c, :, 0:m], wi, ALU.mult))
                    sync()
                    put(tt(tab4[:, 0, :, m:2 * m], pa[:, 0, :, 0:m], pb[:, 1, :, 0:m], ALU.subtract))
                    put(tt(tab4[:, 1, :, m:2 * m], pa[:, 1, :, 0:m], pb[:, 0, :, 0:m], ALU.add))
                    sync()
                if between:
                    between()
                for half in range(2):
                    s = slice(half * 512, half * 512 + 512)
                    cos, sin = (tab[:, z:z + 1, s].broadcast_to([P, 2, 512]) for z in range(2))
                    dve.wait_ge(q_bu, g * 2 + (half + 1))
                    put(tt(pr1[:, :, s], aux[:, :, :], cos, ALU.mult))
                    put(tt(pr2[:, :, s], aux[:, :, :], sin, ALU.mult))
                    sync()
                    dve.sem_inc(q_bu_used, 1)
                    put(tt(st[:, 0, s], pr1[:, 0, s], pr2[:, 1, s], ALU.add))
                    put(tt(st[:, 1, s], pr1[:, 1, s], pr2[:, 0, s], ALU.subtract))
                    sync()
                    for c in range(2):
                        for i in range(2 * half, 2 * half + 2):
                            s = slice(i * SEQ, (i + 1) * SEQ)
                            put(v.tensor_tensor_scan(st[:, c, s], prm_q[:, 0, i:i + 1].broadcast_to([P, SEQ]),
                                                     st[:, c, s], 0.0, ALU.mult, ALU.add))
                sync()
                cos, sin = (tab[:, z:z + 1, :].broadcast_to([P, 2, 1024]) for z in range(2))
                put(tt(pr1, st, cos, ALU.mult))
                put(tt(pr2, st, sin, ALU.mult))
                sync()
                put(tt(pr1[:, 0, :], pr1[:, 0, :], pr2[:, 1, :], ALU.subtract))
                put(tt(pr1[:, 1, :], pr1[:, 1, :], pr2[:, 0, :], ALU.add))
                sync()
                dve.sem_inc(q_h, 1)

            def quad_out(l, n, br):
                q = n + 4 * (2 - br)
                dve.wait_ge(q_y, l * QUADS + q + 1)
                chain(v.tensor_tensor(ys[:, :, 0, ds(q * P, P)], y_q,
                                      aux[:, 0, 0:SEQ].rearrange("p (t c) -> p t c", t=TOK), ALU.add))
                dve.sem_inc(q_y_out, 1)

            def merged_block(l, br, n, done):
                dve.wait_ge(sig_ready, l * 12 + n + (4 * (2 - br) + 1))
                dve.wait_ge(slab_used, done)
                dst = merged[:, :, ds(n * NB, NB)]
                if br == 2:
                    chain(v.tensor_tensor(dst, sig, main[:, 2:4, :], ALU.mult))
                    dve.sem_inc(block_out[1], 1)
                else:
                    chain(v.tensor_tensor(sig, sig, main[:, 2:4, :], ALU.mult))
                    dve.sem_inc(block_out[1], 1)
                    chain(v.tensor_tensor(dst, dst, sig, ALU.add))
                dve.sem_inc(sig_used, 1)
                if br == 0:
                    dve.sem_inc(merged_ready, 1)

            def merge_step(l, br, n, first, j0=0):
                seg = f"merge{br}"
                if br:
                    quad(l, n, br, (lambda: lows(l, f"ys{br}", 4, yT_hi, yT_lo)) if first else None)
                merged_block(l, br, n, used(l, seg, 11 + j0, n, 12))
                if br:
                    quad_out(l, n, br)
                chain.clear()

            dve.wait_ge(x_in, 16)
            with dve.Fori(0, DEPTH) as l:
                chain(v.tensor_copy(gc[:, :], g_all[:, ds(l * NG, NG)]))
                norm(l * 4 + 1, l * 8 + 4).then_inc(xn_ready, 1)
                dve.wait_ge(s5_rows_in, l * 48 + 48)
                chain(v.tensor_copy(dt_wide[:, :, :], dt_rows[:, :].rearrange("j (g o) -> j g o", o=1)
                                    .broadcast_to([NTILE, 2, STATE])))
                dve.sem_inc(dt_wide_ready, 1)
                lows(l, "ln", 8, hT_hi, hT_lo, gain=0)
                s5_parameters(l)
                chain.clear()
                for b in range(2):
                    dve.wait_ge(slab_used, used(l, "proj", 8 * b + 7))
                    v.tensor_copy(ys[:, :, 0, b * NB:(b + 1) * NB], main[:, 2 * b:2 * b + 2, :])\
                        .then_inc(block_out[b], 1)
                for b in range(2):
                    dve.wait_ge(lat_sq, l * 2 + (b + 1))
                    mean_square(l * 4 + 2 + b, 2 * (1 - b), LAT)
                    for t in range(TOK):
                        chain(v.tensor_scalar(lat[:, t, b * LAT:(b + 1) * LAT], main[:, 2 * b + t, :],
                                              st_r[:, 2 * (1 - b) + t:2 * (1 - b) + t + 1], None, ALU.mult))
                    dve.sem_inc(block_out[b], 1)
                    dve.sem_inc(lat_norm, 1)
                lows(l, "qlat", 2, yT_hi, yT_lo, gain=32)
                lows(l, "kvlat", 2, yT_hi, yT_lo, gain=36, k0=4)
                dve.wait_ge(x_kept, l * 16 + 16)
                dve.wait_ge(slab_used, used(l, "lat", 1))
                for t in range(TOK):
                    chain(v.tensor_copy(kr[:, t, :], main[:, t, 0:ROPE]))
                dve.sem_inc(block_out[0], 1)
                for t in range(TOK):
                    k3 = kr[:, t, :].rearrange("p (h c) -> p h c", h=1)
                    rotary(k3[:, :, 0:ROPE // 2], k3[:, :, ROPE // 2:ROPE], t, 1)
                dve.sem_inc(kr_ready, 1)
                for b in range(1, 8):
                    dst, c = (mla_q, b - 1) if b < 4 else (mla_kv, b - 4)
                    dve.wait_ge(slab_used, used(l, "lat", 2 * b + 1))
                    chain(v.tensor_copy(dst[:, :, c * NB:(c + 1) * NB], main[:, 2 * (b % 2):2 * (b % 2) + 2, :]))
                    dve.sem_inc(block_out[b % 2], 1)
                    if b == 3:
                        for t in range(TOK):
                            q4 = mla_q[:, t, :].rearrange("p (h c) -> p h c", h=HEADS)
                            rotary(q4[:, :, HD:HD + ROPE // 2], q4[:, :, HD + ROPE // 2:HD + ROPE], t, HEADS)
                dve.sem_inc(mla_in, 1)
                dve.wait_ge(kr_out, l + 1)
                dve.sem_inc(dve_mark, 1)
                with dve.Fori(0, HEADS // 2) as it:
                    for b in range(2):
                        chain.clear()
                        n = l * 2 * HEADS + it * 2 + b
                        chain(v.tensor_copy(q_s, mla_q[:, :, ds(it * 384 + b * 192, 192)]))
                        chain(v.tensor_copy(k_s, mla_kv[:, :, ds(it * 512 + b * 256, HD)]))
                        dve.sem_inc(h_static, 1)
                        dve.wait_ge(h_scores, n + 1)
                        chain(v.tensor_tensor(s_a, aux[:, 0, 0:384], masks[:, 0, :], ALU.add))
                        chain(v.reduce_max(mx[:, 0:1], s_a[:, 0:P], AX.X))
                        chain(v.reduce_max(mx[:, 1:2], s_a[:, P:384], AX.X))
                        chain(v.tensor_scalar(nmx[:, :], mx[:, :], -1.0, None, ALU.mult))
                        dve.sem_inc(h_max, 1)
                        dve.wait_ge(h_probs, n + 1)
                        chain(v.reciprocal(rsum[:, :], sums[:, :]))
                        if b == 1:
                            dve.wait_ge(slab_used, used(l, "sb", 15, it, 16))
                            v.tensor_copy(sb_qk[:, :, ds(it * 2 + 1, 1), :].rearrange("p t o c -> p t (o c)"),
                                          main[:, 2:4, 0:256])
                            v.tensor_copy(ys[:, :, 2, ds(it * 256 + HD, HD)], main[:, 2:4, 256:384])\
                                .then_inc(block_out[1], 1)
                        dve.wait_ge(h_o_in, n + 1)
                        for t in range(TOK):
                            chain(v.tensor_scalar(ys[:, t, 1, ds(it * 256 + b * HD, HD)],
                                                  trb[:, 1, 256 + t * P:384 + t * P], rsum[:, t:t + 1], None,
                                                  ALU.mult))
                        dve.sem_inc(h_o_out, 1)
                with dve.Fori(0, HEADS // 2) as it:
                    for b in range(2):
                        chain.clear()
                        n = l * 2 * HEADS + it * 2 + (HEADS + b)
                        chain(v.tensor_copy(qk_s, sb_qk[:, :, ds(it * 2 + b, 1), :].rearrange("p t o c -> p t (o c)")))
                        dve.sem_inc(h_static, 1)
                        dve.wait_ge(sb_soft, l * HEADS + it * 2 + (b + 1))
                        chain(v.scalar_tensor_tensor(out=s_a, in0=aux[:, 0, 0:384], scalar=0.0, in1=s_a, op0=ALU.max,
                                                     op1=ALU.add))
                        chain(v.tensor_tensor(s_a, s_a, masks[:, 2, :], ALU.mult))
                        for a, e in ((0, P), (P, 384)):
                            back = slice(e - 1, a - 1 if a else None, -1)
                            chain(v.tensor_tensor_scan(s_b[:, back], one[:, 0:1].broadcast_to([P, e - a]),
                                                       s_a[:, back], 0.0, ALU.mult, ALU.add))
                        chain(v.tensor_tensor(s_c, aux[:, 0, 0:384], s_b, ALU.subtract))
                        chain(v.tensor_tensor(s_c, s_c, masks[:, 1, :], ALU.add))
                        dve.sem_inc(sb_arg, 1)
                        if b == 1:
                            dve.wait_ge(slab_used, used(l, "gate", 15, it, 16))
                            v.tensor_copy(gates[:, :, :, ds(it * 256 + HD, HD)],
                                          main[:, 2:4, 0:HB].rearrange("p t (c n) -> p t c n", c=3))\
                                .then_inc(block_out[1], 1)
                        dve.wait_ge(h_o_in, n + 1)
                        chain(v.tensor_copy(ys[:, :, 2, ds(it * 256 + b * HD, HD)],
                                            trb[:, 1, 256:512].rearrange("p (t c) -> p t c", t=TOK)))
                        dve.sem_inc(h_o_out, 1)
                chain.clear()
                for i, br in enumerate((2, 1)):
                    dve.wait_ge(silu_done, l * 3 + (i + 1))
                    v.tensor_tensor(ys[:, :, br, :], ys[:, :, br, :], gates[:, :, br, :], ALU.mult)\
                        .then_inc(ys_ready, 1)
                dve.wait_ge(silu_done, l * 3 + 3)
                dve.wait_ge(ys_ready, l * 4 + 2)
                for br in (2, 1):
                    merge_step(l, br, 0, True)
                    with dve.Fori(1, 4) as n:
                        merge_step(l, br, n, False)
                lows(l, "glu", 4, yT_hi, yT_lo)
                for b in range(2):
                    dve.wait_ge(glu_sig, (l * 2 + b) * 2 + 2)
                    dve.sem_inc(block_out[1 - b], 1)
                    s = slice(b * NB, (b + 1) * NB)
                    chain(v.tensor_tensor(sig2, sig2, gate_ssm[:, :, s], ALU.mult))
                    chain(v.tensor_tensor(ys[:, :, 0, s], ys[:, :, 0, s], sig2, ALU.mult))
                    dve.sem_inc(glu_sig, 1)
                    dve.sem_inc(ys_ready, 1)
                lows(l, "ys0", 4, yT_hi, yT_lo)
                merged_block(l, 0, 0, used(l, "branch0", 3))
                chain.clear()
                with dve.Fori(1, 4) as n:
                    merge_step(l, 0, n, False, j0=-12)
                lows(l, "merged", 8, hT_hi, hT_lo)
                dve.wait_ge(x_back, l * 16 + 16)
                for b in range(4):
                    dve.wait_ge(slab_used, used(l, "out", 8 * b + 7))
                    s = slice(b * NB, (b + 1) * NB)
                    pair = slice(2 * (b % 2), 2 * (b % 2) + 2)
                    chain(v.tensor_tensor(xs[:, :, s], xs[:, :, s], main[:, pair, :], ALU.add))
                    dve.sem_inc(block_out[b % 2], 1)
                    dve.sem_inc(x_block, 1)
                lows(l, "p", 2, yT_hi, yT_lo, per=1)
                for b in range(4):
                    dve.wait_ge(slab_used, used(l, "pproj", b))
                    v.tensor_copy(reg1[:, :, b * NB:(b + 1) * NB], main[:, 2 * (b % 2):2 * (b % 2) + 2, :])\
                        .then_inc(block_out[b % 2], 1)
                norm(l * 4 + 4, l * 8 + 8).then_inc(xn_ready, 1)
                lows(l, "ple", 8, hT_hi, hT_lo, gain=16)
                for b in range(4):
                    s = slice(b * NB, (b + 1) * NB)
                    dve.wait_ge(ple_sig, (l * 4 + b) * 2 + 2)
                    dve.sem_inc(block_out[b % 2], 1)
                    chain(v.tensor_tensor(reg1[:, :, s], reg1[:, :, s], sig, ALU.mult))
                    dve.sem_inc(ple_sig, 1)
                    chain(v.tensor_tensor(xs[:, :, s], xs[:, :, s], reg1[:, :, s], ALU.add))
                    dve.sem_inc(x_block, 1)
                dve.sem_inc(layer_done, 1)
                chain.clear()
            dve.wait_ge(sq_done, DEPTH * 8 + 5)
            chain(v.reduce_sum(st_ss[:, 0:2], st_p[:, :, :], AX.X))
            mean_square(DEPTH * 4 + 1, 0, D)
            dve.wait_ge(fin_g_in, 16)
            for t in range(TOK):
                v.scalar_tensor_tensor(out=xn[:, t, :], in0=xs[:, t, :], scalar=st_r[:, t:t + 1], in1=fin_g,
                                       op0=ALU.mult, op1=ALU.mult).then_inc(out_ready, 1)


def constants():
    ident = np.eye(P, dtype=np.float32)
    q = np.arange(P)[:, None]
    k = np.arange(P)[None, :]
    masks = np.zeros((P, 3, 384), np.float32)
    for i, ok in enumerate((k <= q, k < q)):
        for c in (0, 256):
            masks[:, i, c:c + P] = np.where(ok, 0.0, NEG)
    masks[:, 2, :] = masks[:, 1, :] == 0.0
    pos = np.arange(SEQ, dtype=np.float32)
    inv = (np.float32(10000.0) ** (-np.arange(0, ROPE, 2, dtype=np.float32) / np.float32(ROPE))).astype(np.float32)
    ang = pos[:, None] * inv[None, :]
    rope = np.stack([np.cos(ang), np.sin(ang)], axis=1).astype(np.float32)
    rope = np.ascontiguousarray(rope.reshape(TOK, P, 2, ROPE // 2).transpose(1, 0, 2, 3))
    return {"ident": ident, "masks": masks, "rope": rope}


INS = ["x", "p", "ln_g", "w_in", "ssm_lam_re", "ssm_lam_im", "ssm_log_dt", "ssm_b_re", "ssm_b_im", "ssm_c_re",
       "ssm_c_im", "ssm_d", "ssm_w_glu", "mla_g_q", "mla_g_kv", "mla_w_uq", "mla_w_ukv", "w_branch", "w_out", "ple_g",
       "w_ple_gate", "w_ple_proj", "final_g"]


def kernel(**inputs):
    import concourse.bacc as bacc
    from concourse.bass_utils import run_bass_kernel_spmd

    nc = bacc.Bacc("TRN2", target_bir_lowering=False, num_devices=1)
    arrays, args = {}, []
    given = {**{n: inputs[n] for n in INS}, **constants()}
    for name, value in given.items():
        a = np.ascontiguousarray(value)
        arrays[f"in_{name}"] = a
        args.append(nc.dram_tensor(f"in_{name}", a.shape, mybir.dt.from_np(a.dtype), kind="ExternalInput").ap())
    args.append(nc.dram_tensor("out", (1, SEQ, D), mybir.dt.float32, kind="ExternalOutput").ap())
    build(nc, *args)
    r = run_bass_kernel_spmd(nc, [arrays], core_ids=[0])
    return r.results[0]["out"]
```

```python
import numpy as np
import concourse.bass as bass
from concourse import mybir
from contextlib import ExitStack


SEQ, D, DEPTH, W = 256, 2048, 2, 1024
P, TOK = 128, SEQ // 128
KT = D // P
PLE, LAT, ROPE, HEADS, HD = 256, 512, 64, 8, 128
GROUP, STATE = 16, 64
NTILE = W // GROUP * STATE // P
QUADS = NTILE // 4
LEVELS = 8
EPS = 1e-6
COL_KR = W + 2 * LAT
COL_SB = COL_KR + ROPE
COL_GATE = COL_SB + 3 * W
COL_MERGE = COL_GATE + 3 * W
NB = 512
HB = 3 * HD
RING = 4
SLOT = 2 * NB

STAGES = [("proj", 4, 8), ("lat", 8, 2), ("sb", 8, 8), ("gate", 8, 8), ("merge2", 8, 6), ("merge1", 8, 6),
          ("ssm", 4, 5), ("merge0", 6, 6), ("out", 4, 8), ("pproj", 4, 1), ("ple", 4, 8)]
SLAB0, PAIR0 = {}, {}
SLABS = PAIRS = 0
_blocks_before = 0
for _name, _blocks, _per in STAGES:
    SLAB0[_name], PAIR0[_name] = SLABS, _blocks_before // 2
    SLABS += _blocks * _per
    _blocks_before += _blocks
PAIRS = _blocks_before // 2
STEPS = [("ln", 8), ("qlat", 2), ("kvlat", 2), ("ys2", 4), ("ys1", 4), ("glu", 4), ("ys0", 4), ("merged", 8),
         ("p", 2), ("ple", 8)]
STEP0 = {}
NSTEP = 0
for _name, _n in STEPS:
    STEP0[_name] = NSTEP
    NSTEP += _n
NG = 40

MLA_SCALE = float((HD + ROPE) ** -0.5)
SB_SCALE = float(HD ** -0.5)
NEG = -1e30
MAGIC = 1.5 * 2.0 ** 23
TWO_PI = 2 * np.pi
TP1 = 6.28125
TP2 = 0.0019350051879882812
TP3 = float(np.float32(TWO_PI - TP1 - TP2))
PI_LOW = 3.1415925


def build(nc, x, p, ln_g, w_in, lam_re, lam_im, log_dt, b_re, b_im, c_re, c_im, d_skip, w_glu, g_q, g_kv, w_uq,
          w_ukv, w_branch, w_out, ple_g, w_ple_gate, w_ple_proj, final_g, ident_in, masks_in, rope_in, out):
    f32, f32r = mybir.dt.float32, mybir.dt.float32r
    ALU, ACT, AX = mybir.AluOpType, mybir.ActivationFunctionType, mybir.AxisListType
    ds = bass.ds
    ctx = ExitStack()
    with ctx:
        def sb(name, shape, dt=f32):
            return ctx.enter_context(nc.sbuf_tensor(name, shape, dt))

        def sem(name):
            return ctx.enter_context(nc.semaphore(name))

        x_keep = nc.dram_tensor("x_keep", [SEQ, D], f32, kind="Internal").ap()

        raw = sb("raw", [P, RING, SLOT])
        w_hi = sb("w_hi", [P, RING, SLOT], f32r)
        w_lo = sb("w_lo", [P, RING, SLOT], f32r)
        hT_hi = sb("hT_hi", [P, KT, SEQ], f32r)
        hT_lo = sb("hT_lo", [P, KT, SEQ], f32r)
        yT_hi = sb("yT_hi", [P, 8, SEQ], f32r)
        yT_lo = sb("yT_lo", [P, 8, SEQ], f32r)
        ys = sb("ys", [P, TOK, 3, W])
        ys_flat = ys[:, :, :, :].rearrange("p t b w -> p (t b w)")
        xn = ys_flat[:, 0:TOK * D].rearrange("p (t d) -> p t d", t=TOK)
        junk = ys_flat[:, TOK * D:TOK * D + D]
        gate_ssm = sb("gate_ssm", [P, TOK, W])
        p_in = gate_ssm[:, :, 0:PLE]
        fin_g = gate_ssm[:, :, :].rearrange("p t w -> p (t w)")
        reg1 = sb("reg1", [P, TOK, D])
        reg2 = sb("reg2", [P, 8192])
        lat = reg1[:, :, 0:2 * LAT]
        e_ple = reg1
        sb_qk = reg1[:, :, :].rearrange("p t (h c) -> p t h c", h=HEADS)
        merged = reg1
        xs = reg2[:, 0:TOK * D].rearrange("p (t d) -> p t d", t=TOK)
        mla_q = reg2[:, 0:3072].rearrange("p (t c) -> p t c", t=TOK)
        mla_kv = reg2[:, 3072:7168].rearrange("p (t c) -> p t c", t=TOK)
        kr = reg2[:, 7168:7296].rearrange("p (t c) -> p t c", t=TOK)
        rope_a = reg2[:, 7296:7552]
        rope_b = reg2[:, 7552:7808]
        rope_c = reg2[:, 7808:8064]
        gates = reg2[:, 0:6144].rearrange("p (b t w) -> p t b w", t=TOK, b=3)
        tab = reg2[:, 4096:6144].rearrange("p (c n) -> p c n", c=2)
        tab4 = reg2[:, 4096:6144].rearrange("p (c j t) -> p c j t", c=2, j=4)
        st = reg2[:, 2048:4096].rearrange("p (c n) -> p c n", c=2)
        pr1 = reg2[:, 0:2048].rearrange("p (c n) -> p c n", c=2)
        pr2 = reg2[:, 6144:8192].rearrange("p (c n) -> p c n", c=2)

        scr = sb("scr", [P, 4480])
        q_s = scr[:, 0:384].rearrange("p (t c) -> p t c", t=TOK)
        k_s = scr[:, 384:640].rearrange("p (t c) -> p t c", t=TOK)
        qk_s = scr[:, 0:512].rearrange("p (t c) -> p t c", t=TOK)
        qkT = scr[:, 640:1152]
        qrT = scr[0:ROPE, 1152:1408]
        krT = scr[0:ROPE, 1408:1664]
        s_a = scr[:, 1664:2048]
        s_b = scr[:, 2048:2432]
        s_c = scr[:, 2432:2816]
        pT = scr[:, 2816:3200]
        sig = scr[:, 0:1024].rearrange("p (t c) -> p t c", t=TOK)
        sig2 = scr[:, 1280:2304].rearrange("p (t c) -> p t c", t=TOK)
        u_q = scr[:, 1024:1280].rearrange("p (t c) -> p t c", t=TOK)
        uT = scr[:, 1280:1536]
        bbT = scr[:, 1536:2560].rearrange("p (c j s) -> p c j s", c=2, j=4)
        b_ld = scr[:, 2560:2688].rearrange("p (c j h) -> p c j h", c=2, j=4)
        c_ld = scr[:, 2688:2944].rearrange("p (c s) -> p c s", c=2)
        b_t1 = scr[:, 2944:3072].rearrange("p (c j h) -> p c j h", c=2, j=4)
        b_t2 = scr[:, 3072:3200].rearrange("p (c j h) -> p c j h", c=2, j=4)
        d_q = scr[:, 3200:3328]
        bb = scr[:, 3968:4224].rearrange("p (c j h) -> p c j h", c=2, j=4)
        cbd = scr[:, 4224:4480].rearrange("p (c j h) -> p c j h", c=2, j=4)
        ident = sb("ident", [P, P])
        masks = sb("masks", [P, 3, 384])
        rope_t = sb("rope_t", [P, TOK, 2, ROPE // 2])
        rowsel = sb("rowsel", [P, 4])
        g_rows = sb("g_rows", [DEPTH * NG, P])
        g_all = sb("g_all", [P, DEPTH * NG])
        gc = sb("gc", [P, NG])
        lam_rows = sb("lam_rows", [NTILE, 2, P])
        dt_rows = sb("dt_rows", [NTILE, 2])
        dt_wide = sb("dt_wide", [NTILE, 2, STATE])
        lam = sb("lam", [P, 3, NTILE])
        prm = sb("prm", [P, 3, NTILE])
        prm_q = sb("prm_q", [P, 3, 4])
        pw = sb("pw", [P, LEVELS, 2, NTILE])
        pw_q = sb("pw_q", [P, LEVELS, 2, 4])
        sm = sb("sm", [P, 8, NTILE])
        st_ss = sb("st_ss", [P, 4])
        st_p = sb("st_p", [P, TOK, D // NB])
        st_r = sb("st_r", [P, 4])
        mx = sb("mx", [P, 2])
        nmx = sb("nmx", [P, 2])
        sums = sb("sums", [P, 2])
        rsum = sb("rsum", [P, 2])
        one = sb("one", [P, 1])
        warm = sb("warm", [P, 1])
        one_ready = sem("one_ready")

        main = ctx.enter_context(nc.psum_tensor("main", [P, 4, NB], f32))
        trb = ctx.enter_context(nc.psum_tensor("trb", [P, 2, NB], f32))
        aux = ctx.enter_context(nc.psum_tensor("aux", [P, 2, NB], f32))

        raw_loaded = [sem(f"raw_loaded{i}") for i in range(RING)]
        hi_ready, lo_ready, slab_used = sem("hi_ready"), sem("lo_ready"), sem("slab_used")
        block_out = [sem("pair_a_out"), sem("pair_b_out")]
        tr_in, tr_hi, tr_lo = sem("tr_in"), sem("tr_hi"), sem("tr_lo")
        consts_in, gains_in, x_kept, x_back, s5_rows_in = (sem(n) for n in (
            "consts_in", "gains_in", "x_kept", "x_back", "s5_rows_in"))
        x_in = [sem(f"x_in{b}") for b in range(D // NB)]
        ident_loaded = sem("ident_loaded")
        heads_left, x_half, ple_used = sem("heads_left"), sem("x_half"), sem("ple_used")
        pair_a_full = sem("pair_a_full")
        p_loaded, fin_g_in, out_done = sem("p_loaded"), sem("fin_g_in"), sem("out_done")
        act_chain, dve_chain = sem("act_chain"), sem("dve_chain")
        gains_t, gains_ready = sem("gains_t"), sem("gains_ready")
        sq_done, ms_ready, root_ready, xn_ready = sem("sq_done"), sem("ms_ready"), sem("root_ready"), sem("xn_ready")
        dt_wide_ready, s5_cols_in, s5_lam_ready, s5_exp_ready = (sem(n) for n in (
            "dt_wide_ready", "s5_cols_in", "s5_lam_ready", "s5_exp_ready"))
        s5_ang_ready, s5_trig_ready = sem("s5_ang_ready"), sem("s5_trig_ready")
        lat_norm, kr_raw, kr_back, kr_ready, kr_t, kr_out = (sem(n) for n in (
            "lat_norm", "kr_raw", "kr_back", "kr_ready", "kr_t", "kr_out"))
        h_static, h_qkT_in, h_qkT, h_scores, h_max, h_probs, h_pT_in, h_pT, h_o_in, h_o_out = (sem(n) for n in (
            "h_static", "h_qkT_in", "h_qkT", "h_scores", "h_max", "h_probs", "h_pT_in", "h_pT", "h_o_in", "h_o_out"))
        sb_soft, sb_arg = sem("sb_soft"), sem("sb_arg")
        silu_done, lat_sq, x_block = sem("silu_done"), sem("lat_sq"), sem("x_block")
        ys_ready = sem("ys_ready")
        q_ld, q_bb, q_T_in, q_T_out, q_bu, q_bu_used, q_h, q_y, q_y_out = (sem(n) for n in (
            "q_ld", "q_bb", "q_T_in", "q_T_out", "q_bu", "q_bu_used", "q_h", "q_y", "q_y_out"))
        sig_ready, sig_used = sem("sig_ready"), sem("sig_used")
        gelu_ready, glu_sig, merged_ready = sem("gelu_ready"), sem("glu_sig"), sem("merged_ready")
        ple_sig = sem("ple_sig")
        layer_done, out_ready = sem("layer_done"), sem("out_ready")

        pe_mark, dve_mark, sp_mark = sem("pe_mark"), sem("dve_mark"), sem("sp_mark")

        class Chain:
            def __init__(self, eng, s):
                self.eng, self.s, self.n = eng, s, 0

            def put(self, ins):
                ins.then_inc(self.s, 1)
                self.n += 1

            def sync(self):
                self.eng.wait_ge(self.s, self.n)

            def __call__(self, ins):
                self.put(ins)
                self.sync()

            def clear(self):
                self.eng.sem_clear(self.s)
                self.n = 0

        block = ctx.enter_context(nc.Block())

        @block.sync
        def _(sp):
            for b in range(D // NB):
                c = slice(b * NB, (b + 1) * NB)
                sp.dma_start(xs[:, :, c], x[0, :, c].rearrange("(t p) d -> p t d", p=P)).then_inc(x_in[b], 16)
            sp.dma_start(ident[:, :], ident_in).then_inc(ident_loaded, 16)
            for src, at, n in ((ln_g, 0, 16), (ple_g, 16, 16), (g_q, 32, 4), (g_kv, 36, 4)):
                sp.dma_start(g_rows[DEPTH * at:DEPTH * (at + n), :], src.rearrange("l (k p) -> (l k) p", p=P))\
                  .then_inc(gains_in, 16)

            def slab(l, seg, j, it, per, dst, src, mark=False):
                sp.wait_ge(lo_ready, l * SLABS + it * per + (SLAB0[seg] + j + 1))
                if mark:
                    sp.sem_inc(sp_mark, 1)
                slot = (SLAB0[seg] + j) % RING
                sp.dma_start(dst(raw[:, slot, :]), src).then_inc(raw_loaded[slot], 16)

            def full(r):
                return r.rearrange("p (k n) -> p k n", k=2)

            def head_dst(r):
                return r[:, 0:2 * HB].rearrange("p (c n) -> p c n", c=3)

            def cols(w, l, k0, nk, c0, nc_):
                return w[ds(l, 1), k0 * P:(k0 + nk) * P, ds(c0, nc_)].rearrange("o (k p) n -> p (o k) n", p=P)

            with sp.Fori(0, DEPTH) as l:
                for c, lm in enumerate((lam_re, lam_im)):
                    sp.dma_start(lam_rows[:, c, :], lm[ds(l, 1), :, :].rearrange("o (j g) s -> (o j) (g s)", g=2))\
                      .then_inc(s5_rows_in, 16)
                sp.dma_start(dt_rows[:, :], log_dt[ds(l, 1), :].rearrange("o (j g) -> (o j) g", g=2))\
                  .then_inc(s5_rows_in, 16)
                with sp.Fori(0, 2) as it:
                    for b in range(2):
                        for j in range(8):
                            slab(l, "proj", 8 * b + j, it, 16, full, cols(w_in, l, 2 * j, 2, it * -W + W + b * NB, NB))
                for j in range(2):
                    slab(l, "lat", j, 0, 0, lambda r: r[:, 0:8 * ROPE].rearrange("p (k n) -> p k n", k=8),
                         cols(w_in, l, 8 * j, 8, COL_KR, ROPE))
                for b in range(7):
                    w, c0 = (w_uq, b * NB) if b < 3 else (w_ukv, (b - 3) * NB)
                    for j in range(2):
                        slab(l, "lat", 2 + 2 * b + j, 0, 0, full, cols(w, l, 2 * j, 2, c0, NB))
                for seg, col in (("sb", COL_SB), ("gate", COL_GATE)):
                    with sp.Fori(0, HEADS // 2) as it:
                        for j in range(KT):
                            src = w_in[ds(l, 1), j * P:(j + 1) * P, col:col + 3 * W]
                            src = src.rearrange("o p (c n) -> (o p) c n", c=3)
                            slab(l, seg, j, it, 16, head_dst, src[:, :, ds(it * 2 * HD, 2 * HD)])

                def merge_step(br, n, j0=0):
                    seg = f"merge{br}"
                    for j in range(8):
                        slab(l, seg, j + j0, n, 12, full,
                             cols(w_in, l, 2 * j, 2, COL_MERGE + br * D + n * NB, NB))
                    for j in range(4):
                        src = w_branch[ds(l, 1), br, 2 * j * P:(2 * j + 2) * P, ds(n * NB, NB)]
                        slab(l, seg, 8 + j + j0, n, 12, full, src.rearrange("o (k p) n -> p (o k) n", p=P))

                for br in (2, 1):
                    with sp.Fori(0, 4) as n:
                        merge_step(br, n)
                for j in range(5):
                    slab(l, "ssm", j, 0, 0, full, cols(w_in, l, 2 * j, 2, COL_MERGE, NB))
                for b in range(2):
                    for j in range(4):
                        slab(l, "ssm", 5 + 4 * b + j, 0, 0, full, cols(w_glu, l, 2 * j, 2, b * NB, NB))
                for j in range(5, 8):
                    slab(l, "ssm", 8 + j, 0, 0, full, cols(w_in, l, 2 * j, 2, COL_MERGE, NB))
                for j in range(4):
                    src = w_branch[ds(l, 1), 0, 2 * j * P:(2 * j + 2) * P, 0:NB]
                    slab(l, "ssm", 16 + j, 0, 0, full, src.rearrange("o (k p) n -> p (o k) n", p=P), mark=j == 0)
                with sp.Fori(1, 4) as n:
                    merge_step(0, n, j0=-12)
                sp.wait_ge(ys_ready, l * 4 + 4)
                sp.dma_start(p_in, p[ds(l, 1), 0, :, :].rearrange("o (t p) c -> p (o t) c", p=P)).then_inc(p_loaded, 16)
                sp.wait_ge(q_y_out, l * QUADS + QUADS)
                sp.wait_ge(x_kept, l * 16 + 16)
                sp.dma_start(xs, x_keep.rearrange("(t p) d -> p t d", p=P)).then_inc(x_back, 16)
                with sp.Fori(0, 2) as it:
                    for b in range(2):
                        for j in range(8):
                            slab(l, "out", 8 * b + j, it, 16, full, cols(w_out, l, 2 * j, 2, it * 1024 + b * NB, NB))
                for b in range(4):
                    slab(l, "pproj", b, 0, 0, full, cols(w_ple_proj, l, 0, 2, b * NB, NB))
                with sp.Fori(0, 2) as it:
                    for b in range(2):
                        for j in range(8):
                            slab(l, "ple", 8 * b + j, it, 16, full,
                                 cols(w_ple_gate, l, 2 * j, 2, it * 1024 + b * NB, NB))
            sp.wait_ge(tr_in, DEPTH * NSTEP)
            sp.dma_start(fin_g, final_g.rearrange("(o n) -> o n", o=1).broadcast_to([P, D])).then_inc(fin_g_in, 16)
            for t in range(TOK):
                for i, c in enumerate((slice(0, D // 2), slice(D // 2, D))):
                    sp.wait_ge(out_ready, 2 * t + i + 1)
                    sp.dma_start(out[0, t * P:(t + 1) * P, c], xn[:, t, c]).then_inc(out_done, 16)
            sp.wait_ge(out_done, 16 * 2 * TOK)

        @block.gpsimd
        def _(pool):
            pool.sem_inc(lo_ready, RING)
            pool.wait_ge(raw_loaded[1], 16)
            pool.dma_start(masks[:, :, :], masks_in).then_inc(consts_in, 16)
            pool.dma_start(rope_t[:, :, :, :], rope_in).then_inc(consts_in, 16)
            with pool.Fori(0, DEPTH) as l:
                def lows(g0, groups, n):
                    with pool.Fori(0, groups) as g:
                        for slot in range(RING):
                            i = l * SLABS + g * RING + (g0 * RING + slot)
                            pool.wait_ge(slab_used, i + 1)
                            pool.wait_ge(hi_ready, i + 1)
                            nc.gpsimd.tensor_tensor(w_lo[:, slot, 0:n], raw[:, slot, 0:n],
                                                    w_hi[:, slot, 0:n].bitcast(f32), ALU.subtract)\
                              .then_inc(lo_ready, 1)
                g1, g2, g3 = SLAB0["sb"] // RING, SLAB0["merge2"] // RING, SLABS // RING
                lows(0, g1, SLOT)
                lows(g1, g2 - g1, 2 * HB)
                lows(g2, g3 - g2, SLOT)

        @block.tensor
        def _(pe):
            pe.sem_inc(slab_used, RING)
            pe.sem_inc(block_out[0], 1)
            pe.sem_inc(block_out[1], 1)
            pe.sem_inc(tr_lo, 2)
            pe.sem_inc(h_o_out, 1)
            pe.wait_ge(ident_loaded, 16)
            pe.wait_ge(gains_in, 16 * 4)
            nc.tensor.transpose(aux[:, 0, 0:DEPTH * NG], g_rows[:, :], ident[0:DEPTH * NG, 0:DEPTH * NG])\
              .then_inc(gains_t, 1)

            def products(l, seg, j, it, per, pair, ks, n, first, last, big=True):
                slot = (SLAB0[seg] + j) % RING
                hi, lo = (hT_hi, hT_lo) if big else (yT_hi, yT_lo)
                pe.wait_ge(lo_ready, l * SLABS + it * per + (SLAB0[seg] + j + 1 + RING))
                for i, k in enumerate(ks):
                    wh, wl = (w[:, slot, i * n:(i + 1) * n] for w in (w_hi, w_lo))
                    for t in range(TOK):
                        o = main[:, 2 * pair + t, 0:n] if pair < 2 else aux[:, t, 0:n]
                        a, b = (z[:, k, t * P:(t + 1) * P] for z in (hi, lo))
                        f, e = first and i == 0, last and i == len(ks) - 1
                        nc.tensor.matmul(o, a, wh, start=f, stop=False)
                        nc.tensor.matmul(o, a, wl, start=False, stop=False)
                        m = nc.tensor.matmul(o, b, wh, start=False, stop=e)
                m.then_inc(slab_used, 1)

            def pair_free(l, seg, it, b):
                pe.wait_ge(block_out[b % 2], l * PAIRS + it + (PAIR0[seg] + b // 2 + 1))

            def whole_block(l, seg, b, nslab, n=NB, big=True, k0=0, before=None):
                pair_free(l, seg, 0, b)
                for j in range(nslab):
                    if before:
                        before(b, j)
                    products(l, seg, nslab * b + j, 0, 0, b % 2, (k0 + 2 * j, k0 + 2 * j + 1), n, j == 0,
                             j == nslab - 1, big)

            def four_blocks(l, seg, operand, src, beside=None):
                def before(b, j):
                    if beside:
                        beside(b, j)
                    if b:
                        return
                    if operand != "merged" and j < 3:
                        transposes(l, operand, src, 2, at=2 * j + 2)
                    if operand == "merged" and j in (0, 2):
                        transposes(l, operand, src, 2, at=j + 4)
                    transposed(l, operand, j + 1)

                if operand == "ln":
                    transposes(l, operand, src, 2)
                for b in range(4):
                    whole_block(l, seg, b, 8, before=before)

            def two_heads_products(l, seg, j, it):
                slot = (SLAB0[seg] + j) % RING
                pe.wait_ge(lo_ready, l * SLABS + it * 16 + (SLAB0[seg] + j + 1 + RING))
                for b in range(2):
                    if j == 0:
                        pair_free(l, seg, it, b)
                    wh, wl = (w[:, slot, 0:2 * HB].rearrange("p (c n) -> p c n", c=3)[:, :, b * HD:(b + 1) * HD]
                              for w in (w_hi, w_lo))
                    for t in range(TOK):
                        o = main[:, 2 * b + t, 0:HB].rearrange("p (c n) -> p c n", c=3)
                        x_hi, x_lo = (z[:, j, t * P:(t + 1) * P] for z in (hT_hi, hT_lo))
                        nc.tensor.matmul(o, x_hi, wh, start=j == 0, stop=False)
                        nc.tensor.matmul(o, x_hi, wl, start=False, stop=False)
                        m = nc.tensor.matmul(o, x_lo, wh, start=False, stop=j == KT - 1)
                    if b == 0 and j == KT - 1:
                        m.then_inc(pair_a_full, 1)
                m.then_inc(slab_used, 1)

            def transposes(l, seg, src, steps, per=2, at=0):
                for i in range(at, at + steps):
                    n = STEP0[seg] + i
                    if seg in ("ln", "ple") and i % 2 == 0:
                        pe.wait_ge(xn_ready, l * 8 + (i // 2 + (1 if seg == "ln" else 5)))
                    if seg == "merged" and i % 2 == 0:
                        pe.wait_ge(merged_ready, l * 4 + (i // 2 + 1))
                    pe.wait_ge(tr_lo, l * NSTEP + (n + 1))
                    for k in range(per):
                        for t in range(TOK):
                            m = nc.tensor.transpose(trb[:, n % 2, (2 * k + t) * P:(2 * k + t + 1) * P],
                                                    src(t)[:, (per * i + k) * P:(per * i + k + 1) * P], ident[:, :])
                    m.then_inc(tr_in, 1)

            def transposed(l, seg, steps):
                pe.wait_ge(tr_lo, l * NSTEP + (STEP0[seg] + steps + 2))

            with pe.Fori(0, DEPTH) as l:
                def s5_rows():
                    pe.wait_ge(gains_ready, 1)
                    pe.wait_ge(dt_wide_ready, l + 1)
                    pe.sem_inc(pe_mark, 1)
                    for c in range(2):
                        nc.tensor.transpose(aux[:, 0, c * NTILE:(c + 1) * NTILE], lam_rows[:, c, :],
                                            ident[0:NTILE, 0:NTILE])
                    nc.tensor.transpose(aux[:, 0, 2 * NTILE:3 * NTILE], dt_wide[:, :, :].rearrange("j g s -> j (g s)"),
                                        ident[0:NTILE, 0:NTILE]).then_inc(s5_cols_in, 1)

                def latents(j):
                    if j in (3, 5):
                        seg = "qlat" if j == 3 else "kvlat"
                        pe.wait_ge(lat_norm, l * 2 + j // 2)
                        transposes(l, seg, lambda t: lat[:, t, (j // 5) * LAT:(j // 5 + 1) * LAT], 2)

                def beside_proj(b, j):
                    if (b, j) == (0, 4):
                        s5_rows()
                    if b == 2:
                        latents(j)

                four_blocks(l, "proj", "ln", lambda t: xn[:, t, :], beside_proj)
                pair_free(l, "lat", 0, 0)
                for j in range(2):
                    slot = (SLAB0["lat"] + j) % RING
                    pe.wait_ge(lo_ready, l * SLABS + (SLAB0["lat"] + j + 1 + RING))
                    for i in range(8):
                        k = 8 * j + i
                        wh, wl = (w[:, slot, i * ROPE:(i + 1) * ROPE] for w in (w_hi, w_lo))
                        o = main[0:ROPE, 0, 0:SEQ]
                        nc.tensor.matmul(o, wh, hT_hi[:, k, :], start=k == 0, stop=False)
                        nc.tensor.matmul(o, wh, hT_lo[:, k, :], start=False, stop=False)
                        m = nc.tensor.matmul(o, wl, hT_hi[:, k, :], start=False, stop=k == KT - 1)
                    m.then_inc(slab_used, 1)
                transposed(l, "qlat", 2)
                for b in range(1, 8):
                    if b == 4:
                        transposed(l, "kvlat", 2)
                    whole_block(l, "lat", b, 2, big=False, k0=0 if b < 4 else 4)
                    if b == 1:
                        pe.wait_ge(kr_raw, l + 1)
                        pe.sem_inc(pe_mark, 1)
                        for t in range(TOK):
                            m = nc.tensor.transpose(aux[:, 0, t * ROPE:(t + 1) * ROPE], krT[:, t * P:(t + 1) * P],
                                                    ident[0:ROPE, 0:ROPE])
                        m.then_inc(kr_back, 1)
                    if b == 5:
                        pe.wait_ge(kr_ready, l + 1)
                        pe.sem_inc(pe_mark, 1)
                        for t in range(TOK):
                            m = nc.tensor.transpose(aux[0:ROPE, 0, t * P:(t + 1) * P], kr[:, t, :], ident[:, :])
                        m.then_inc(kr_t, 1)

                def head_transposes(n, rope):
                    pe.wait_ge(h_static, n + 1)
                    pe.wait_ge(h_o_out, n + 1)
                    for i, z in enumerate((q_s, k_s) if rope else (qk_s, qk_s)):
                        for t in range(TOK):
                            c = 0 if rope or i == 0 else P
                            m = nc.tensor.transpose(trb[:, 0, (2 * i + t) * P:(2 * i + t + 1) * P],
                                                    z[:, t, c:c + P], ident[:, :])
                    if rope:
                        for t in range(TOK):
                            m = nc.tensor.transpose(trb[0:ROPE, 1, t * P:(t + 1) * P], q_s[:, t, P:P + ROPE],
                                                    ident[:, :])
                    m.then_inc(h_qkT_in, 1)

                def head_scores(n, rope):
                    pe.wait_ge(h_qkT, n + 1)
                    for t, (c, nk) in enumerate(((0, P), (P, 2 * P))):
                        m = nc.tensor.matmul(aux[:, 0, c:c + nk], qkT[:, t * P:(t + 1) * P], qkT[:, 256:256 + nk],
                                             start=True, stop=not rope)
                        if rope:
                            m = nc.tensor.matmul(aux[:, 0, c:c + nk], qrT[:, t * P:(t + 1) * P], krT[:, 0:nk],
                                                 start=False, stop=True)
                    m.then_inc(h_scores, 1)

                def head_probs(n):
                    pe.wait_ge(h_probs, n + 1)
                    for i in range(3):
                        m = nc.tensor.transpose(aux[:, 1, i * P:(i + 1) * P], s_b[:, i * P:(i + 1) * P], ident[:, :])
                    m.then_inc(h_pT_in, 1)

                def head_out(n, v):
                    pe.wait_ge(h_pT, n + 1)
                    nc.tensor.matmul(trb[:, 1, 256:384], pT[:, 0:P], v(0), start=True, stop=True)
                    nc.tensor.matmul(trb[:, 1, 384:512], pT[:, P:2 * P], v(0), start=True, stop=False)
                    nc.tensor.matmul(trb[:, 1, 384:512], pT[:, 2 * P:3 * P], v(1), start=False, stop=True)\
                      .then_inc(h_o_in, 1)

                for seg in ("sb", "gate"):
                    mla = seg == "sb"
                    if mla:
                        pe.wait_ge(kr_out, l + 1)
                        pe.sem_inc(pe_mark, 1)
                    with pe.Fori(0, HEADS // 2) as it:
                        for b in range(2):
                            n = l * 2 * HEADS + it * 2 + (b if mla else HEADS + b)
                            for j in range(8):
                                two_heads_products(l, seg, 8 * b + j, it)
                                if j == 1:
                                    head_transposes(n, mla)
                                if j == 2:
                                    head_scores(n, mla)
                                if j == (5 if mla else 6):
                                    head_probs(n)
                            if mla:
                                head_out(n, lambda t: mla_kv[:, t, ds(it * 4 * HD + (2 * b + 1) * HD, HD)])
                            else:
                                head_out(n, lambda t: ys[:, t, 2, ds(it * 2 * HD + b * HD, HD)])

                def s5_out(quads):
                    pe.wait_ge(q_h, quads)
                    for t in range(TOK):
                        for i in range(4):
                            for c in range(2):
                                m = nc.tensor.matmul(aux[:, 0, t * P + i * 32:t * P + (i + 1) * 32],
                                                     pr1[:, c, i * SEQ + t * P:i * SEQ + (t + 1) * P],
                                                     cbd[:, c, i, :], start=c == 0, stop=c == 1)
                    m.then_inc(q_y, 1)

                def merge_step(br, n, first=False, last=False, j0=0):
                    seg = f"merge{br}"
                    q = l * QUADS + n + 4 * (2 - br)
                    at_T, at_bu, at_ys = (3, (6, 8), (6, 8)) if first and br == 2 else (2, (4, 7), (5, 7))
                    for j in range(12):
                        if j in (0, 8):
                            pair_free(l, seg, n, j // 8 + j0 // 6)
                        if j >= 8:
                            transposed(l, f"ys{br}", j - 7)
                        ks = (2 * j, 2 * j + 1) if j < 8 else (2 * j - 16, 2 * j - 15)
                        products(l, seg, j + j0, n, 12, j // 8, ks, NB, j in (0, 8), j in (7, 11), j < 8)
                        if br and j == 1 and not (first and br == 2):
                            s5_out(q)
                        if br and j == at_T:
                            pe.wait_ge(q_bb, q + 1)
                            if not (first and br == 2):
                                pe.wait_ge(q_y_out, q)
                            for t in range(TOK):
                                nc.tensor.transpose(aux[:, 0, t * P:(t + 1) * P], u_q[:, t, :], ident[:, :])
                            for c in range(2):
                                nc.tensor.transpose(aux[:, 0, (2 + c) * P:(3 + c) * P],
                                                    bb[:, c, :, :].rearrange("p j h -> p (j h)"), ident[:, :])
                            for c in range(2):
                                m = nc.tensor.transpose(aux[:, 1, c * P:(c + 1) * P], c_ld[:, c, :], ident[:, :])
                            m.then_inc(q_T_in, 1)
                        if first and j in at_ys:
                            pe.wait_ge(ys_ready, l * 4 + (3 - br))
                            transposes(l, f"ys{br}", lambda t: ys[:, t, br, :], 2, at=2 * at_ys.index(j))
                        if br and j in at_bu:
                            half = at_bu.index(j)
                            if half == 0:
                                pe.wait_ge(q_T_out, q + 2)
                            else:
                                pe.wait_ge(q_bu_used, q * 2 + 1)
                            for c in range(2):
                                for i in range(2):
                                    m = nc.tensor.matmul(aux[:, c, i * SEQ:(i + 1) * SEQ],
                                                         bbT[:, c, 2 * half + i, :], uT, start=True, stop=True)
                            m.then_inc(q_bu, 1)
                        if last and j in (8, 10):
                            transposes(l, "merged", lambda t: merged[:, t, :], 2, at=j - 8)

                for br in (2, 1):
                    merge_step(br, 0, True)
                    with pe.Fori(1, 4) as n:
                        merge_step(br, n)
                def logits(j):
                    products(l, "ssm", j if j < 5 else 8 + j, 0, 0, 0, (2 * j, 2 * j + 1), NB, j == 0, j == 7)

                pair_free(l, "ssm", 0, 0)
                for j in range(5):
                    logits(j)
                    if j == 1:
                        s5_out((l + 1) * QUADS)
                    if j >= 3:
                        pe.wait_ge(gelu_ready, l + 1)
                        transposes(l, "glu", lambda t: ys[:, t, 0, :], 2, at=2 * (j - 3))
                pair_free(l, "ssm", 0, 1)
                for b in range(2):
                    for j in range(4):
                        transposed(l, "glu", j + 1)
                        products(l, "ssm", 5 + 4 * b + j, 0, 0, 1 + b, (2 * j, 2 * j + 1), NB, j == 0, j == 3, False)
                for j in range(5, 8):
                    if j != 6:
                        pe.wait_ge(ys_ready, l * 4 + (3 + j // 6))
                        transposes(l, "ys0", lambda t: ys[:, t, 0, :], 2, at=2 * (j // 6))
                    logits(j)
                pair_free(l, "ssm", 0, 3)
                for j in range(4):
                    transposed(l, "ys0", j + 1)
                    products(l, "ssm", 16 + j, 0, 0, 1, (2 * j, 2 * j + 1), NB, j == 0, j == 3, False)
                with pe.Fori(1, 3) as n:
                    merge_step(0, n, j0=-12)
                merge_step(0, 3, last=True, j0=-12)

                def p_transposes(b, j):
                    if (b, j) == (3, 4):
                        pe.wait_ge(p_loaded, l * 16 + 16)
                        transposes(l, "p", lambda t: p_in[:, t, :], 2, per=1)

                four_blocks(l, "out", "merged", lambda t: merged[:, t, :], p_transposes)
                transposed(l, "p", 2)
                for b in range(4):
                    if b == 3:
                        transposes(l, "ple", lambda t: xn[:, t, :], 2)
                    pair_free(l, "pproj", 0, b)
                    products(l, "pproj", b, 0, 0, b % 2, (0, 1), NB, True, True, False)
                four_blocks(l, "ple", "ple", lambda t: xn[:, t, :])

        def used(l, seg, j, it=0, per=0):
            return l * SLABS + it * per + (SLAB0[seg] + j + 1 + RING)

        @block.scalar
        def _(act):
            A = nc.scalar.activation
            chain = Chain(act, act_chain)

            def split(l, seg, j, it=0, per=0):
                at = SLAB0[seg] + j
                slot = at % RING
                n = 2 * HB if SLAB0["sb"] <= at < SLAB0["merge2"] and not (seg == "gate" and j >= per) else SLOT
                i = l * SLABS + it * per + at
                act.wait_ge(raw_loaded[slot], (l * (SLABS // RING) + it * (per // RING) + (at // RING + 1)) * 16)
                act.wait_ge(slab_used, i + 1)
                A(w_hi[:, slot, 0:n], raw[:, slot, 0:n], ACT.Copy).then_inc(hi_ready, 1)

            def splits(l, seg, a, b, it=0, per=0):
                for j in range(a, b):
                    split(l, seg, j, it, per)

            def squares(b, ready=None):
                for t in range(TOK):
                    if ready is not None:
                        act.wait_ge(x_half, ready + t)
                    m = A(junk[:, t * NB:(t + 1) * NB], xs[:, t, ds(b * NB, NB)], ACT.Square,
                          accum_out=st_p[:, t, ds(b, 1)])
                m.then_inc(sq_done, 1)

            def root(value, at):
                act.wait_ge(ms_ready, value)
                A(st_r[:, at:at + 2], st_ss[:, at:at + 2], ACT.Sqrt).then_inc(root_ready, 1)

            def highs(l, seg, steps, dst, per=2, gain=None, k0=0, at=0):
                for i in range(at, at + steps):
                    n = STEP0[seg] + i
                    act.wait_ge(tr_in, l * NSTEP + (n + 1))
                    for k in range(per):
                        kk = k0 + per * i + k
                        s = 1.0 if gain is None else gc[:, gain + per * i + k:gain + per * i + k + 1]
                        m = A(dst[:, kk, :], trb[:, n % 2, 2 * k * P:(2 * k + 2) * P], ACT.Copy, scale=s)
                    m.then_inc(tr_hi, 1)

            act.wait_ge(one_ready, 1)
            A(warm[:, :], one[:, :], ACT.Sqrt)
            for b in range(D // NB):
                act.wait_ge(x_in[b], 16)
                act.wait_ge(sq_done, b + 1)
                squares(b)
            with act.Fori(0, DEPTH) as l:
                root(l * 4 + 1, 0)
                for i in range(RING):
                    split(l, "proj", i)
                    highs(l, "ln", 2, hT_hi, gain=0, at=2 * i)
                act.wait_ge(layer_done, l + 1)
                act.dma_start(x_keep.rearrange("(t p) d -> p t d", p=P), xs).then_inc(x_kept, 16)
                splits(l, "proj", RING, 8)
                act.wait_ge(s5_lam_ready, l * 2 + 1)
                A(sm[:, 0, :], lam[:, 2, :], ACT.Exp).then_inc(s5_exp_ready, 1)
                splits(l, "proj", 8, 12)
                act.wait_ge(s5_lam_ready, l * 2 + 2)
                A(prm[:, 0, :], sm[:, 1, :], ACT.Exp).then_inc(s5_exp_ready, 1)
                act.wait_ge(s5_ang_ready, l + 1)
                A(pw[:, 0, 1, :], sm[:, 2, :], ACT.Sin)
                A(pw[:, 0, 0, :], sm[:, 3, :], ACT.Sin).then_inc(s5_trig_ready, 1)
                splits(l, "proj", 12, 13)
                for b in range(2):
                    act.wait_ge(slab_used, used(l, "proj", 8 * b + 7))
                    for t in range(TOK):
                        m = A(junk[:, t * NB:(t + 1) * NB], main[:, 2 * b + t, :], ACT.Square,
                              accum_out=st_ss[:, 2 * (1 - b) + t:2 * (1 - b) + t + 1])
                    m.then_inc(lat_sq, 1)
                    root(l * 4 + 2 + b, 2 * (1 - b))
                    splits(l, "proj", 13 + 7 * b, 20 + 4 * b)
                highs(l, "qlat", 2, yT_hi, gain=32)
                splits(l, "proj", 24, 26)
                highs(l, "kvlat", 2, yT_hi, gain=36, k0=4)
                splits(l, "proj", 26, 32 + RING)
                splits(l, "lat", RING, 16)
                act.wait_ge(kr_t, l + 1)
                A(krT, aux[0:ROPE, 0, 0:SEQ], ACT.Copy).then_inc(kr_out, 1)
                splits(l, "lat", 16, 16 + RING)

                def quad_loads(q):
                    for c, bm in enumerate((b_re, b_im)):
                        act.dma_start(b_ld[:, c, :, :], bm[ds(l, 1), ds(q * 8, 8), :, :]
                                      .rearrange("o (j g) s h -> (g s) (o j) h", g=2)).then_inc(q_ld, 16)
                    for c, cm in enumerate((c_re, c_im)):
                        act.dma_start(c_ld[:, c, :].rearrange("p (z s) -> p z s", z=2),
                                      cm[ds(l, 1), ds(q * 8, 8), :, :].rearrange("o g h s -> (g h) o s")
                                      .broadcast_to([P, 2, STATE])).then_inc(q_ld, 16)
                    act.dma_start(d_q, d_skip[ds(l, 1), ds(q * P, P)].broadcast_to([P, P])).then_inc(q_ld, 16)

                with act.Fori(0, HEADS // 2) as it:
                    for b in range(2):
                        n = l * 2 * HEADS + it * 2 + b
                        splits(l, "sb", 8 * b + 4, 8 * b + 6, it, 16)
                        act.wait_ge(h_qkT_in, n + 1)
                        A(qkT[:, 0:256], trb[:, 0, 0:256], ACT.Copy, scale=MLA_SCALE)
                        A(qkT[:, 256:512], trb[:, 0, 256:512], ACT.Copy)
                        A(qrT, trb[0:ROPE, 1, 0:256], ACT.Copy, scale=MLA_SCALE).then_inc(h_qkT, 1)
                        splits(l, "sb", 8 * b + 6, 8 * b + 8, it, 16)
                        act.wait_ge(h_max, l * HEADS + it * 2 + (b + 1))
                        A(s_b[:, 0:P], s_a[:, 0:P], ACT.Exp, bias=nmx[:, 0:1], accum_out=sums[:, 0:1])
                        A(s_b[:, P:384], s_a[:, P:384], ACT.Exp, bias=nmx[:, 1:2], accum_out=sums[:, 1:2])\
                            .then_inc(h_probs, 1)
                        splits(l, "sb", 8 * b + 8, 8 * b + 10, it, 16)
                        act.wait_ge(h_pT_in, n + 1)
                        A(pT, aux[:, 1, 0:384], ACT.Copy).then_inc(h_pT, 1)
                        splits(l, "sb", 8 * b + 10, 8 * b + 11, it, 16)
                        if b == 1:
                            act.wait_ge(pair_a_full, l * HEADS + it + 1)
                            A(sb_qk[:, :, ds(it * 2, 1), :].rearrange("p t o c -> p t (o c)"), main[:, 0:2, 0:256],
                              ACT.Copy)
                            A(ys[:, :, 2, ds(it * 256, HD)], main[:, 0:2, 256:384], ACT.Copy)\
                                .then_inc(block_out[0], 1)
                        splits(l, "sb", 8 * b + 11, 8 * b + 12, it, 16)
                with act.Fori(0, HEADS // 2) as it:
                    for b in range(2):
                        n = l * 2 * HEADS + it * 2 + (HEADS + b)
                        g = l * HEADS + it * 2 + b
                        chain.clear()
                        splits(l, "gate", 8 * b + 4, 8 * b + 6, it, 16)
                        act.wait_ge(h_qkT_in, n + 1)
                        A(qkT[:, 0:256], trb[:, 0, 0:256], ACT.Copy, scale=SB_SCALE)
                        A(qkT[:, 256:512], trb[:, 0, 256:512], ACT.Copy).then_inc(h_qkT, 1)
                        splits(l, "gate", 8 * b + 6, 8 * b + 7, it, 16)
                        act.wait_ge(h_scores, n + 1)
                        chain(A(s_a, aux[:, 0, 0:384], ACT.Abs))
                        chain(A(s_b, s_a, ACT.Exp, scale=-1.0))
                        A(s_a, s_b, ACT.Ln, bias=one[:, 0:1]).then_inc(sb_soft, 1)
                        splits(l, "gate", 8 * b + 7, 8 * b + 9, it, 16)
                        act.wait_ge(sb_arg, g + 1)
                        A(s_b, s_c, ACT.Exp).then_inc(h_probs, 1)
                        splits(l, "gate", 8 * b + 9, 8 * b + 11, it, 16)
                        act.wait_ge(h_pT_in, n + 1)
                        A(pT, aux[:, 1, 0:384], ACT.Copy).then_inc(h_pT, 1)
                        if b == 1:
                            act.wait_ge(pair_a_full, l * HEADS + it + (HEADS // 2 + 1))
                            A(gates[:, :, :, ds(it * 256, HD)],
                              main[:, 0:2, 0:HB].rearrange("p t (c n) -> p t c n", c=3), ACT.Copy)\
                                .then_inc(block_out[0], 1)
                        splits(l, "gate", 8 * b + 11, 8 * b + 12, it, 16)
                chain.clear()
                for b in range(2):
                    act.wait_ge(block_out[b], l * PAIRS + (PAIR0["gate"] + 5))
                A(gates[:, :, 2, :], gates[:, :, 2, :], ACT.Silu).then_inc(silu_done, 1)
                act.wait_ge(heads_left, l + 1)
                quad_loads(0)
                A(gates[:, :, 1, :], gates[:, :, 1, :], ACT.Silu).then_inc(silu_done, 1)
                splits(l, "merge2", 4, 6)
                A(gate_ssm[:, :, :], gates[:, :, 0, :], ACT.Silu).then_inc(silu_done, 1)

                def sigmoid(done, pair, dst, ready):
                    act.wait_ge(slab_used, done)
                    A(dst, main[:, 2 * pair:2 * pair + 2, :] if pair < 2 else aux[:, :, :], ACT.Sigmoid).then_inc(ready, 1)

                def merge_step(br, n, first=False, last=False, j0=0):
                    seg = f"merge{br}"
                    q = l * QUADS + n + 4 * (2 - br)
                    at_T = 8 if first and br == 2 else 7
                    splits(l, seg, (6 if first and br == 2 else 4) + j0, at_T + j0, n, 12)
                    if br:
                        act.wait_ge(q_T_in, q + 1)
                        A(uT, aux[:, 0, 0:SEQ], ACT.Copy)
                        for c in range(2):
                            for i in range(4):
                                A(bbT[:, c, i, :], aux[:, 0, (2 + c) * P:(3 + c) * P], ACT.Copy,
                                  scale=rowsel[:, i:i + 1])
                        for c in range(2):
                            for g in range(2):
                                s = slice(g * STATE, (g + 1) * STATE)
                                src = aux[s, 1, c * P:(c + 1) * P].rearrange("p (j g h) -> p j g h", j=4, g=2)
                                m = A(cbd[s, c, :, g * GROUP:(g + 1) * GROUP], src[:, :, g, :], ACT.Copy,
                                      scale=-1.0 if c else 1.0)
                        m.then_inc(q_T_out, 1)
                        if not (last and br == 1):
                            quad_loads(n + (4 * (2 - br) + 1))
                    if first:
                        at_ys = 11 if br == 2 else 10
                        splits(l, seg, at_T, at_ys, n, 12)
                        highs(l, f"ys{br}", 2, yT_hi)
                        splits(l, seg, at_ys, 12, n, 12)
                        if br == 1:
                            highs(l, f"ys{br}", 2, yT_hi, at=2)
                    else:
                        splits(l, seg, at_T + j0, 12 + j0, n, 12)
                    act.wait_ge(sig_used, l * 12 + n + (4 * (2 - br) + 1))
                    sigmoid(used(l, seg, 7 + j0, n, 12), 0, sig, sig_ready)
                    act.wait_ge(sig_ready, l * 12 + n + (4 * (2 - br) + 1))
                    act.sem_inc(block_out[0], 1)
                    for j in range(12, 16):
                        split(l, seg, j + j0, n, 12)
                        if first and br == 2 and j == 12:
                            highs(l, f"ys{br}", 2, yT_hi, at=2)
                        if last and br == 0 and j in (12, 14):
                            highs(l, "merged", 2, hT_hi, at=j - 12)

                for br in (2, 1):
                    merge_step(br, 0, first=True)
                    with act.Fori(1, 3) as n:
                        merge_step(br, n)
                    merge_step(br, 3, last=True)
                splits(l, "ssm", 4, 6)
                act.wait_ge(q_y_out, l * QUADS + QUADS)
                A(ys[:, :, 0, :], ys[:, :, 0, :], ACT.Gelu_apprx_tanh).then_inc(gelu_ready, 1)
                splits(l, "ssm", 6, 8)
                highs(l, "glu", 2, yT_hi)
                split(l, "ssm", 8)
                highs(l, "glu", 2, yT_hi, at=2)
                for b in range(2):
                    splits(l, "ssm", 9 + 4 * b, 13 + 4 * b)
                    act.wait_ge(glu_sig, (l * 2 + b) * 2 + 1)
                    sigmoid(used(l, "ssm", 8 + 4 * b), 1 + b, sig2, glu_sig)
                highs(l, "ys0", 2, yT_hi)
                splits(l, "ssm", 17, 19)
                highs(l, "ys0", 2, yT_hi, at=2)
                split(l, "ssm", 19)
                act.wait_ge(sig_used, l * 12 + 9)
                sigmoid(used(l, "ssm", 15), 0, sig, sig_ready)
                act.wait_ge(sig_ready, l * 12 + 9)
                act.sem_inc(block_out[0], 1)
                splits(l, "ssm", 20, 24)
                with act.Fori(1, 3) as n:
                    merge_step(0, n, j0=-12)
                merge_step(0, 3, last=True, j0=-12)
                highs(l, "merged", 4, hT_hi, at=4)
                for b in range(4):
                    splits(l, "out", 8 * b + 4, 8 * b + 8)
                    if b == 3:
                        highs(l, "p", 2, yT_hi, per=1)
                    splits(l, "out", 8 * b + 8, 8 * b + 12)
                    act.wait_ge(x_block, l * 4 + (b + 1))
                    act.wait_ge(sq_done, l * 8 + (b + 5))
                    squares(b)
                root(l * 4 + 4, 0)
                for b in range(4):
                    act.wait_ge(slab_used, used(l, "pproj", b))
                    A(e_ple[:, :, b * NB:(b + 1) * NB], main[:, 2 * (b % 2):2 * (b % 2) + 2, :], ACT.Copy)\
                        .then_inc(block_out[b % 2], 1)
                    split(l, "pproj", 4 + b)
                    if b == 2:
                        highs(l, "ple", 2, hT_hi, gain=16)
                highs(l, "ple", 6, hT_hi, gain=16, at=2)
                for b in range(4):
                    splits(l, "ple", 8 * b + 4, min(8 * b + 12, 32))
                    act.wait_ge(slab_used, used(l, "ple", 8 * b + 7))
                    for t in range(TOK):
                        act.wait_ge(ple_used, (l * 4 + b) * 2 + (t + 1))
                        A(sig[:, t, :], main[:, 2 * (b % 2) + t, :], ACT.Sigmoid).then_inc(ple_sig, 1)
                    if b == 3:
                        A(warm[:, :], one[:, :], ACT.Sqrt)
                    act.wait_ge(sq_done, l * 8 + (b + 9))
                    squares(b, (l * 4 + b) * 2 + 1)
            root(DEPTH * 4 + 1, 0)

        @block.vector
        def _(dve):
            v = nc.vector
            chain = Chain(dve, dve_chain)
            dve.sem_inc(sq_done, 1)
            dve.sem_inc(sig_used, 1)
            dve.sem_inc(glu_sig, 1)
            dve.sem_inc(ple_used, 2)
            dve.sem_inc(layer_done, 1)
            dve.sem_inc(q_T_out, 1)
            v.memset(one[:, :], 1.0).then_inc(one_ready, 1)
            chain(v.memset(bb, 0.0))
            chain(v.memset(cbd, 0.0))
            dve.wait_ge(ident_loaded, 16)
            for i in range(4):
                chain(v.reduce_sum(rowsel[:, i:i + 1], ident[:, 32 * i:32 * i + 32], AX.X))
            dve.wait_ge(gains_t, 1)
            v.tensor_copy(g_all[:, :], aux[:, 0, 0:DEPTH * NG]).then_inc(gains_ready, 1)
            dve.wait_ge(gains_ready, 1)
            chain.clear()

            def lows(l, seg, steps, hi, lo, per=2, gain=None, k0=0, at=0):
                for i in range(at, at + steps):
                    n = STEP0[seg] + i
                    dve.wait_ge(tr_hi, l * NSTEP + (n + 1))
                    for k in range(per):
                        kk = k0 + per * i + k
                        s = 1.0 if gain is None else gc[:, gain + per * i + k:gain + per * i + k + 1]
                        m = v.scalar_tensor_tensor(out=lo[:, kk, :], in0=trb[:, n % 2, 2 * k * P:(2 * k + 2) * P],
                                                   scalar=s, in1=hi[:, kk, :].bitcast(f32), op0=ALU.mult,
                                                   op1=ALU.subtract)
                    m.then_inc(tr_lo, 1)

            def mean_square(value, at, n):
                v.tensor_scalar(st_ss[:, at:at + 2], st_ss[:, at:at + 2], 1.0 / n, EPS, ALU.mult, ALU.add)\
                    .then_inc(ms_ready, 1)
                dve.wait_ge(root_ready, value)
                chain(v.reciprocal(st_r[:, at:at + 2], st_r[:, at:at + 2]))

            def norm(value, blocks):
                dve.wait_ge(sq_done, blocks + 1)
                chain(v.reduce_sum(st_ss[:, 0:2], st_p[:, :, :], AX.X))
                mean_square(value, 0, D)
                for b in range(D // NB):
                    c = slice(b * NB, (b + 1) * NB)
                    for t in range(TOK):
                        m = v.tensor_scalar(xn[:, t, c], xs[:, t, c], st_r[:, t:t + 1], None, ALU.mult)
                    m.then_inc(xn_ready, 1)

            def s5_parameters(l):
                lre, lim, ldt = (lam[:, i, :] for i in range(3))
                dt, ar, ang, quarter, k, r, ni, den = (sm[:, i, :] for i in range(8))
                tt = v.tensor_tensor
                dve.wait_ge(s5_cols_in, l + 1)
                chain(v.tensor_copy(lam[:, :, :].rearrange("p c j -> p (c j)"), aux[:, 0, 0:3 * NTILE]))
                dve.sem_inc(s5_lam_ready, 1)
                dve.wait_ge(s5_exp_ready, l * 2 + 1)
                chain(tt(ar, lre, dt, ALU.mult))
                chain(tt(ang, lim, dt, ALU.mult))
                dve.sem_inc(s5_lam_ready, 1)
                chain(v.tensor_scalar(k, ang, float(1 / TWO_PI), MAGIC, ALU.mult, ALU.add))
                chain(v.tensor_scalar(k, k, MAGIC, None, ALU.subtract))
                for part in (TP1, TP2, TP3):
                    chain(v.scalar_tensor_tensor(out=ang, in0=k, scalar=-part, in1=ang, op0=ALU.mult, op1=ALU.add))
                chain(v.tensor_scalar(ang, ang, PI_LOW, -PI_LOW, ALU.min, ALU.max))
                chain(v.scalar_tensor_tensor(out=quarter, in0=ang, scalar=-1.0, in1=ang, op0=ALU.mult, op1=ALU.min))
                chain(v.tensor_scalar(quarter, quarter, float(np.pi / 2), None, ALU.add))
                dve.sem_inc(s5_ang_ready, 1)

            def s5_coefficients(l):
                lre, lim = lam[:, 0, :], lam[:, 1, :]
                _, _, ang, _, k, r, ni, den = (sm[:, i, :] for i in range(8))
                tt = v.tensor_tensor
                dve.wait_ge(s5_exp_ready, l * 2 + 2)
                dve.wait_ge(s5_trig_ready, l + 1)
                chain(tt(r, prm[:, 0, :], pw[:, 0, 0, :], ALU.mult))
                chain(v.tensor_scalar(r, r, 1.0, None, ALU.subtract))
                chain(tt(ni, prm[:, 0, :], pw[:, 0, 1, :], ALU.mult))
                chain(tt(den, lre, lre, ALU.mult))
                chain(tt(k, lim, lim, ALU.mult))
                chain(tt(den, den, k, ALU.add))
                chain(v.reciprocal(den, den))
                chain(tt(k, r, lre, ALU.mult))
                chain(tt(ang, ni, lim, ALU.mult))
                chain(tt(k, k, ang, ALU.add))
                chain(tt(prm[:, 1, :], k, den, ALU.mult))
                chain(tt(k, ni, lre, ALU.mult))
                chain(tt(ang, r, lim, ALU.mult))
                chain(tt(k, k, ang, ALU.subtract))
                chain(tt(prm[:, 2, :], k, den, ALU.mult))
                for i in range(1, LEVELS):
                    c, s = pw[:, i - 1, 0, :], pw[:, i - 1, 1, :]
                    chain(tt(k, c, c, ALU.mult))
                    chain(tt(r, s, s, ALU.mult))
                    chain(tt(pw[:, i, 0, :], k, r, ALU.subtract))
                    chain(v.scalar_tensor_tensor(out=pw[:, i, 1, :], in0=c, scalar=2.0, in1=s, op0=ALU.mult,
                                                 op1=ALU.mult))

            def rotary(x1, x2, t, heads):
                half = ROPE // 2
                shape = [P, heads, half]
                c = rope_t[:, t, 0:1, :].broadcast_to(shape)
                s = rope_t[:, t, 1:2, :].broadcast_to(shape)
                a, b_, d = (z[:, 0:heads * half].rearrange("p (h c) -> p h c", h=heads)
                            for z in (rope_a, rope_b, rope_c))
                chain(v.tensor_tensor(a, x1, s, ALU.mult))
                chain(v.tensor_tensor(b_, x2, s, ALU.mult))
                chain(v.tensor_tensor(d, x1, c, ALU.mult))
                chain(v.tensor_tensor(x1, d, b_, ALU.subtract))
                chain(v.tensor_tensor(b_, x2, c, ALU.mult))
                chain(v.tensor_tensor(x2, a, b_, ALU.add))

            def quad_in(l, n, br):
                q = n + 4 * (2 - br)
                g = l * QUADS + q
                tt = v.tensor_tensor
                put, sync = chain.put, chain.sync
                put(v.tensor_copy(u_q, ys[:, :, 0, ds(q * P, P)]))
                put(v.tensor_copy(prm_q[:, :, :], prm[:, :, ds(q * 4, 4)]))
                put(v.tensor_copy(pw_q[:, :, :, :].rearrange("p a b j -> p (a b) j"),
                                  pw[:, :, :, :].rearrange("p a b j -> p (a b) j")[:, :, ds(q * 4, 4)]))
                sync()
                dve.wait_ge(q_ld, (g + 1) * (16 * 5))
                wide = [P, 4, GROUP]
                cr = prm_q[:, 1, :].rearrange("p (j o) -> p j o", o=1).broadcast_to(wide)
                ci = prm_q[:, 2, :].rearrange("p (j o) -> p j o", o=1).broadcast_to(wide)
                for c in range(2):
                    put(tt(b_t1[:, c, :, :], b_ld[:, c, :, :], cr, ALU.mult))
                    put(tt(b_t2[:, c, :, :], b_ld[:, c, :, :], ci, ALU.mult))
                put(tt(ys[:, :, 0, ds(q * P, P)], u_q, d_q.rearrange("p (o c) -> p o c", o=1).broadcast_to([P, TOK, P]), ALU.mult))
                sync()
                for h in range(2):
                    s = slice(h * STATE, (h + 1) * STATE)
                    o = slice(h * GROUP, (h + 1) * GROUP)
                    put(tt(bb[s, 0, :, o], b_t1[s, 0, :, :], b_t2[s, 1, :, :], ALU.subtract))
                    put(tt(bb[s, 1, :, o], b_t1[s, 1, :, :], b_t2[s, 0, :, :], ALU.add))
                sync()
                dve.sem_inc(q_bb, 1)

            def quad(l, n, br, between):
                q = n + 4 * (2 - br)
                g = l * QUADS + q
                tt = v.tensor_tensor
                put, sync = chain.put, chain.sync
                chain(v.memset(tab4[:, 0, :, 0:1], 1.0))
                chain(v.memset(tab4[:, 1, :, 0:1], 0.0))
                pa = pr2[:, 0, :].rearrange("p (c j t) -> p c j t", c=2, j=4)
                pb = pr2[:, 1, :].rearrange("p (c j t) -> p c j t", c=2, j=4)
                for k in range(LEVELS):
                    m = 1 << k
                    wr, wi = (pw_q[:, k, z, :].rearrange("p (c j o) -> p c j o", c=1, o=1)
                              .broadcast_to([P, 2, 4, m]) for z in range(2))
                    put(tt(pa[:, :, :, 0:m], tab4[:, :, :, 0:m], wr, ALU.mult))
                    put(tt(pb[:, :, :, 0:m], tab4[:, :, :, 0:m], wi, ALU.mult))
                    sync()
                    put(tt(tab4[:, 0, :, m:2 * m], pa[:, 0, :, 0:m], pb[:, 1, :, 0:m], ALU.subtract))
                    put(tt(tab4[:, 1, :, m:2 * m], pa[:, 1, :, 0:m], pb[:, 0, :, 0:m], ALU.add))
                    sync()
                for half in range(2):
                    if between:
                        between(half)
                    s = slice(half * 512, half * 512 + 512)
                    cos, sin = (tab[:, z:z + 1, s].broadcast_to([P, 2, 512]) for z in range(2))
                    dve.wait_ge(q_bu, g * 2 + (half + 1))
                    put(tt(pr1[:, :, s], aux[:, :, :], cos, ALU.mult))
                    put(tt(pr2[:, :, s], aux[:, :, :], sin, ALU.mult))
                    sync()
                    dve.sem_inc(q_bu_used, 1)
                    put(tt(st[:, 0, s], pr1[:, 0, s], pr2[:, 1, s], ALU.add))
                    put(tt(st[:, 1, s], pr1[:, 1, s], pr2[:, 0, s], ALU.subtract))
                    sync()
                    for c in range(2):
                        for i in range(2 * half, 2 * half + 2):
                            s = slice(i * SEQ, (i + 1) * SEQ)
                            put(v.tensor_tensor_scan(st[:, c, s], prm_q[:, 0, i:i + 1].broadcast_to([P, SEQ]),
                                                     st[:, c, s], 0.0, ALU.mult, ALU.add))
                sync()
                cos, sin = (tab[:, z:z + 1, :].broadcast_to([P, 2, 1024]) for z in range(2))
                put(tt(pr1, st, cos, ALU.mult))
                put(tt(pr2, st, sin, ALU.mult))
                sync()
                put(tt(pr1[:, 0, :], pr1[:, 0, :], pr2[:, 1, :], ALU.subtract))
                put(tt(pr1[:, 1, :], pr1[:, 1, :], pr2[:, 0, :], ALU.add))
                sync()
                dve.sem_inc(q_h, 1)

            def quad_out(l, q):
                dve.wait_ge(q_y, l * QUADS + q + 1)
                y = ys[:, :, 0, ds(q * P, P)]
                chain(v.tensor_tensor(y, y, aux[:, 0, 0:SEQ].rearrange("p (t c) -> p t c", t=TOK), ALU.add))
                dve.sem_inc(q_y_out, 1)

            def merged_block(l, br, n, done):
                dve.wait_ge(sig_ready, l * 12 + n + (4 * (2 - br) + 1))
                dve.wait_ge(slab_used, done)
                dst = merged[:, :, ds(n * NB, NB)]
                if br == 2:
                    chain(v.tensor_tensor(dst, sig, main[:, 2:4, :], ALU.mult))
                    dve.sem_inc(block_out[1], 1)
                else:
                    chain(v.tensor_tensor(sig, sig, main[:, 2:4, :], ALU.mult))
                    dve.sem_inc(block_out[1], 1)
                    chain(v.tensor_tensor(dst, dst, sig, ALU.add))
                dve.sem_inc(sig_used, 1)
                if br == 0:
                    dve.sem_inc(merged_ready, 1)

            def merge_step(l, br, n, first=False, last=False, j0=0):
                seg = f"merge{br}"
                if br:
                    quad_in(l, n, br)
                    if not (first and br == 2):
                        quad_out(l, n + (4 * (2 - br) - 1))

                    def branch_lows(half):
                        if br == 2 and half == 0:
                            gated(1)
                            dve.wait_ge(silu_done, l * 3 + 3)
                        lows(l, f"ys{br}", 2, yT_hi, yT_lo, at=2 * half)

                    quad(l, n, br, branch_lows if first else None)
                if last and br == 0:
                    lows(l, "merged", 4, hT_hi, hT_lo)
                merged_block(l, br, n, used(l, seg, 11 + j0, n, 12))
                chain.clear()

            with dve.Fori(0, DEPTH) as l:
                for at, n in ((0, 16), (32, 4)):
                    chain.put(v.tensor_copy(gc[:, at:at + 2 * n].rearrange("p (s n) -> p s n", s=2),
                                            g_all[:, DEPTH * at:DEPTH * (at + 2 * n)]
                                            .rearrange("p (s l n) -> p s l n", s=2, l=DEPTH)[:, :, ds(l, 1), :]
                                            .rearrange("p s o n -> p s (o n)")))
                norm(l * 4 + 1, l * 8 + 4)
                dve.wait_ge(s5_rows_in, l * 48 + 48)
                chain(v.tensor_copy(dt_wide[:, :, :], dt_rows[:, :].rearrange("j (g o) -> j g o", o=1)
                                    .broadcast_to([NTILE, 2, STATE])))
                dve.sem_inc(dt_wide_ready, 1)
                lows(l, "ln", 8, hT_hi, hT_lo, gain=0)
                s5_parameters(l)
                chain.clear()
                for b in range(2):
                    dve.wait_ge(lat_sq, l * 2 + (b + 1))
                    mean_square(l * 4 + 2 + b, 2 * (1 - b), LAT)
                    for t in range(TOK):
                        chain(v.tensor_scalar(lat[:, t, b * LAT:(b + 1) * LAT], main[:, 2 * b + t, :],
                                              st_r[:, 2 * (1 - b) + t:2 * (1 - b) + t + 1], None, ALU.mult))
                    dve.sem_inc(block_out[b], 1)
                    dve.sem_inc(lat_norm, 1)
                lows(l, "qlat", 2, yT_hi, yT_lo, gain=32)
                lows(l, "kvlat", 2, yT_hi, yT_lo, gain=36, k0=4)
                s5_coefficients(l)
                for b in range(2):
                    dve.wait_ge(slab_used, used(l, "proj", 16 + 8 * b + 7))
                    v.tensor_copy(ys[:, :, 0, b * NB:(b + 1) * NB], main[:, 2 * b:2 * b + 2, :])\
                        .then_inc(block_out[b], 1)
                dve.wait_ge(consts_in, 32)
                dve.wait_ge(x_kept, l * 16 + 16)
                dve.wait_ge(slab_used, used(l, "lat", 1))
                chain(v.tensor_copy(krT, main[0:ROPE, 0, 0:SEQ]))
                dve.sem_inc(block_out[0], 1)
                dve.sem_inc(kr_raw, 1)
                for b in range(1, 8):
                    dst, c = (mla_q, b - 1) if b < 4 else (mla_kv, b - 4)
                    dve.wait_ge(slab_used, used(l, "lat", 2 * b + 1))
                    chain(v.tensor_copy(dst[:, :, c * NB:(c + 1) * NB], main[:, 2 * (b % 2):2 * (b % 2) + 2, :]))
                    dve.sem_inc(block_out[b % 2], 1)
                    if b == 2:
                        dve.wait_ge(kr_back, l + 1)
                        chain(v.tensor_copy(kr, aux[:, 0, 0:TOK * ROPE].rearrange("p (t c) -> p t c", t=TOK)))
                        for t in range(TOK):
                            k3 = kr[:, t, :].rearrange("p (h c) -> p h c", h=1)
                            rotary(k3[:, :, 0:ROPE // 2], k3[:, :, ROPE // 2:ROPE], t, 1)
                        dve.sem_inc(kr_ready, 1)
                    if b == 3:
                        for t in range(TOK):
                            q4 = mla_q[:, t, :].rearrange("p (h c) -> p h c", h=HEADS)
                            rotary(q4[:, :, HD:HD + ROPE // 2], q4[:, :, HD + ROPE // 2:HD + ROPE], t, HEADS)
                dve.wait_ge(kr_out, l + 1)
                dve.sem_inc(dve_mark, 1)
                with dve.Fori(0, HEADS // 2) as it:
                    for b in range(2):
                        chain.clear()
                        n = l * 2 * HEADS + it * 2 + b
                        chain(v.tensor_copy(q_s, mla_q[:, :, ds(it * 384 + b * 192, 192)]))
                        chain(v.tensor_copy(k_s, mla_kv[:, :, ds(it * 512 + b * 256, HD)]))
                        dve.sem_inc(h_static, 1)
                        dve.wait_ge(h_scores, n + 1)
                        chain(v.tensor_tensor(s_a, aux[:, 0, 0:384], masks[:, 0, :], ALU.add))
                        chain(v.reduce_max(mx[:, 0:1], s_a[:, 0:P], AX.X))
                        chain(v.reduce_max(mx[:, 1:2], s_a[:, P:384], AX.X))
                        chain(v.tensor_scalar(nmx[:, :], mx[:, :], -1.0, None, ALU.mult))
                        dve.sem_inc(h_max, 1)
                        dve.wait_ge(h_probs, n + 1)
                        chain(v.reciprocal(rsum[:, :], sums[:, :]))
                        if b == 1:
                            dve.wait_ge(slab_used, used(l, "sb", 15, it, 16))
                            v.tensor_copy(sb_qk[:, :, ds(it * 2 + 1, 1), :].rearrange("p t o c -> p t (o c)"),
                                          main[:, 2:4, 0:256])
                            v.tensor_copy(ys[:, :, 2, ds(it * 256 + HD, HD)], main[:, 2:4, 256:384])\
                                .then_inc(block_out[1], 1)
                        dve.wait_ge(h_o_in, n + 1)
                        for t in range(TOK):
                            chain(v.tensor_scalar(ys[:, t, 1, ds(it * 256 + b * HD, HD)],
                                                  trb[:, 1, 256 + t * P:384 + t * P], rsum[:, t:t + 1], None,
                                                  ALU.mult))
                        dve.sem_inc(h_o_out, 1)
                with dve.Fori(0, HEADS // 2) as it:
                    for b in range(2):
                        chain.clear()
                        n = l * 2 * HEADS + it * 2 + (HEADS + b)
                        chain(v.tensor_copy(qk_s, sb_qk[:, :, ds(it * 2 + b, 1), :].rearrange("p t o c -> p t (o c)")))
                        dve.sem_inc(h_static, 1)
                        dve.wait_ge(sb_soft, l * HEADS + it * 2 + (b + 1))
                        chain(v.scalar_tensor_tensor(out=s_a, in0=aux[:, 0, 0:384], scalar=0.0, in1=s_a, op0=ALU.max,
                                                     op1=ALU.add))
                        chain(v.tensor_tensor(s_a, s_a, masks[:, 2, :], ALU.mult))
                        for a, e in ((0, P), (P, 384)):
                            back = slice(e - 1, a - 1 if a else None, -1)
                            chain(v.tensor_tensor_scan(s_b[:, back], one[:, 0:1].broadcast_to([P, e - a]),
                                                       s_a[:, back], 0.0, ALU.mult, ALU.add))
                        chain(v.tensor_tensor(s_c, aux[:, 0, 0:384], s_b, ALU.subtract))
                        chain(v.tensor_tensor(s_c, s_c, masks[:, 1, :], ALU.add))
                        dve.sem_inc(sb_arg, 1)
                        if b == 1:
                            dve.wait_ge(slab_used, used(l, "gate", 15, it, 16))
                            v.tensor_copy(gates[:, :, :, ds(it * 256 + HD, HD)],
                                          main[:, 2:4, 0:HB].rearrange("p t (c n) -> p t c n", c=3))\
                                .then_inc(block_out[1], 1)
                        dve.wait_ge(h_o_in, n + 1)
                        chain(v.tensor_copy(ys[:, :, 2, ds(it * 256 + b * HD, HD)],
                                            trb[:, 1, 256:512].rearrange("p (t c) -> p t c", t=TOK)))
                        dve.sem_inc(h_o_out, 1)
                chain.clear()
                dve.sem_inc(heads_left, 1)

                def gated(br):
                    dve.wait_ge(silu_done, l * 3 + (3 - br))
                    chain(v.tensor_tensor(ys[:, :, br, :], ys[:, :, br, :], gates[:, :, br, :], ALU.mult))
                    dve.sem_inc(ys_ready, 1)

                gated(2)
                for br in (2, 1):
                    merge_step(l, br, 0, True)
                    with dve.Fori(1, 4) as n:
                        merge_step(l, br, n)
                quad_out(l, QUADS - 1)
                lows(l, "glu", 4, yT_hi, yT_lo)
                for b in range(2):
                    dve.wait_ge(glu_sig, (l * 2 + b) * 2 + 2)
                    dve.sem_inc(block_out[1 - b], 1)
                    s = slice(b * NB, (b + 1) * NB)
                    chain(v.tensor_tensor(sig2, sig2, gate_ssm[:, :, s], ALU.mult))
                    chain(v.tensor_tensor(ys[:, :, 0, s], ys[:, :, 0, s], sig2, ALU.mult))
                    dve.sem_inc(glu_sig, 1)
                    dve.sem_inc(ys_ready, 1)
                lows(l, "ys0", 4, yT_hi, yT_lo)
                merged_block(l, 0, 0, used(l, "ssm", 19))
                chain.clear()
                with dve.Fori(1, 3) as n:
                    merge_step(l, 0, n, j0=-12)
                merge_step(l, 0, 3, last=True, j0=-12)
                lows(l, "merged", 4, hT_hi, hT_lo, at=4)
                dve.wait_ge(x_back, l * 16 + 16)
                for b in range(4):
                    if b == 3:
                        lows(l, "p", 2, yT_hi, yT_lo, per=1)
                    dve.wait_ge(slab_used, used(l, "out", 8 * b + 7))
                    s = slice(b * NB, (b + 1) * NB)
                    pair = slice(2 * (b % 2), 2 * (b % 2) + 2)
                    chain(v.tensor_tensor(xs[:, :, s], xs[:, :, s], main[:, pair, :], ALU.add))
                    dve.sem_inc(block_out[b % 2], 1)
                    dve.sem_inc(x_block, 1)
                norm(l * 4 + 4, l * 8 + 8)
                lows(l, "ple", 8, hT_hi, hT_lo, gain=16)
                for b in range(4):
                    s = slice(b * NB, (b + 1) * NB)
                    for t in range(TOK):
                        dve.wait_ge(ple_sig, (l * 4 + b) * 2 + (t + 1))
                        v.tensor_tensor(e_ple[:, t, s], e_ple[:, t, s], sig[:, t, :], ALU.mult).then_inc(ple_used, 1)
                        if t == 1:
                            dve.sem_inc(block_out[b % 2], 1)
                    for t in range(TOK):
                        dve.wait_ge(ple_used, (l * 4 + b) * 2 + (t + 3))
                        chain(v.tensor_tensor(xs[:, t, s], xs[:, t, s], e_ple[:, t, s], ALU.add))
                        dve.sem_inc(x_half, 1)
                dve.sem_inc(layer_done, 1)
                chain.clear()
            dve.wait_ge(sq_done, DEPTH * 8 + 5)
            chain(v.reduce_sum(st_ss[:, 0:2], st_p[:, :, :], AX.X))
            mean_square(DEPTH * 4 + 1, 0, D)
            dve.wait_ge(fin_g_in, 16)
            for t in range(TOK):
                for c in (slice(0, D // 2), slice(D // 2, D)):
                    v.scalar_tensor_tensor(out=xn[:, t, c], in0=xs[:, t, c], scalar=st_r[:, t:t + 1], in1=fin_g[:, c],
                                           op0=ALU.mult, op1=ALU.mult).then_inc(out_ready, 1)


def constants():
    ident = np.eye(P, dtype=np.float32)
    q = np.arange(P)[:, None]
    k = np.arange(P)[None, :]
    masks = np.zeros((P, 3, 384), np.float32)
    for i, ok in enumerate((k <= q, k < q)):
        for c in (0, 256):
            masks[:, i, c:c + P] = np.where(ok, 0.0, NEG)
    masks[:, 2, :] = masks[:, 1, :] == 0.0
    pos = np.arange(SEQ, dtype=np.float32)
    inv = (np.float32(10000.0) ** (-np.arange(0, ROPE, 2, dtype=np.float32) / np.float32(ROPE))).astype(np.float32)
    ang = pos[:, None] * inv[None, :]
    rope = np.stack([np.cos(ang), np.sin(ang)], axis=1).astype(np.float32)
    rope = np.ascontiguousarray(rope.reshape(TOK, P, 2, ROPE // 2).transpose(1, 0, 2, 3))
    return {"ident": ident, "masks": masks, "rope": rope}


INS = ["x", "p", "ln_g", "w_in", "ssm_lam_re", "ssm_lam_im", "ssm_log_dt", "ssm_b_re", "ssm_b_im", "ssm_c_re",
       "ssm_c_im", "ssm_d", "ssm_w_glu", "mla_g_q", "mla_g_kv", "mla_w_uq", "mla_w_ukv", "w_branch", "w_out", "ple_g",
       "w_ple_gate", "w_ple_proj", "final_g"]


def kernel(**inputs):
    import concourse.bacc as bacc
    from concourse.bass_utils import run_bass_kernel_spmd

    nc = bacc.Bacc("TRN2", target_bir_lowering=False, num_devices=1)
    arrays, args = {}, []
    given = {**{n: inputs[n] for n in INS}, **constants()}
    for name, value in given.items():
        a = np.ascontiguousarray(value)
        arrays[f"in_{name}"] = a
        args.append(nc.dram_tensor(f"in_{name}", a.shape, mybir.dt.from_np(a.dtype), kind="ExternalInput").ap())
    args.append(nc.dram_tensor("out", (1, SEQ, D), mybir.dt.float32, kind="ExternalOutput").ap())
    build(nc, *args)
    r = run_bass_kernel_spmd(nc, [arrays], core_ids=[0])
    return r.results[0]["out"]
```
